# Optimizing a Trainium2 kernel written in Bass

```python
import jax
import jax.numpy as jnp
from jax import lax
import numpy as np
import jax, jax.numpy as jnp

D_MODEL = 1024
BATCH = 1
SEQ = 256
DEPTH = 2

GRID_W = 64
CTX_LEN = 256
CHUNK = 64
GLA_HEADS = 4
GLA_DK = 64
GLA_DV = 128
GLA_GATE_RANK = 16
GLA_GATE_TAU = 16.0
ATT_Q_HEADS = 8
ATT_KV_HEADS = 2
ATT_HEAD_DIM = 64
ATT_GROUP = ATT_Q_HEADS // ATT_KV_HEADS
ROPE_AXIS_DIM = ATT_HEAD_DIM // 2
ROPE_THETA = 10000.0
Q_BLOCK = 128
HGRN_HEADS = 8
HGRN_DF = 128
HGRN_DV = D_MODEL // HGRN_HEADS
D_FF = ((8 * D_MODEL + 3 * 256 - 1) // (3 * 256)) * 256

EVEN_SIZES = (GLA_HEADS * GLA_DK, GLA_HEADS * GLA_DK, GLA_HEADS * GLA_DV, GLA_HEADS * GLA_DV, 2 * GLA_GATE_RANK,
              ATT_Q_HEADS * ATT_HEAD_DIM, ATT_KV_HEADS * ATT_HEAD_DIM, ATT_KV_HEADS * ATT_HEAD_DIM)
ODD_SIZES = (HGRN_HEADS * HGRN_DF,) * 3 + (HGRN_HEADS * HGRN_DV,) * 2
EVEN_MIX = GLA_HEADS * GLA_DV + ATT_Q_HEADS * ATT_HEAD_DIM
ODD_MIX = HGRN_HEADS * HGRN_DV


def _rms(x, gain, eps=1e-6):
    xf = x.astype(jnp.float32)
    y = xf * lax.rsqrt(jnp.mean(xf * xf, axis=-1, keepdims=True) + eps)
    return (y * gain.astype(jnp.float32)).astype(x.dtype)

def _modulate(h, shift, scale):
    return h * (1 + scale) + shift

def _split(a, sizes):
    return jnp.split(a, np.cumsum(sizes)[:-1].tolist(), axis=-1)

def _heads(a, n_heads):
    B, N, _ = a.shape
    return a.reshape(B, N, n_heads, -1).transpose(0, 2, 1, 3)

def _merge(a):
    B, H, N, d = a.shape
    return a.transpose(0, 2, 1, 3).reshape(B, N, H * d)

def _gated_readout(o, og, gain):
    return _merge(_rms(o, gain) * jax.nn.silu(og))

def _swiglu(h, w_gate, w_up, w_down):
    return (jax.nn.silu(h @ w_gate) * (h @ w_up)) @ w_down

def _chunk_gla(q, k, v, g, s0):
    B, H, T, K = q.shape
    V = v.shape[-1]
    n = T // CHUNK

    def blocks(a):
        return jnp.moveaxis(a.astype(jnp.float32).reshape(B, H, n, CHUNK, a.shape[-1]), 2, 0)

    tri = jnp.tril(jnp.ones((CHUNK, CHUNK), dtype=bool))[:, :, None]

    def step(s, blk):
        qc, kc, vc, gc = blk
        G = jnp.cumsum(gc, axis=2)
        decay = jnp.exp(jnp.where(tri, G[:, :, :, None, :] - G[:, :, None, :, :], -jnp.inf))
        scores = jnp.einsum('bhik,bhjk,bhijk->bhij', qc, kc, decay)
        o = jnp.einsum('bhij,bhjv->bhiv', scores, vc) + jnp.einsum('bhik,bhkv->bhiv', qc * jnp.exp(G), s)
        G_last = G[:, :, -1:, :]
        s = s * jnp.exp(G_last)[:, :, 0, :, None] + jnp.einsum('bhjk,bhjv->bhkv', kc * jnp.exp(G_last - G), vc)
        return s, o

    s, o = lax.scan(step, s0, (blocks(q), blocks(k), blocks(v), blocks(g)))
    return jnp.moveaxis(o, 0, 2).reshape(B, H, T, V).astype(v.dtype), s

def _directional_scan(q, k, v, g, n_ctx, reverse):
    def seg(a, sl):
        a = a[:, :, sl]
        return jnp.flip(a, 2) if reverse else a
    c_sl, t_sl = slice(0, n_ctx), slice(n_ctx, None)
    B, H, _, K = q.shape
    s0 = jnp.zeros((B, H, K, v.shape[-1]), jnp.float32)
    o_ctx, s_ctx = _chunk_gla(seg(q, c_sl), seg(k, c_sl), seg(v, c_sl), seg(g, c_sl), s0)
    o_lat, _ = _chunk_gla(seg(q, t_sl), seg(k, t_sl), seg(v, t_sl), seg(g, t_sl), s_ctx)
    if reverse:
        o_ctx, o_lat = jnp.flip(o_ctx, 2), jnp.flip(o_lat, 2)
    return o_ctx, o_lat

def _axial_rope_tables(n_tokens):
    rows_n = n_tokens // GRID_W
    row = jnp.repeat(jnp.arange(rows_n), GRID_W).astype(jnp.float32)
    col = jnp.tile(jnp.arange(GRID_W), rows_n).astype(jnp.float32)
    inv = ROPE_THETA ** (-jnp.arange(0, ROPE_AXIS_DIM, 2, dtype=jnp.float32) / ROPE_AXIS_DIM)
    ang = jnp.concatenate([row[:, None] * inv, col[:, None] * inv], axis=-1)
    return jnp.cos(ang), jnp.sin(ang)

def _rope(x, cos, sin):
    xf = x.astype(jnp.float32).reshape(x.shape[:-1] + (-1, 2))
    x0, x1 = xf[..., 0], xf[..., 1]
    out = jnp.stack([x0 * cos - x1 * sin, x0 * sin + x1 * cos], axis=-1)
    return out.reshape(x.shape).astype(x.dtype)

def _softmax_attend(q, k, v):
    s = jnp.einsum('bhgqd,bhkd->bhgqk', q, k, preferred_element_type=jnp.float32) * (ATT_HEAD_DIM ** -0.5)
    p = jax.nn.softmax(s, axis=-1).astype(v.dtype)
    return jnp.einsum('bhgqk,bhkd->bhgqd', p, v)

def _even_mixer(h_ctx, h_lat, w_in, gla_w_gate, gla_b_gate, gla_out_norm, att_q_norm, att_k_norm, cos, sin, ctx_out):
    B, n_ctx, _ = h_ctx.shape
    h = jnp.concatenate([h_ctx, h_lat], axis=1)
    N = h.shape[1]
    T = N - n_ctx
    gq, gk, gv, gog, gz, aq, ak, av = _split(h @ w_in, EVEN_SIZES)

    q = _heads(gq, GLA_HEADS) * (GLA_DK ** -0.5)
    k = _heads(gk, GLA_HEADS)
    v = _heads(gv, GLA_HEADS)
    og = _heads(gog, GLA_HEADS)
    dirs = []
    for d, z in enumerate(jnp.split(gz, 2, axis=-1)):
        logit = (z @ gla_w_gate[d] + gla_b_gate[d]).astype(jnp.float32)
        g = _heads(jax.nn.log_sigmoid(logit) / GLA_GATE_TAU, GLA_HEADS)
        dirs.append(_directional_scan(q, k, v, g, n_ctx, reverse=(d == 1)))
    a_lat = _gated_readout(dirs[0][1] + dirs[1][1], og[:, :, n_ctx:], gla_out_norm)

    qa = _rms(aq.reshape(B, N, ATT_KV_HEADS, ATT_GROUP, ATT_HEAD_DIM), att_q_norm).transpose(0, 2, 3, 1, 4)
    ka = _rms(ak.reshape(B, N, ATT_KV_HEADS, ATT_HEAD_DIM), att_k_norm).transpose(0, 2, 1, 3)
    va = av.reshape(B, N, ATT_KV_HEADS, ATT_HEAD_DIM).transpose(0, 2, 1, 3)
    q_lat = _rope(qa[:, :, :, n_ctx:], cos, sin)
    k_all = jnp.concatenate([ka[:, :, :n_ctx], _rope(ka[:, :, n_ctx:], cos, sin)], axis=2)
    q_blocks = jnp.moveaxis(q_lat.reshape(B, ATT_KV_HEADS, ATT_GROUP, T // Q_BLOCK, Q_BLOCK, ATT_HEAD_DIM), 3, 0)
    o_blocks = lax.map(lambda qb: _softmax_attend(qb, k_all, va), q_blocks)
    b_lat = jnp.moveaxis(o_blocks, 0, 3).reshape(B, ATT_KV_HEADS, ATT_GROUP, T, ATT_HEAD_DIM)
    b_lat = b_lat.transpose(0, 3, 1, 2, 4).reshape(B, T, ATT_Q_HEADS * ATT_HEAD_DIM)
    o_lat = jnp.concatenate([a_lat, b_lat], axis=-1)
    if not ctx_out:
        return None, o_lat
    a_ctx = _gated_readout(dirs[0][0] + dirs[1][0], og[:, :, :n_ctx], gla_out_norm)
    b_ctx = _softmax_attend(qa[:, :, :, :n_ctx], ka[:, :, :n_ctx], va[:, :, :n_ctx])
    b_ctx = b_ctx.transpose(0, 3, 1, 2, 4).reshape(B, n_ctx, ATT_Q_HEADS * ATT_HEAD_DIM)
    return jnp.concatenate([a_ctx, b_ctx], axis=-1), o_lat

def _odd_mixer(h_ctx, h_lat, w_in, lower_bounds, layer, out_norm, ctx_out):
    n_ctx = h_ctx.shape[1]
    h = jnp.concatenate([h_ctx, h_lat], axis=1)
    fq, f_fwd, f_bwd, fi, fog = _split(h @ w_in, ODD_SIZES)
    q = _heads(jax.nn.silu(fq), HGRN_HEADS)
    i = _heads(fi, HGRN_HEADS)
    og = _heads(fog, HGRN_HEADS)
    lbs = jnp.cumsum(jax.nn.softmax(lower_bounds.astype(jnp.float32), axis=1), axis=1)
    lb = (lbs[:, layer] - lbs[:, 0]).reshape(2, HGRN_HEADS, 1, HGRN_DF)
    dirs = []
    for d, f in enumerate((f_fwd, f_bwd)):
        log_f = jnp.logaddexp(jnp.log(lb[d]), jnp.log1p(-lb[d]) + jax.nn.log_sigmoid(_heads(f, HGRN_HEADS).astype(jnp.float32)))
        k = -jnp.expm1(log_f)
        dirs.append(_directional_scan(q, k, i, log_f, n_ctx, reverse=(d == 1)))
    o_lat = _gated_readout(dirs[0][1] + dirs[1][1], og[:, :, n_ctx:], out_norm)
    if not ctx_out:
        return None, o_lat
    return _gated_readout(dirs[0][0] + dirs[1][0], og[:, :, :n_ctx], out_norm), o_lat

def first_inputs(seed: int = 0) -> dict:
    key = jax.random.key(seed)
    ks = iter(jax.random.split(key, 32))
    n_even, n_odd = (DEPTH + 1) // 2, DEPTH // 2
    D = D_MODEL

    def nrm(shape, scale):
        return scale * jax.random.normal(next(ks), shape, jnp.float32)

    def gain(shape):
        return 1.0 + nrm(shape, 0.02)

    return {
        'x': nrm((BATCH, SEQ, D), 1.0),
        'c': nrm((BATCH, D), 1.0),
        'ctx': nrm((BATCH, CTX_LEN, D), 1.0),
        'c_ctx': nrm((D,), 1.0),
        'mod_w': nrm((DEPTH, D, 6 * D), D ** -0.5),
        'mod_b': nrm((DEPTH, 6 * D), 0.02),
        'norm_pre_mix': gain((DEPTH, D)),
        'norm_post_mix': gain((DEPTH, D)),
        'norm_pre_ffn': gain((DEPTH, D)),
        'norm_post_ffn': gain((DEPTH, D)),
        'even_w_in': nrm((n_even, D, sum(EVEN_SIZES)), D ** -0.5),
        'gla_w_gate': nrm((n_even, 2, GLA_GATE_RANK, GLA_HEADS * GLA_DK), GLA_GATE_RANK ** -0.5),
        'gla_b_gate': nrm((n_even, 2, GLA_HEADS * GLA_DK), 0.02),
        'gla_out_norm': gain((n_even, GLA_DV)),
        'att_q_norm': gain((n_even, ATT_HEAD_DIM)),
        'att_k_norm': gain((n_even, ATT_HEAD_DIM)),
        'even_w_out': nrm((n_even, EVEN_MIX, D), EVEN_MIX ** -0.5),
        'odd_w_in': nrm((n_odd, D, sum(ODD_SIZES)), D ** -0.5),
        'hgrn_lower_bounds': nrm((2, DEPTH, HGRN_HEADS * HGRN_DF), 0.1),
        'hgrn_out_norm': gain((n_odd, HGRN_DV)),
        'odd_w_out': nrm((n_odd, ODD_MIX, D), ODD_MIX ** -0.5),
        'ffn_w_gate': nrm((DEPTH, D, D_FF), D ** -0.5),
        'ffn_w_up': nrm((DEPTH, D, D_FF), D ** -0.5),
        'ffn_w_down': nrm((DEPTH, D_FF, D), D_FF ** -0.5),
    }

def first_block(x, c, ctx, c_ctx, mod_w, mod_b, norm_pre_mix, norm_post_mix, norm_pre_ffn, norm_post_ffn,
              even_w_in, gla_w_gate, gla_b_gate, gla_out_norm, att_q_norm, att_k_norm, even_w_out,
              odd_w_in, hgrn_lower_bounds, hgrn_out_norm, odd_w_out, ffn_w_gate, ffn_w_up, ffn_w_down):
    cos, sin = _axial_rope_tables(x.shape[1])
    sc = jax.nn.silu(c)
    scc = jax.nn.silu(c_ctx)
    x_ctx, x_lat = ctx, x
    for l in range(DEPTH):
        last = l == DEPTH - 1
        j = l // 2
        m_lat = jnp.split((sc @ mod_w[l] + mod_b[l])[:, None, :], 6, axis=-1)
        m_ctx = jnp.split((scc @ mod_w[l] + mod_b[l])[None, None, :], 6, axis=-1)
        h_ctx = _modulate(_rms(x_ctx, norm_pre_mix[l]), m_ctx[0], m_ctx[1])
        h_lat = _modulate(_rms(x_lat, norm_pre_mix[l]), m_lat[0], m_lat[1])
        if l % 2 == 0:
            o_ctx, o_lat = _even_mixer(h_ctx, h_lat, even_w_in[j], gla_w_gate[j], gla_b_gate[j], gla_out_norm[j],
                                       att_q_norm[j], att_k_norm[j], cos, sin, not last)
            w_out = even_w_out[j]
        else:
            o_ctx, o_lat = _odd_mixer(h_ctx, h_lat, odd_w_in[j], hgrn_lower_bounds, l, hgrn_out_norm[j], not last)
            w_out = odd_w_out[j]
        x_lat = x_lat + m_lat[2] * _rms(o_lat @ w_out, norm_post_mix[l])
        h_lat = _modulate(_rms(x_lat, norm_pre_ffn[l]), m_lat[3], m_lat[4])
        x_lat = x_lat + m_lat[5] * _rms(_swiglu(h_lat, ffn_w_gate[l], ffn_w_up[l], ffn_w_down[l]), norm_post_ffn[l])
        if not last:
            x_ctx = x_ctx + m_ctx[2] * _rms(o_ctx @ w_out, norm_post_mix[l])
            h_ctx = _modulate(_rms(x_ctx, norm_pre_ffn[l]), m_ctx[3], m_ctx[4])
            x_ctx = x_ctx + m_ctx[5] * _rms(_swiglu(h_ctx, ffn_w_gate[l], ffn_w_up[l], ffn_w_down[l]), norm_post_ffn[l])
    return x_lat


N_HEADS = 16
N_KV_HEADS = 4
HEAD_DIM = D_MODEL // N_HEADS
GROUP = N_HEADS // N_KV_HEADS
QKV_DIM = (N_HEADS + 2 * N_KV_HEADS) * HEAD_DIM
ROT_DIM = HEAD_DIM // 4
ROPE_THETA_2 = 500000.0
MOBA_BLOCK = 256
MOBA_TOPK = 3
MOBA_QCHUNK = 16
SWA_WINDOW = 128
D_FF_2 = 3584
N_EXPERTS = 8
TOP_K = 2
PLE_DIM = 256
LN_EPS = 1e-5
N_EVEN = (DEPTH + 1) // 2
N_ODD = DEPTH // 2


def rope_tables(positions):
    inv = 1.0 / (ROPE_THETA_2 ** (jnp.arange(0, ROT_DIM, 2, dtype=jnp.float32) / ROT_DIM))
    ang = positions.astype(jnp.float32)[..., None] * inv
    return jnp.cos(ang), jnp.sin(ang)

def apply_partial_rope(x, cos, sin):
    half = ROT_DIM // 2
    c = cos[:, :, None, :].astype(x.dtype)
    s = sin[:, :, None, :].astype(x.dtype)
    x1, x2, xp = x[..., :half], x[..., half:ROT_DIM], x[..., ROT_DIM:]
    return jnp.concatenate([x1 * c - x2 * s, x2 * c + x1 * s, xp], axis=-1)

def layer_norm(x, g, b):
    xf = x.astype(jnp.float32)
    mu = jnp.mean(xf, axis=-1, keepdims=True)
    var = jnp.mean(jnp.square(xf - mu), axis=-1, keepdims=True)
    return ((xf - mu) * lax.rsqrt(var + LN_EPS) * g.astype(jnp.float32) + b.astype(jnp.float32)).astype(x.dtype)

def project_qkv(x, w_qkv, cos, sin):
    B, S, _ = x.shape
    qkv = x @ w_qkv
    nq = N_HEADS * HEAD_DIM
    nk = N_KV_HEADS * HEAD_DIM
    q = qkv[..., :nq].reshape(B, S, N_HEADS, HEAD_DIM)
    k = qkv[..., nq:nq + nk].reshape(B, S, N_KV_HEADS, HEAD_DIM)
    v = qkv[..., nq + nk:].reshape(B, S, N_KV_HEADS, HEAD_DIM)
    return apply_partial_rope(q, cos, sin), apply_partial_rope(k, cos, sin), v

def moba_attention(q, k, v):
    B, S, H, Dh = q.shape
    nb = -(-S // MOBA_BLOCK)
    S_pad = nb * MOBA_BLOCK
    pad = ((0, 0), (0, S_pad - S), (0, 0), (0, 0))
    q = jnp.pad(q * (HEAD_DIM ** -0.5), pad)
    k = jnp.pad(k, pad)
    v = jnp.pad(v, pad)
    kb = k.reshape(B, nb, MOBA_BLOCK, N_KV_HEADS, Dh).transpose(0, 1, 3, 2, 4)
    vb = v.reshape(B, nb, MOBA_BLOCK, N_KV_HEADS, Dh).transpose(0, 1, 3, 2, 4)
    kmean = jnp.mean(kb.astype(jnp.float32), axis=3)
    qg = q.reshape(B, S_pad, N_KV_HEADS, GROUP, Dh).astype(jnp.float32)
    gate = jnp.einsum('bskgd,bnkd->bskgn', qg, kmean).reshape(B, S_pad, H, nb)
    qblk = jnp.arange(S_pad) // MOBA_BLOCK
    past = jnp.arange(nb)[None, :] < qblk[:, None]
    gate = jnp.where(past[None, :, None, :], gate, -jnp.inf)
    n_sel = min(MOBA_TOPK, nb)
    _, sel = lax.top_k(gate, n_sel)

    QC = MOBA_QCHUNK
    NC = S_pad // QC
    q_c = q.reshape(B, NC, QC, H, Dh).transpose(1, 0, 2, 3, 4)
    sel_c = sel.reshape(B, NC, QC, H, n_sel).transpose(1, 0, 2, 3, 4)
    b_idx = jnp.arange(B)[:, None, None, None]
    g_idx = (jnp.arange(H) // GROUP)[None, None, :, None]

    def chunk(args):
        qc, selc, cid = args
        t = cid * QC + jnp.arange(QC)
        c = (cid * QC) // MOBA_BLOCK
        kg = kb[b_idx, selc, g_idx]
        vg = vb[b_idx, selc, g_idx]
        lp = jnp.einsum('bqhd,bqhnjd->bqhnj', qc, kg).astype(jnp.float32)
        valid = jnp.arange(n_sel)[None, :] < (t // MOBA_BLOCK)[:, None]
        lp = jnp.where(valid[None, :, None, :, None], lp, -jnp.inf).reshape(B, QC, H, n_sel * MOBA_BLOCK)
        ko = lax.dynamic_index_in_dim(kb, c, axis=1, keepdims=False)
        vo = lax.dynamic_index_in_dim(vb, c, axis=1, keepdims=False)
        qcg = qc.reshape(B, QC, N_KV_HEADS, GROUP, Dh)
        lo = jnp.einsum('bqkgd,bkjd->bqkgj', qcg, ko).astype(jnp.float32).reshape(B, QC, H, MOBA_BLOCK)
        kpos = c * MOBA_BLOCK + jnp.arange(MOBA_BLOCK)
        lo = jnp.where((kpos[None, :] <= t[:, None])[None, :, None, :], lo, -jnp.inf)
        probs = jax.nn.softmax(jnp.concatenate([lp, lo], axis=-1), axis=-1)
        pp = probs[..., :n_sel * MOBA_BLOCK].reshape(B, QC, H, n_sel, MOBA_BLOCK).astype(v.dtype)
        po = probs[..., n_sel * MOBA_BLOCK:].reshape(B, QC, N_KV_HEADS, GROUP, MOBA_BLOCK).astype(v.dtype)
        out = jnp.einsum('bqhnj,bqhnjd->bqhd', pp, vg) + \
            jnp.einsum('bqkgj,bkjd->bqkgd', po, vo).reshape(B, QC, H, Dh)
        return out

    out = lax.map(chunk, (q_c, sel_c, jnp.arange(NC)))
    return out.transpose(1, 0, 2, 3, 4).reshape(B, S_pad, H, Dh)[:, :S]

def sliding_window_attention(q, k, v, sinks):
    B, S, H, Dh = q.shape
    W = SWA_WINDOW
    n = S // W
    qb = (q * (HEAD_DIM ** -0.5)).reshape(B, n, W, N_KV_HEADS, GROUP, Dh)
    kb = k.reshape(B, n, W, N_KV_HEADS, Dh)
    vb = v.reshape(B, n, W, N_KV_HEADS, Dh)
    zpad = ((0, 0), (1, 0), (0, 0), (0, 0), (0, 0))
    kk = jnp.concatenate([jnp.pad(kb, zpad)[:, :-1], kb], axis=2)
    vv = jnp.concatenate([jnp.pad(vb, zpad)[:, :-1], vb], axis=2)
    logits = jnp.einsum('bnqkgd,bnjkd->bnkgqj', qb, kk).astype(jnp.float32)
    rel = (jnp.arange(W)[:, None] + W) - jnp.arange(2 * W)[None, :]
    band = (rel >= 0) & (rel < W)
    first = (jnp.arange(n) == 0)[:, None, None] & (jnp.arange(2 * W) < W)[None, None, :]
    mask = band[None] & ~first
    logits = jnp.where(mask[None, :, None, None, :, :], logits, -jnp.inf)
    sink = sinks.astype(jnp.float32).reshape(1, 1, N_KV_HEADS, GROUP, 1, 1)
    m = jnp.maximum(jnp.max(logits, axis=-1, keepdims=True), sink)
    e = jnp.exp(logits - m)
    probs = e / (jnp.sum(e, axis=-1, keepdims=True) + jnp.exp(sink - m))
    out = jnp.einsum('bnkgqj,bnjkd->bnqkgd', probs.astype(v.dtype), vv)
    return out.reshape(B, S, H, Dh)

def swiglu(x, w_gate, w_up, w_down):
    return (jax.nn.silu(x @ w_gate) * (x @ w_up)) @ w_down

def moe_swiglu(x, w_router, w_gate, w_up, w_down):
    logits = (x @ w_router).astype(jnp.float32)
    top_v, top_i = lax.top_k(logits, TOP_K)
    top_w = jax.nn.softmax(top_v, axis=-1)
    gates = jnp.sum(jax.nn.one_hot(top_i, N_EXPERTS, dtype=jnp.float32) * top_w[..., None], axis=-2)
    out = jnp.zeros_like(x)
    for e in range(N_EXPERTS):
        out = out + gates[..., e:e + 1].astype(x.dtype) * swiglu(x, w_gate[e], w_up[e], w_down[e])
    return out

def second_inputs(seed: int = 0) -> dict:
    key = jax.random.key(seed)
    ks = jax.random.split(key, 20)
    f32 = jnp.float32
    beta = (8.0 * DEPTH) ** -0.25

    def nrm(k, shape, fan_in, scale=1.0):
        return jax.random.normal(k, shape, f32) * (scale * fan_in ** -0.5)

    x = jax.random.normal(ks[0], (BATCH, SEQ, D_MODEL), f32)
    p = jax.random.normal(ks[1], (DEPTH, BATCH, SEQ, PLE_DIM), f32)
    positions = jnp.broadcast_to(jnp.arange(SEQ, dtype=jnp.int32)[None, :], (BATCH, SEQ))
    w_qkv = nrm(ks[2], (DEPTH, D_MODEL, QKV_DIM), D_MODEL)
    w_o = nrm(ks[3], (DEPTH, N_HEADS * HEAD_DIM, D_MODEL), N_HEADS * HEAD_DIM, beta)
    ln_mix_g = 1.0 + 0.05 * jax.random.normal(ks[4], (DEPTH, D_MODEL), f32)
    ln_mix_b = 0.02 * jax.random.normal(ks[5], (DEPTH, D_MODEL), f32)
    ln_ffn_g = 1.0 + 0.05 * jax.random.normal(ks[6], (DEPTH, D_MODEL), f32)
    ln_ffn_b = 0.02 * jax.random.normal(ks[7], (DEPTH, D_MODEL), f32)
    sinks = 0.5 * jax.random.normal(ks[8], (N_ODD, N_HEADS), f32)
    w_ffn_gate = nrm(ks[9], (N_EVEN, D_MODEL, D_FF_2), D_MODEL)
    w_ffn_up = nrm(ks[10], (N_EVEN, D_MODEL, D_FF_2), D_MODEL)
    w_ffn_down = nrm(ks[11], (N_EVEN, D_FF_2, D_MODEL), D_FF_2, beta)
    w_router = nrm(ks[12], (N_ODD, D_MODEL, N_EXPERTS), D_MODEL)
    w_exp_gate = nrm(ks[13], (N_ODD, N_EXPERTS, D_MODEL, D_FF_2), D_MODEL)
    w_exp_up = nrm(ks[14], (N_ODD, N_EXPERTS, D_MODEL, D_FF_2), D_MODEL)
    w_exp_down = nrm(ks[15], (N_ODD, N_EXPERTS, D_FF_2, D_MODEL), D_FF_2, beta)
    w_ple_proj = nrm(ks[16], (DEPTH, PLE_DIM, D_MODEL), PLE_DIM, 0.5)
    w_ple_gate = nrm(ks[17], (DEPTH, D_MODEL, D_MODEL), D_MODEL)
    return {"x": x, "p": p, "positions": positions, "w_qkv": w_qkv, "w_o": w_o,
            "ln_mix_g": ln_mix_g, "ln_mix_b": ln_mix_b, "ln_ffn_g": ln_ffn_g, "ln_ffn_b": ln_ffn_b,
            "sinks": sinks, "w_ffn_gate": w_ffn_gate, "w_ffn_up": w_ffn_up, "w_ffn_down": w_ffn_down,
            "w_router": w_router, "w_exp_gate": w_exp_gate, "w_exp_up": w_exp_up, "w_exp_down": w_exp_down,
            "w_ple_proj": w_ple_proj, "w_ple_gate": w_ple_gate}

def second_block(x, p, positions, w_qkv, w_o, ln_mix_g, ln_mix_b, ln_ffn_g, ln_ffn_b, sinks,
              w_ffn_gate, w_ffn_up, w_ffn_down, w_router, w_exp_gate, w_exp_up, w_exp_down,
              w_ple_proj, w_ple_gate):
    alpha = (2.0 * DEPTH) ** 0.25
    B, S, _ = x.shape
    cos, sin = rope_tables(positions)
    for i in range(DEPTH):
        j = i // 2
        q, k, v = project_qkv(x, w_qkv[i], cos, sin)
        if i % 2 == 0:
            a = moba_attention(q, k, v)
        else:
            a = sliding_window_attention(q, k, v, sinks[j])
        x = layer_norm(alpha * x + a.reshape(B, S, N_HEADS * HEAD_DIM) @ w_o[i], ln_mix_g[i], ln_mix_b[i])
        if i % 2 == 0:
            f = swiglu(x, w_ffn_gate[j], w_ffn_up[j], w_ffn_down[j])
        else:
            f = moe_swiglu(x, w_router[j], w_exp_gate[j], w_exp_up[j], w_exp_down[j])
        x = layer_norm(alpha * x + f, ln_ffn_g[i], ln_ffn_b[i])
        x = x + (p[i] @ w_ple_proj[i]) * jax.nn.sigmoid(x @ w_ple_gate[i])
    return x


def setup_inputs(seed=0):
    out = dict(first_inputs(seed))
    for name, value in second_inputs(seed + 1).items():
        if name != "x":
            out[name + "_2"] = value
    return out


def reference(
    x, c, ctx, c_ctx, mod_w, mod_b, norm_pre_mix, norm_post_mix, norm_pre_ffn, norm_post_ffn,
    even_w_in, gla_w_gate, gla_b_gate, gla_out_norm, att_q_norm, att_k_norm, even_w_out,
    odd_w_in, hgrn_lower_bounds, hgrn_out_norm, odd_w_out, ffn_w_gate, ffn_w_up, ffn_w_down,
    p_2, positions_2, w_qkv_2, w_o_2, ln_mix_g_2, ln_mix_b_2, ln_ffn_g_2, ln_ffn_b_2, sinks_2,
    w_ffn_gate_2, w_ffn_up_2, w_ffn_down_2, w_router_2, w_exp_gate_2, w_exp_up_2, w_exp_down_2,
    w_ple_proj_2, w_ple_gate_2,
):
    x = first_block(
        x, c, ctx, c_ctx, mod_w, mod_b, norm_pre_mix, norm_post_mix, norm_pre_ffn,
        norm_post_ffn, even_w_in, gla_w_gate, gla_b_gate, gla_out_norm, att_q_norm, att_k_norm,
        even_w_out, odd_w_in, hgrn_lower_bounds, hgrn_out_norm, odd_w_out, ffn_w_gate, ffn_w_up,
        ffn_w_down,
    )
    return second_block(
        x, p_2, positions_2, w_qkv_2, w_o_2, ln_mix_g_2, ln_mix_b_2, ln_ffn_g_2, ln_ffn_b_2,
        sinks_2, w_ffn_gate_2, w_ffn_up_2, w_ffn_down_2, w_router_2, w_exp_gate_2, w_exp_up_2,
        w_exp_down_2, w_ple_proj_2, w_ple_gate_2,
    )


_drawn_inputs = setup_inputs


def setup_inputs(seed=0):
    import zlib

    import numpy as np

    out = dict(_drawn_inputs(seed))
    spreads = {}
    factors = {'gla_b_gate': 4.051,
     'gla_out_norm': 10.73,
     'att_q_norm': 8.0,
     'att_k_norm': 8.0,
     'hgrn_lower_bounds': 7.287,
     'hgrn_out_norm': 14.629,
     'sinks_2': 8.0,
     'norm_post_mix': 3.277,
     'norm_pre_ffn': 2.768,
     'norm_post_ffn': 3.286}
    for name, (base, spread) in spreads.items():
        noise = np.random.default_rng([zlib.crc32(name.encode()), seed]).standard_normal(out[name].shape)
        drawn = base * np.exp(spread * noise) if base else spread * noise
        out[name] = jnp.asarray(drawn.astype(out[name].dtype))
    for name, factor in factors.items():
        out[name] = (out[name] * factor).astype(out[name].dtype)
    return out
```

```python
from contextlib import ExitStack

import numpy as np
import concourse.bass as bass
from concourse import mybir

F32 = mybir.dt.float32
I32 = mybir.dt.int32
U32 = mybir.dt.uint32
ALU = mybir.AluOpType
ACT = mybir.ActivationFunctionType
AX = mybir.AxisListType

P = 128
D = 1024
KD = D // P
CTX_TILES = (0, 1)
LAT_TILES = (2, 3)
ALL_TILES = CTX_TILES + LAT_TILES
START = 4
SLOTS = 3
SLOT = 7168
EPS_RMS = 1e-6
EPS_LN = 1e-5
LEVELS = (64, 32, 16, 8, 4, 2, 1)
NL = 1 + len(LEVELS)
ATT_D = 64
NEG = -1e30

C_IDENT = 0
C_ONES = C_IDENT + P
C_SEL = C_ONES + P
C_IOTA = C_SEL + 4 * P
C_TRI = C_IOTA + P
C_MISC = C_TRI + P
C_BASE = C_MISC + P
C_SUM = C_BASE
C_REST = C_SUM + 2 * NL * P
C_MASK = C_REST + 2 * P
C_GRID = C_MASK + 2 * NL * P
C_CAUSAL = C_GRID + 2 * 2 * 32
C_INVF = C_CAUSAL + 2 * 2 * 256
C_ALL = C_INVF + 8


def constants():
    c = np.zeros((P, C_ALL), np.float32)
    i = np.arange(P)
    c[:, C_IDENT:C_IDENT + P] = np.eye(P)
    c[:, C_ONES:C_ONES + P] = 1
    for r in range(4):
        c[r, C_SEL + r * P:C_SEL + (r + 1) * P] = 1
    c[:, C_IOTA:C_IOTA + P] = i[None, :]
    c[:, C_TRI:C_TRI + P] = i[:, None] < i[None, :]
    c[:, C_MISC] = -0.5
    c[0, C_MISC + 8:C_MISC + 16] = 2 * np.arange(8)
    c[0, C_MISC + 16:C_MISC + 32] = np.arange(16)
    t, x = i[:, None], i[None, :]
    for d in range(2):
        sums = np.zeros((NL, P, P), np.float32)
        masks = np.zeros((NL, P, P), np.float32)
        sums[0] = (t <= x) if d == 0 else (t >= x)
        for n, h in enumerate(LEVELS):
            mid = x // (2 * h) * (2 * h) + h
            upper = x >= mid
            if d == 0:
                sums[n + 1] = np.where(upper, (t >= mid) & (t <= x), (t > x) & (t < mid))
            else:
                sums[n + 1] = np.where(upper, (t >= mid) & (t < x), (t >= x) & (t < mid))
            same = t // (2 * h) == x // (2 * h)
            late, early = (x, t) if d == 0 else (t, x)
            masks[n] = same & (late % (2 * h) >= h) & (early % (2 * h) < h)
        masks[NL - 1] = np.eye(P)
        c[:, C_SUM + d * NL * P:C_SUM + (d + 1) * NL * P] = sums.transpose(1, 0, 2).reshape(P, -1)
        c[:, C_MASK + d * NL * P:C_MASK + (d + 1) * NL * P] = masks.transpose(1, 0, 2).reshape(P, -1)
        c[:, C_REST + d * P:C_REST + (d + 1) * P] = (t > x) if d == 0 else (t < x)
    grid_w, axis, theta = 64, 32, 10000.0
    inv = theta ** (-np.arange(0, axis, 2, dtype=np.float32) / axis)
    tok = np.arange(2 * P)
    ang = np.concatenate([(tok // grid_w).astype(np.float32)[:, None] * inv,
                          (tok % grid_w).astype(np.float32)[:, None] * inv], axis=-1).astype(np.float32)
    for n, f in enumerate((np.cos(ang), np.sin(ang))):
        c[:, C_GRID + n * 64:C_GRID + (n + 1) * 64] = f.reshape(2, P, 32).transpose(1, 0, 2).reshape(P, 64)
    q, k = np.arange(2 * P)[:, None], np.arange(2 * P)[None, :]
    for n, ok in enumerate((k <= q, (k <= q) & (k > q - P))):
        m = np.where(ok, 0.0, NEG).astype(np.float32)
        c[:, C_CAUSAL + n * 512:C_CAUSAL + (n + 1) * 512] = m.reshape(2, P, 256).transpose(1, 0, 2).reshape(P, 512)
    c[:, C_INVF:C_INVF + 8] = 1.0 / (500000.0 ** (np.arange(0, 16, 2, dtype=np.float32) / 16))
    return c


class Signal:

    def __init__(self, handle, owner):
        self.handle, self.owner, self.base = handle, owner, START

    def at(self, n):
        return self.base + n

    def passed(self, n):
        self.base += n


class Chain:

    def __init__(self, handle):
        self.handle, self.base, self.n, self.extra, self.per = handle, 0, 0, 0, 0

    def link(self, eng, ins):
        self.n += 1
        ins.then_inc(self.handle, 1)
        eng.wait_ge(self.handle, self.base + self.n + self.extra)

    def enter(self, index, per):
        self.base, self.n, self.per = self.base + self.n, 0, per
        self.extra = index * per

    def leave(self, times):
        assert self.n == self.per, (self.n, self.per)
        self.base, self.n, self.extra = self.base + self.per * times, 0, 0


class Ring:

    def __init__(self, loaded, free):
        self.loaded, self.free, self.pos = loaded, free, 0

    def slot(self, j):
        return (self.pos + j) % SLOTS

    def round(self, j):
        return (self.pos + j) // SLOTS


def program(nc, a, out):
    root = ExitStack()
    uses = {}

    def unique(name):
        uses[name] = uses.get(name, 0) + 1
        return name if uses[name] == 1 else f"{name}_{uses[name]}"

    def sb(cx, name, shape, dt=F32):
        return cx.enter_context(nc.sbuf_tensor(unique(name), shape, dt))

    def pb(cx, name, shape, dt=F32):
        return cx.enter_context(nc.psum_tensor(unique(name), shape, dt))

    sem = lambda name: root.enter_context(nc.semaphore(name))
    signals = []

    def signal(name, owner):
        s = Signal(sem(name), owner)
        signals.append(s)
        return s

    ring_loaded = [sem(f"ring_loaded{s}") for s in range(SLOTS)]
    ring_free = [signal(f"ring_free{s}", "tensor") for s in range(SLOTS)]
    ring = Ring(ring_loaded, ring_free)
    loads = {q: [sem(f"loads_{q}{k}"), 0] for q in ("act", "pool") for k in ("",)}
    act_chain, dve_chain, pool_chain = Chain(sem("act_chain")), Chain(sem("dve_chain")), Chain(sem("pool_chain"))
    loads_ready = signal("loads_ready", "gpsimd")
    met = {e: [sem(f"met_{e}"), 0] for e in ("tensor", "scalar", "vector", "gpsimd")}

    ring_buf = sb(root, "ring_buf", [P, SLOTS, SLOT])
    X = sb(root, "X", [P, 4, D])
    hT = sb(root, "hT", [P, KD, 4 * P])
    const = sb(root, "const", [P, C_BASE])
    scT = sb(root, "scT", [P, KD, 2])
    mod_gain = sb(root, "mod_gain", [P, 2, KD, 2])
    mod_shift = sb(root, "mod_shift", [P, 2, KD, 2])
    gate_row = sb(root, "gate_row", [2, 2, D])
    ident = const[:, C_IDENT:C_IDENT + P]
    ones = const[:, C_ONES:C_ONES + P]
    sel = lambda r, n: const[0:n, C_SEL + r * P:C_SEL + (r + 1) * P]
    half_power = const[:, C_MISC:C_MISC + 1]

    block = root.enter_context(nc.Block())
    link_a = lambda ins: act_chain.link(nc.scalar, ins)
    link_v = lambda ins: dve_chain.link(nc.vector, ins)
    link_g = lambda ins: pool_chain.link(nc.gpsimd, ins)

    def load(eng, queue, *pairs):
        s = loads[queue]
        for dst, src in pairs:
            eng.dma_start(dst, src).then_inc(s[0], 16)
            s[1] += 16
            eng.wait_ge(s[0], s[1])

    waited = {e: sem(f"waited_{e}") for e in ("tensor", "scalar", "gpsimd")}

    def settle(eng):
        eng.sem_inc(waited["tensor" if eng is nc.tensor else "scalar" if eng is nc.scalar else "gpsimd"], 1)

    def meet():
        for e in met:
            met[e][1] += 1

        def body(name):
            def _(eng):
                eng.drain().then_inc(met[name][0], 1)
                for other in met:
                    if other != name:
                        eng.wait_ge(met[other][0], met[other][1])
            return _
        for e in met:
            on_engine[e](body(e))

    on_engine = {"tensor": block.tensor, "scalar": block.scalar, "vector": block.vector,
                     "gpsimd": block.gpsimd}

    def slot_view(j, rows, width):
        return ring_buf[:, ring.slot(j), 0:rows * width].rearrange("p (k n) -> p k n", k=rows)

    def stream(sp, j, src, turn=0):
        rows, width = src.shape[1], src.shape[2]
        sp.wait_ge(ring_free[ring.slot(j)].handle, START + ring.round(j) + turn)
        sp.dma_start(slot_view(j, rows, width), src).then_inc(ring_loaded[ring.slot(j)], 16)

    def await_item(pe, j, turn=0):
        pe.wait_ge(ring_loaded[ring.slot(j)], 16 * (ring.round(j) + 1) + 16 * turn)

    def free_item(j):
        nc.tensor.drain().then_inc(ring_free[ring.slot(j)].handle, 1)

    def by_rows(w):
        return w.rearrange("(k p) n -> p k n", p=P)

    s_start = {n: signal(n, o) for n, o in (
        ("cond_silu", "scalar"), ("cond_psum", "tensor"), ("const_ready", "scalar"), ("x_ready", "scalar"))}

    def start():
        with ExitStack() as cx:
            cond = sb(cx, "cond", [16, P])
            ps = pb(cx, "ps_cond", [P, 16])
            S = s_start

            def counters(owner):
                def _(eng):
                    for s in signals:
                        if s.owner == owner:
                            eng.sem_inc(s.handle, START)
                return _
            for e in met:
                on_engine[e](counters(e))

            @block.scalar
            def _(act):
                load(act, "act", (const[:, :], a["table"][:, 0:C_BASE]),
                     (cond[0:8, :], a["c"].rearrange("o (k p) -> (o k) p", p=P)),
                     (cond[8:16, :], a["c_ctx"].rearrange("(k p) -> k p", p=P)))
                nc.scalar.activation(cond[:, :], cond[:, :], ACT.Silu).then_inc(S["cond_silu"].handle, 1)
                load(act, "act", (X[:, 0:2, :], a["ctx"].rearrange("o (t p) d -> p (o t) d", p=P)),
                     (X[:, 2:4, :], a["x"].rearrange("o (t p) d -> p (o t) d", p=P)))

            @block.tensor
            def _(pe):
                pe.wait_ge(S["cond_silu"].handle, S["cond_silu"].at(1))
                nc.tensor.transpose(ps[:, :], cond[:, :], ident[0:16, 0:16]).then_inc(S["cond_psum"].handle, 1)

            @block.vector
            def _(dve):
                dve.wait_ge(S["cond_psum"].handle, S["cond_psum"].at(1))
                link_v(nc.vector.tensor_copy(scT[:, :, :], ps[:, :].rearrange("p (w k) -> p k w", w=2)))
            for s in S.values():
                s.passed(1)
            meet()

    s_mod = {n: signal(n, o) for n, o in (
        ("mod_psum", "tensor"), ("mod_taken", "vector"), ("mod_rows", "vector"), ("mod_cols", "tensor"),
        ("mod_cols_taken", "vector"))}

    def modulate(layer):
        items = 6
        with ExitStack() as cx:
            rows = sb(cx, "mod_rows_buf", [2, 4, 512])
            bias = sb(cx, "mod_bias", [2, 2, items, 512])
            gains = sb(cx, "mod_gains", [2, 2, 2, D])
            tmp = sb(cx, "mod_tmp", [2, 2, 512])
            ps_row = [pb(cx, f"ps_row{i}", [P, 512]) for i in range(2)]
            ps_col = pb(cx, "ps_col", [P, 4, 4, 2])
            S = s_mod

            @block.sync
            def _(sp):
                with sp.Fori(0, 2) as site:
                    for q in range(items):
                        w = by_rows(a["mod_w"][layer])[:, :, bass.ds(site * (items * 512) + q * 512, 512)]
                        stream(sp, q, w, site * (items // SLOTS))

            @block.tensor
            def _(pe):
                with pe.Fori(0, 2) as site:
                    for q in range(items):
                        n = site * items + q
                        await_item(pe, q, site * (items // SLOTS))
                        pe.wait_ge(S["mod_taken"].handle, S["mod_taken"].at(-1) + n)
                        w = slot_view(q, KD, 512)
                        for k in range(KD):
                            mm = nc.tensor.matmul(ps_row[q % 2][0:2, :], scT[:, k, :], w[:, k, :],
                                                  start=k == 0, stop=k == KD - 1)
                        mm.then_inc(S["mod_psum"].handle, 1)
                        free_item(q)
                    pe.wait_ge(S["mod_rows"].handle, S["mod_rows"].at(1) + site)
                    pe.wait_ge(S["mod_cols_taken"].handle, S["mod_cols_taken"].at(0) + site)
                    settle(pe)
                    for q in range(4):
                        for c in range(4):
                            mm = nc.tensor.transpose(ps_col[:, q, c, :], rows[:, q, c * P:(c + 1) * P],
                                                     ident[0:2, 0:2])
                    mm.then_inc(S["mod_cols"].handle, 1)

            @block.gpsimd
            def _(pool):
                for s in range(2):
                    pre, post = (("norm_pre_mix", "norm_post_mix"), ("norm_pre_ffn", "norm_post_ffn"))[s]
                    load(pool, "pool", (gains[:, s, 0, :], a[pre][layer:layer + 1, :].partition_broadcast(2)),
                         (gains[:, s, 1, :], a[post][layer:layer + 1, :].partition_broadcast(2)))
                load(pool, "pool", (bias[:, :, :, :].rearrange("w s q n -> w (s q n)"),
                                    a["mod_b"][layer:layer + 1, :].partition_broadcast(2)))
                pool.sem_inc(loads_ready.handle, 1)

            @block.vector
            def _(dve):
                dve.wait_ge(loads_ready.handle, loads_ready.at(1))
                per = items + 4
                with dve.Fori(0, 2) as site:
                    dve_chain.enter(site, per)
                    dve.wait_ge(S["mod_cols"].handle, S["mod_cols"].at(0) + site)
                    for q in range(items):
                        n = site * items + q
                        half = (q % 2) * 512
                        b = bias[:, bass.ds(site, 1), q, :].rearrange("w s n -> w (s n)")
                        pre = gains[:, bass.ds(site, 1), 0, half:half + 512].rearrange("w s n -> w (s n)")
                        post = gains[:, bass.ds(site, 1), 1, half:half + 512].rearrange("w s n -> w (s n)")
                        dve.wait_ge(S["mod_psum"].handle, S["mod_psum"].at(1) + n)
                        dst = rows[:, q, :] if q < 2 else tmp[:, q % 2, :]
                        link_v(nc.vector.tensor_tensor(dst, ps_row[q % 2][0:2, :], b, ALU.add))
                        nc.vector.sem_inc(S["mod_taken"].handle, 1)
                        if 2 <= q < 4:
                            link_v(nc.vector.scalar_tensor_tensor(
                                out=rows[:, q, :], in0=tmp[:, q % 2, :], scalar=1.0, in1=pre,
                                op0=ALU.add, op1=ALU.mult))
                        if q == 3:
                            nc.vector.sem_inc(S["mod_rows"].handle, 1)
                        if q >= 4:
                            g = gate_row[:, bass.ds(site, 1), half:half + 512].rearrange("w s n -> w (s n)")
                            link_v(nc.vector.tensor_tensor(g, tmp[:, q % 2, :], post, ALU.mult))
                    dve.wait_ge(S["mod_cols"].handle, S["mod_cols"].at(1) + site)
                    for dst, q in ((mod_shift, 0), (mod_gain, 2)):
                        last = nc.vector.tensor_copy(
                            dst[:, bass.ds(site, 1), :, :].rearrange("p s k w -> p (s k w)"),
                            ps_col[:, q:q + 2, :, :].rearrange("p q c w -> p (q c w)"))
                    last.then_inc(S["mod_cols_taken"].handle, 1)
                dve_chain.leave(2)
            loads_ready.passed(1)
            ring.pos += 2 * items
            S["mod_psum"].passed(12), S["mod_taken"].passed(12)
            for n in ("mod_rows", "mod_cols", "mod_cols_taken"):
                S[n].passed(2)
            meet()

    s_norm = {n: signal(n, o) for n, o in (
        ("norm_sums", "scalar"), ("norm_rstd", "gpsimd"), ("norm_scaled", "vector"), ("norm_psum", "tensor"),
        ("norm_out_v", "vector"), ("norm_out_a", "scalar"))}

    def normalise(site, tiles):
        with ExitStack() as cx:
            junk = sb(cx, "norm_junk", [P, D])
            sums = sb(cx, "norm_sums_buf", [P, 4])
            rstd = sb(cx, "norm_rstd_buf", [P, 4])
            xn = sb(cx, "norm_xn", [P, 2, D])
            ps = [pb(cx, f"ps_norm{i}", [P, KD, P]) for i in range(2)]
            S = s_norm
            nt = len(tiles)

            @block.scalar
            def _(act):
                for i, t in enumerate(tiles):
                    nc.scalar.activation(junk[:, :], X[:, t, :], ACT.Square, accum_out=sums[:, i:i + 1])\
                        .then_inc(S["norm_sums"].handle, 1)
                    act.wait_ge(S["norm_sums"].handle, S["norm_sums"].at(i + 1))
                for i, t in enumerate(tiles):
                    act.wait_ge(S["norm_psum"].handle, S["norm_psum"].at(i + 1))
                    w = 0 if t in LAT_TILES else 1
                    for k in range(KD // 2):
                        last = nc.scalar.activation(hT[:, k, t * P:(t + 1) * P], ps[i % 2][:, k, :], ACT.Identity,
                                                    bias=mod_shift[:, site, k, w:w + 1],
                                                    scale=mod_gain[:, site, k, w:w + 1])
                    last.then_inc(S["norm_out_a"].handle, 1)

            @block.gpsimd
            def _(pool):
                pool.wait_ge(S["norm_sums"].handle, S["norm_sums"].at(nt))
                link_g(nc.gpsimd.tensor_scalar(rstd[:, 0:nt], sums[:, 0:nt], 1.0 / D, EPS_RMS, ALU.mult, ALU.add))
                nc.gpsimd.tensor_tensor(rstd[:, 0:nt], rstd[:, 0:nt], half_power.to_broadcast([P, nt]), ALU.pow)\
                    .then_inc(S["norm_rstd"].handle, 1)

            @block.vector
            def _(dve):
                dve.wait_ge(S["norm_rstd"].handle, S["norm_rstd"].at(1))
                for i, t in enumerate(tiles):
                    if i >= 2:
                        dve.wait_ge(S["norm_psum"].handle, S["norm_psum"].at(i - 1))
                    nc.vector.tensor_scalar(xn[:, i % 2, :], X[:, t, :], rstd[:, i:i + 1], None, ALU.mult)\
                        .then_inc(S["norm_scaled"].handle, 1)
                    dve.wait_ge(S["norm_psum"].handle, S["norm_psum"].at(i + 1))
                    w = 0 if t in LAT_TILES else 1
                    for k in range(KD // 2, KD):
                        last = nc.vector.tensor_scalar(hT[:, k, t * P:(t + 1) * P], ps[i % 2][:, k, :],
                                                       mod_gain[:, site, k, w:w + 1],
                                                       mod_shift[:, site, k, w:w + 1], ALU.mult, ALU.add)
                    last.then_inc(S["norm_out_v"].handle, 1)

            @block.tensor
            def _(pe):
                for i, t in enumerate(tiles):
                    pe.wait_ge(S["norm_scaled"].handle, S["norm_scaled"].at(i + 1))
                    if i >= 2:
                        pe.wait_ge(S["norm_out_v"].handle, S["norm_out_v"].at(i - 1))
                        pe.wait_ge(S["norm_out_a"].handle, S["norm_out_a"].at(i - 1))
                    for k in range(KD):
                        mm = nc.tensor.transpose(ps[i % 2][:, k, :], xn[:, i % 2, k * P:(k + 1) * P], ident)
                    mm.then_inc(S["norm_psum"].handle, 1)
            for n in S:
                S[n].passed(1 if n == "norm_rstd" else nt)
            meet()

    s_tr = {n: signal(n, o) for n, o in (
        ("turn_psum", "tensor"), ("turn_taken", "scalar"))}

    def turn(src, tiles, parts=KD):
        with ExitStack() as cx:
            ps = [pb(cx, f"ps_turn{i}", [P, KD, P]) for i in range(2)]
            S = s_tr

            @block.tensor
            def _(pe):
                for i, t in enumerate(tiles):
                    pe.wait_ge(S["turn_taken"].handle, S["turn_taken"].at(i - 1))
                    for k in range(parts):
                        mm = nc.tensor.transpose(ps[i % 2][:, k, :], src(t, k), ident)
                    mm.then_inc(S["turn_psum"].handle, 1)

            @block.scalar
            def _(act):
                for i, t in enumerate(tiles):
                    act.wait_ge(S["turn_psum"].handle, S["turn_psum"].at(i + 1))
                    nc.scalar.activation(hT[:, 0:parts, t * P:(t + 1) * P], ps[i % 2][:, 0:parts, :], ACT.Copy)\
                        .then_inc(S["turn_taken"].handle, 1)
            for s in S.values():
                s.passed(len(tiles))
            meet()

    s_lin = {n: signal(n, o) for n, o in (
        ("lin_psum", "tensor"), ("lin_taken_a", "scalar"), ("lin_taken_v", "vector"))}

    def linear(w, tiles, take, cuts, parts=KD, turns=None):
        with ExitStack() as cx:
            ps = [pb(cx, f"ps_lin{i}", [P, 512]) for i in range(4)]
            S = s_lin
            groups = [(j, t, lo + o, min(lo + o + step, hi), o) for j, (lo, hi, step) in enumerate(cuts)
                      for t in tiles for o in range(0, hi - lo, step)]

            @block.sync
            def _(sp):
                for j, (lo, hi, step) in enumerate(cuts):
                    stream(sp, j, by_rows(w)[:, :, lo:hi], turns["sync"] * CHUNKS2 if turns else 0)

            @block.tensor
            def _(pe):
                for n, (j, t, lo, hi, o) in enumerate(groups):
                    if n == 0 or groups[n - 1][0] != j:
                        await_item(pe, j, turns["tensor"] * CHUNKS2 if turns else 0)
                    reader = S["lin_taken_a"] if n % 2 == 0 else S["lin_taken_v"]
                    pe.wait_ge(reader.handle, reader.at(n // 2 - 1))
                    view = slot_view(j, parts, cuts[j][1] - cuts[j][0])
                    for k in range(parts):
                        mm = nc.tensor.matmul(ps[n % 4][:, 0:hi - lo], hT[:, k, t * P:(t + 1) * P],
                                              view[:, k, o:o + hi - lo], start=k == 0, stop=k == parts - 1)
                    mm.then_inc(S["lin_psum"].handle, 1)
                    if n + 1 == len(groups) or groups[n + 1][0] != j:
                        free_item(j)

            @block.scalar
            def _(act):
                for n, (j, t, lo, hi, o) in enumerate(groups):
                    if n % 2 == 0:
                        act.wait_ge(S["lin_psum"].handle, S["lin_psum"].at(n + 1))
                        take(nc.scalar, t, lo, hi, ps[n % 4][:, 0:hi - lo]).then_inc(S["lin_taken_a"].handle, 1)

            @block.vector
            def _(dve):
                for n, (j, t, lo, hi, o) in enumerate(groups):
                    if n % 2 == 1:
                        dve.wait_ge(S["lin_psum"].handle, S["lin_psum"].at(n + 1))
                        take(nc.vector, t, lo, hi, ps[n % 4][:, 0:hi - lo]).then_inc(S["lin_taken_v"].handle, 1)
            S["lin_psum"].passed(len(groups))
            S["lin_taken_a"].passed((len(groups) + 1) // 2)
            S["lin_taken_v"].passed(len(groups) // 2)
            ring.pos += len(cuts)
            meet()

    def copy_on(eng, dst, src):
        return nc.scalar.activation(dst, src, ACT.Copy) if eng is nc.scalar else nc.vector.tensor_copy(dst, src)

    s_post = {n: signal(n, o) for n, o in (
        ("post_sums", "scalar"), ("post_rstd", "gpsimd"), ("post_gate", "tensor"), ("post_done", "vector"))}

    def add_gated(site, Y, tiles):
        with ExitStack() as cx:
            junk = sb(cx, "post_junk", [P, D])
            sums = sb(cx, "post_sums_buf", [P, 4])
            rstd = sb(cx, "post_rstd_buf", [P, 4])
            term = sb(cx, "post_term", [P, D])
            ps = [pb(cx, f"ps_gate{i}", [P, D]) for i in range(2)]
            S = s_post
            nt = len(tiles)

            @block.tensor
            def _(pe):
                for w in range(2):
                    for h in range(2):
                        mm = nc.tensor.matmul(ps[w][:, h * 512:(h + 1) * 512], sel(w, 2),
                                              gate_row[:, site, h * 512:(h + 1) * 512], start=True, stop=True)
                mm.then_inc(S["post_gate"].handle, 1)

            @block.scalar
            def _(act):
                for i, t in enumerate(tiles):
                    nc.scalar.activation(junk[:, :], Y[:, t, :], ACT.Square, accum_out=sums[:, i:i + 1])\
                        .then_inc(S["post_sums"].handle, 1)
                    act.wait_ge(S["post_sums"].handle, S["post_sums"].at(i + 1))

            @block.gpsimd
            def _(pool):
                pool.wait_ge(S["post_sums"].handle, S["post_sums"].at(nt))
                link_g(nc.gpsimd.tensor_scalar(rstd[:, 0:nt], sums[:, 0:nt], 1.0 / D, EPS_RMS, ALU.mult, ALU.add))
                nc.gpsimd.tensor_tensor(rstd[:, 0:nt], rstd[:, 0:nt], half_power.to_broadcast([P, nt]), ALU.pow)\
                    .then_inc(S["post_rstd"].handle, 1)

            @block.vector
            def _(dve):
                dve.wait_ge(S["post_rstd"].handle, S["post_rstd"].at(1))
                dve.wait_ge(S["post_gate"].handle, S["post_gate"].at(1))
                for i, t in enumerate(tiles):
                    w = 0 if t in LAT_TILES else 1
                    link_v(nc.vector.scalar_tensor_tensor(out=term[:, :], in0=Y[:, t, :], scalar=rstd[:, i:i + 1],
                                                          in1=ps[w][:, :], op0=ALU.mult, op1=ALU.mult))
                    link_v(nc.vector.tensor_tensor(X[:, t, :], X[:, t, :], term[:, :], ALU.add))
            S["post_sums"].passed(nt), S["post_rstd"].passed(1), S["post_gate"].passed(1)
            meet()

    s_ffn = {n: signal(n, o) for n, o in (
        ("ffn_gate", "tensor"), ("ffn_up", "tensor"), ("ffn_silu", "scalar"), ("ffn_hidden", "vector"),
        ("ffn_turned", "tensor"), ("ffn_turned_taken", "scalar"), ("ffn_down", "tensor"), ("ffn_added", "vector"))}

    class Hidden:

        def __init__(self, cx, width):
            self.width, self.half = width, width // 2
            self.parts = [(o, min(P, width - o)) for o in range(0, width, P)]
            self.silu = sb(cx, "ffn_silu_buf", [P, width])
            self.hid = sb(cx, "ffn_hidden_buf", [P, width])
            self.hidT = sb(cx, "ffn_hiddenT", [P, len(self.parts), P])
            self.ps_g = pb(cx, "ps_ffn_gate", [P, 2, 512])
            self.ps_u = pb(cx, "ps_ffn_up", [P, 2, 512])
            self.ps_t = pb(cx, "ps_ffn_turn", [P, 8, P])
            self.ps_y = pb(cx, "ps_ffn_down", [P, 2, 512])

    def ffn_steps(H, act_tile, Y, add):
        S, hw = s_ffn, H.half

        def product(pe, ps, n, view, t, taken, ready):
            pe.wait_ge(taken.handle, taken.at(0) + n)
            for h in range(2):
                for k in range(KD):
                    mm = nc.tensor.matmul(ps[:, h, 0:hw], act_tile(k, t), view[:, k, h * hw:(h + 1) * hw],
                                          start=k == 0, stop=k == KD - 1)
            mm.then_inc(ready.handle, 1)

        def pe_gate(pe, n, view, t):
            product(pe, H.ps_g, n, view, t, S["ffn_silu"], S["ffn_gate"])

        def pe_up(pe, n, view, t):
            product(pe, H.ps_u, n, view, t, S["ffn_hidden"], S["ffn_up"])

        def pe_turn(pe, n):
            pe.wait_ge(S["ffn_hidden"].handle, S["ffn_hidden"].at(1) + n)
            pe.wait_ge(S["ffn_turned_taken"].handle, S["ffn_turned_taken"].at(0) + n)
            settle(pe)
            for i, (o, m) in enumerate(H.parts):
                mm = nc.tensor.transpose(H.ps_t[0:m, i, :], H.hid[:, o:o + m], ident)
            mm.then_inc(S["ffn_turned"].handle, 1)

        def pe_down(pe, n, view):
            pe.wait_ge(S["ffn_turned_taken"].handle, S["ffn_turned_taken"].at(1) + n)
            pe.wait_ge(S["ffn_added"].handle, S["ffn_added"].at(0) + n)
            for h in range(2):
                for i, (o, m) in enumerate(H.parts):
                    mm = nc.tensor.matmul(H.ps_y[:, h, :], H.hidT[0:m, i, :], view[0:m, i, h * 512:(h + 1) * 512],
                                          start=i == 0, stop=i == len(H.parts) - 1)
            mm.then_inc(S["ffn_down"].handle, 1)

        def act_silu(act, n):
            act.wait_ge(S["ffn_gate"].handle, S["ffn_gate"].at(1) + n)
            act.wait_ge(S["ffn_hidden"].handle, S["ffn_hidden"].at(0) + n)
            nc.scalar.activation(H.silu[:, :].rearrange("p (h n) -> p h n", h=2), H.ps_g[:, :, 0:hw], ACT.Silu)\
                .then_inc(S["ffn_silu"].handle, 1)

        def act_turned(act, n):
            act.wait_ge(S["ffn_turned"].handle, S["ffn_turned"].at(1) + n)
            act.wait_ge(S["ffn_down"].handle, S["ffn_down"].at(0) + n)
            full = H.width // P
            last = nc.scalar.activation(H.hidT[:, 0:full, :], H.ps_t[:, 0:full, :], ACT.Copy)
            if H.width % P:
                m = H.width % P
                last = nc.scalar.activation(H.hidT[0:m, full, :], H.ps_t[0:m, full, :], ACT.Copy)
            last.then_inc(S["ffn_turned_taken"].handle, 1)

        def dve_hidden(dve, n):
            dve.wait_ge(S["ffn_silu"].handle, S["ffn_silu"].at(1) + n)
            dve.wait_ge(S["ffn_up"].handle, S["ffn_up"].at(1) + n)
            dve.wait_ge(S["ffn_turned"].handle, S["ffn_turned"].at(0) + n)
            nc.vector.tensor_tensor(H.hid[:, :].rearrange("p (h n) -> p h n", h=2),
                                    H.silu[:, :].rearrange("p (h n) -> p h n", h=2), H.ps_u[:, :, 0:hw],
                                    ALU.mult).then_inc(S["ffn_hidden"].handle, 1)

        def dve_add(dve, n, t):
            dve.wait_ge(S["ffn_down"].handle, S["ffn_down"].at(1) + n)
            dve.wait_ge(S["ffn_added"].handle, S["ffn_added"].at(0) + n)
            add(Y[:, t, :], H.ps_y[:, :, :].rearrange("p h n -> p (h n)")).then_inc(S["ffn_added"].handle, 1)

        return pe_gate, pe_up, pe_turn, pe_down, act_silu, act_turned, dve_hidden, dve_add

    def down_view(j, width):
        return ring_buf[:, ring.slot(j), 0:(width + P - 1) // P * D].rearrange("p (k n) -> p k n", n=D)

    def stream_down(sp, j, w, row, width, turn=0):
        full, rest = width // P, width % P
        view = down_view(j, width)
        sp.wait_ge(ring_free[ring.slot(j)].handle, START + ring.round(j) + turn)
        h = ring_loaded[ring.slot(j)]
        if rest:
            sp.dma_start(view[0:rest, full, :], w[bass.ds(row + full * P, rest), :]).then_inc(down_rest, 16)
        sp.dma_start(view[:, 0:full, :], w[bass.ds(row, full * P), :].rearrange("(k p) n -> p k n", p=P))\
            .then_inc(h, 16)

    down_rest = sem("down_rest_loaded")
    down_rest_count = [0]

    def feed_forward(w_gate, w_up, w_down, width, tiles, Y):
        hidden = w_gate.shape[1]
        chunks, nt = hidden // width, len(tiles)
        assert chunks * width == hidden
        rest = width % P != 0
        with ExitStack() as cx:
            H = Hidden(cx, width)
            S = s_ffn
            add = lambda y, ps: nc.vector.tensor_tensor(y, y, ps, ALU.add)
            pe_gate, pe_up, pe_turn, pe_down, act_silu, act_turned, dve_hidden, dve_add = ffn_steps(
                H, lambda k, t: hT[:, k, t * P:(t + 1) * P], Y, add)
            view_g, view_u, view_d = slot_view(0, KD, width), slot_view(1, KD, width), down_view(2, width)
            rests = down_rest_count[0]

            @block.sync
            def _(sp):
                with sp.Fori(0, chunks) as c:
                    stream(sp, 0, by_rows(w_gate)[:, :, bass.ds(c * width, width)], c)
                    stream(sp, 1, by_rows(w_up)[:, :, bass.ds(c * width, width)], c)
                    stream_down(sp, 2, w_down, c * width, width, c)

            @block.vector
            def _(dve):
                link_v(nc.vector.memset(Y[:, tiles[0]:tiles[-1] + 1, :], 0.0))
                dve_hidden(dve, 0)

                def chunk(c, last):
                    for i, t in enumerate(tiles):
                        n = c * nt + i
                        if not (last and i == nt - 1):
                            dve_hidden(dve, n + 1)
                        dve_add(dve, n, t)
                with dve.Fori(0, chunks - 1) as c:
                    chunk(c, False)
                chunk(chunks - 1, True)

            @block.scalar
            def _(act):
                act_silu(act, 0)

                def chunk(c, last):
                    for i in range(nt):
                        n = c * nt + i
                        if not (last and i == nt - 1):
                            act_silu(act, n + 1)
                        act_turned(act, n)
                with act.Fori(0, chunks - 1) as c:
                    chunk(c, False)
                chunk(chunks - 1, True)

            @block.tensor
            def _(pe):
                await_item(pe, 0)
                pe_gate(pe, 0, view_g, tiles[0])
                await_item(pe, 1)
                pe_up(pe, 0, view_u, tiles[0])

                def chunk(c, last):
                    for i in range(nt):
                        n = c * nt + i
                        wrap = i == nt - 1
                        if wrap:
                            free_item(0)
                            free_item(1)
                        nxt = tiles[(i + 1) % nt]
                        go = not (last and wrap)
                        if go:
                            if wrap:
                                await_item(pe, 0, c + 1)
                            pe_gate(pe, n + 1, view_g, nxt)
                        pe_turn(pe, n)
                        if go:
                            if wrap:
                                await_item(pe, 1, c + 1)
                            pe_up(pe, n + 1, view_u, nxt)
                        if i == 0:
                            await_item(pe, 2, c)
                            if rest:
                                pe.wait_ge(down_rest, 16 * (rests + 1) + 16 * c)
                        pe_down(pe, n, view_d)
                    free_item(2)
                with pe.Fori(0, chunks - 1) as c:
                    chunk(c, False)
                chunk(chunks - 1, True)
            for s in S.values():
                s.passed(chunks * nt)
            if rest:
                down_rest_count[0] += chunks
            ring.pos += 3 * chunks
            meet()

    s_rec = {n: signal(n, o) for n, o in (
        ("rec_staged", "gpsimd"), ("rec_head_done", "vector"), ("rec_qk_psum", "tensor"), ("rec_qk_ready", "scalar"),
        ("rec_sums", "tensor"), ("rec_decays", "scalar"), ("rec_q", "vector"), ("rec_k", "gpsimd"),
        ("rec_scores", "tensor"), ("rec_masked", "vector"), ("rec_out", "tensor"), ("rec_state", "vector"),
        ("rec_rms", "gpsimd"), ("rec_squares", "vector"))}

    class Recurrence:

        def __init__(self, cx, width, scale, room=None):
            self.width, self.scale = width, scale
            K = width
            self.sums = sb(cx, "rec_sum_table", [P, 2, NL, P])
            self.rest = sb(cx, "rec_rest_table", [P, 2, P])
            self.mask = sb(cx, "rec_mask_table", [P, 2, NL, P])
            self.decay = sb(cx, "rec_decay", [K, NL, P])
            self.rest_decay = sb(cx, "rec_rest_decay", [P, K])
            self.total = sb(cx, "rec_total", [K, 2])
            if room is None:
                room = sb(cx, "rec_room", [P, 2 * (2 * NL - 1) * P])
            nq, nk = 2 * NL * P, 2 * (NL - 1) * P
            self.qd = room[0:K, 0:nq].rearrange("k (b l n) -> k b l n", b=2, l=NL)
            self.kd = room[0:K, nq:nq + nk].rearrange("k (b l n) -> k b l n", b=2, l=NL - 1)
            self.k_end = sb(cx, "rec_k_end", [P, 2, K])
            self.masked = sb(cx, "rec_masked_buf", [P, NL, P])
            self.state = sb(cx, "rec_state_buf", [K, P])
            self.ps_sums = pb(cx, "ps_rec_sums", [P, NL, P])
            self.ps_scores = pb(cx, "ps_rec_scores", [P, NL, P])
            self.ps_out = [pb(cx, f"ps_rec_out{i}", [P, 512]) for i in range(2)]
            self.ps_state = pb(cx, "ps_rec_state", [P, 512])
            self.ps_rest = pb(cx, "ps_rec_rest", [P, 512])

        def tables(self):
            return ((self.sums[:, :, :, :].rearrange("p d l n -> p (d l n)"), a["table"][:, C_SUM:C_REST]),
                    (self.rest[:, :, :].rearrange("p d n -> p (d n)"), a["table"][:, C_REST:C_MASK]),
                    (self.mask[:, :, :, :].rearrange("p d l n -> p (d l n)"), a["table"][:, C_MASK:C_GRID]))

    def recurrence(R, units, first, last, operands, o_acc, start_units=None):
        S, K = s_rec, R.width

        def pe_sums(pe, u, i):
            d, t = units[i]
            g = operands(d, t)[0]
            pe.wait_ge(S["rec_decays"].handle, S["rec_decays"].at(0) + u)
            for h in range(2):
                nc.tensor.matmul(R.ps_sums[0:K, h * 4:h * 4 + 4, :], g, R.sums[:, d, h * 4:h * 4 + 4, :],
                                 start=True, stop=True)
            nc.tensor.matmul(R.ps_rest[:, 0:K], R.rest[:, d, :], g, start=True, stop=True)\
                .then_inc(S["rec_sums"].handle, 1)

        def pe_scores(pe, u, i):
            d, t = units[i]
            _, _, _, qT, kT = operands(d, t)
            pe.wait_ge(S["rec_q"].handle, S["rec_q"].at(1) + u)
            pe.wait_ge(S["rec_k"].handle, S["rec_k"].at(1) + u)
            pe.wait_ge(S["rec_masked"].handle, S["rec_masked"].at(0) + u)
            for l in range(NL - 1):
                nc.tensor.matmul(R.ps_scores[:, l, :], R.kd[:, i % 2, l, :], R.qd[:, i % 2, l + 1, :],
                                 start=True, stop=True)
            nc.tensor.matmul(R.ps_scores[:, NL - 1, :], kT, qT, start=True, stop=True)\
                .then_inc(S["rec_scores"].handle, 1)

        def pe_out(pe, u, i):
            d, t = units[i]
            _, _, v, _, _ = operands(d, t)
            pe.wait_ge(S["rec_masked"].handle, S["rec_masked"].at(1) + u)
            pe.wait_ge(S["rec_state"].handle, S["rec_state"].at(0) + u)
            if i not in last:
                nc.tensor.matmul(R.ps_state[0:K, 0:P], R.k_end[:, i % 2, :], v, start=True, stop=True)
            if i not in first:
                nc.tensor.matmul(R.ps_out[i % 2][:, 0:P], R.qd[:, i % 2, 0, :], R.state[:, :], start=True, stop=False)
            for l in range(NL):
                mm = nc.tensor.matmul(R.ps_out[i % 2][:, 0:P], R.masked[:, l, :], v,
                                      start=l == 0 and i in first, stop=l == NL - 1)
            mm.then_inc(S["rec_out"].handle, 1)

        def act_decays(act, u, i):
            act.wait_ge(S["rec_sums"].handle, S["rec_sums"].at(1) + u)
            act.wait_ge(S["rec_q"].handle, S["rec_q"].at(0) + u)
            act.wait_ge(S["rec_k"].handle, S["rec_k"].at(0) + u)
            nc.scalar.activation(R.decay[:, :, :], R.ps_sums[0:K, :, :], ACT.Exp, scale=R.scale)
            nc.scalar.activation(R.rest_decay[:, :], R.ps_rest[:, 0:K], ACT.Exp, scale=R.scale)\
                .then_inc(S["rec_decays"].handle, 1)

        def dve_q(dve, u, i):
            d, t = units[i]
            _, k, _, qT, _ = operands(d, t)
            dve.wait_ge(S["rec_decays"].handle, S["rec_decays"].at(1) + u)
            dve.wait_ge(S["rec_out"].handle, S["rec_out"].at(-1) + u)
            dve.wait_ge(S["rec_state"].handle, S["rec_state"].at(-1) + u)
            end = P - 1 if d == 0 else 0
            nc.vector.tensor_copy(R.total[:, i % 2:i % 2 + 1], R.decay[:, 0, end:end + 1])
            nc.vector.tensor_tensor(R.k_end[:, i % 2, :], k, R.rest_decay[:, :], ALU.mult)
            nc.vector.tensor_tensor(R.qd[:, i % 2, :, :], R.decay[:, :, :],
                                    qT.unsqueeze(1).to_broadcast([K, NL, P]), ALU.mult)\
                .then_inc(S["rec_q"].handle, 1)

        def pool_k(pool, u, i):
            d, t = units[i]
            kT = operands(d, t)[4]
            pool.wait_ge(S["rec_decays"].handle, S["rec_decays"].at(1) + u)
            pool.wait_ge(S["rec_scores"].handle, S["rec_scores"].at(-1) + u)
            nc.gpsimd.tensor_tensor(R.kd[:, i % 2, :, :], R.decay[:, 1:NL, :],
                                    kT.unsqueeze(1).to_broadcast([K, NL - 1, P]), ALU.mult)\
                .then_inc(S["rec_k"].handle, 1)

        def dve_mask(dve, u, i):
            d, t = units[i]
            dve.wait_ge(S["rec_scores"].handle, S["rec_scores"].at(1) + u)
            dve.wait_ge(S["rec_out"].handle, S["rec_out"].at(0) + u)
            nc.vector.tensor_tensor(R.masked[:, :, :], R.ps_scores[:, :, :], R.mask[:, d, :, :], ALU.mult)\
                .then_inc(S["rec_masked"].handle, 1)

        def dve_state(dve, u, i):
            d, t = units[i]
            dve.wait_ge(S["rec_out"].handle, S["rec_out"].at(1) + u)
            if d == 0:
                nc.vector.tensor_copy(o_acc(t), R.ps_out[i % 2][:, 0:P])
            else:
                nc.vector.tensor_tensor(o_acc(t), o_acc(t), R.ps_out[i % 2][:, 0:P], ALU.add)
            if i in last:
                nc.vector.engine_nop().then_inc(S["rec_state"].handle, 1)
            elif i in first:
                nc.vector.tensor_copy(R.state[:, :], R.ps_state[0:K, 0:P]).then_inc(S["rec_state"].handle, 1)
            else:
                nc.vector.scalar_tensor_tensor(out=R.state[:, :], in0=R.state[:, :], scalar=R.total[:, i % 2:i % 2 + 1],
                                               in1=R.ps_state[0:K, 0:P], op0=ALU.mult, op1=ALU.add)\
                    .then_inc(S["rec_state"].handle, 1)

        n = len(units)

        def tensor(pe, u):
            pe_sums(pe, u, 0)
            for i in range(n):
                pe_scores(pe, u + i, i)
                if i + 1 < n:
                    pe_sums(pe, u + i + 1, i + 1)
                pe_out(pe, u + i, i)

        def scalar(act, u):
            for i in range(n):
                act_decays(act, u + i, i)

        def gpsimd(pool, u):
            for i in range(n):
                pool_k(pool, u + i, i)

        def vector(dve, u):
            dve_q(dve, u, 0)
            for i in range(n):
                dve_mask(dve, u + i, i)
                if i + 1 < n:
                    dve_q(dve, u + i + 1, i + 1)
                dve_state(dve, u + i, i)
        return tensor, scalar, gpsimd, vector

    REC_PER_UNIT = ("rec_sums", "rec_decays", "rec_q", "rec_k", "rec_scores", "rec_masked", "rec_out", "rec_state")

    GH, GK, GV, RANK = 4, 64, 128, 16
    O_Q, O_K, O_V, O_G, O_Z = 0, 256, 512, 1024, 1536
    O_AQ, O_AK, O_AV, O_END = 1568, 2080, 2208, 2336
    s_gate = {n: signal(n, o) for n, o in (
        ("z_psum", "tensor"), ("z_ready", "scalar"), ("logit_psum", "tensor"), ("logit_low", "vector"),
        ("logit_log", "scalar"), ("gate_ready", "vector"))}

    def gla_gates(A, g):
        with ExitStack() as cx:
            w = sb(cx, "gla_w", [RANK, 2, GH * GK])
            b = sb(cx, "gla_b", [1, 2, GH * GK])
            zT = sb(cx, "gla_zT", [RANK, 4, 2, P])
            low = sb(cx, "gla_low", [P, 4, 512])
            mag = sb(cx, "gla_mag", [P, 4, 512])
            ps_z = [pb(cx, f"ps_z{i}", [P, 4, P]) for i in range(2)]
            ps_l = [pb(cx, f"ps_logit{i}", [P, 512]) for i in range(4)]
            S = s_gate

            @block.gpsimd
            def _(pool):
                load(pool, "pool", (w[:, :, :], a["gla_w_gate"][0].rearrange("d r n -> r d n")),
                     (b[:, :, :], a["gla_b_gate"][0:1]))
                pool.sem_inc(loads_ready.handle, 1)

            @block.tensor
            def _(pe):
                for d in range(2):
                    for t in range(4):
                        mm = nc.tensor.transpose(ps_z[d][0:RANK, t, :],
                                                 A[:, t, O_Z + d * RANK:O_Z + (d + 1) * RANK], ident)
                mm.then_inc(S["z_psum"].handle, 1)
                pe.wait_ge(S["z_ready"].handle, S["z_ready"].at(1))
                pe.wait_ge(loads_ready.handle, loads_ready.at(1))
                for t in range(4):
                    for d in range(2):
                        dst = ps_l[t][:, d * 256:(d + 1) * 256]
                        nc.tensor.matmul(dst, zT[:, t, d, :], w[:, d, :], start=True, stop=False)
                        mm = nc.tensor.matmul(dst, ones[0:1, :], b[:, d, :], start=False, stop=True)
                    mm.then_inc(S["logit_psum"].handle, 1)

            @block.scalar
            def _(act):
                act.wait_ge(S["z_psum"].handle, S["z_psum"].at(1))
                for d in range(2):
                    last = nc.scalar.activation(zT[:, :, d, :], ps_z[d][0:RANK, :, :], ACT.Copy)
                last.then_inc(S["z_ready"].handle, 1)
                nc.scalar.preload_act_table_set("natural_log_exp_and_others")
                for t in range(4):
                    act.wait_ge(S["logit_low"].handle, S["logit_low"].at(t + 1))
                    link_a(nc.scalar.activation(mag[:, t, :], ps_l[t][:, :], ACT.Abs))
                    link_a(nc.scalar.activation(mag[:, t, :], mag[:, t, :], ACT.Exp, scale=-1.0))
                    nc.scalar.activation(mag[:, t, :], mag[:, t, :], ACT.Ln, bias=1.0)\
                        .then_inc(S["logit_log"].handle, 1)

            @block.vector
            def _(dve):
                for t in range(4):
                    dve.wait_ge(S["logit_psum"].handle, S["logit_psum"].at(t + 1))
                    nc.vector.tensor_scalar(low[:, t, :], ps_l[t][:, :], 0.0, None, ALU.min)\
                        .then_inc(S["logit_low"].handle, 1)
                for t in range(4):
                    dve.wait_ge(S["logit_log"].handle, S["logit_log"].at(t + 1))
                    link_v(nc.vector.tensor_tensor(g[:, t, :, :].rearrange("p d n -> p (d n)"), low[:, t, :],
                                                   mag[:, t, :], ALU.subtract))
            S["z_psum"].passed(1), S["z_ready"].passed(1), loads_ready.passed(1)
            for k in ("logit_psum", "logit_low", "logit_log"):
                S[k].passed(4)
            meet()

    def gla_heads(A, g):
        with ExitStack() as cx:
            R = Recurrence(cx, GK, 1.0 / 16.0, hT[:, :, :].rearrange("p k n -> p (k n)"))
            qs = hT[:, KD - 1, 256:512].rearrange("p (t n) -> p t n", t=4)
            vs = A[:, :, O_AK:O_AV]
            o = A[:, :, O_AV:O_END]
            ks = sb(cx, "gla_k", [P, 4, GK])
            gs = sb(cx, "gla_g", [P, 4, 2, GK])
            qT = sb(cx, "gla_qT", [GK, 4, P])
            kT = sb(cx, "gla_kT", [GK, 4, P])
            sq = R.masked[:, 0:4, :]
            rstd = sb(cx, "gla_rstd", [P, 4])
            gain = sb(cx, "gla_gain", [P, GV])
            S = s_rec
            units = [(0, t) for t in (0, 1, 2, 3)] + [(1, t) for t in (1, 0, 3, 2)]
            tensor, scalar, gpsimd, vector = recurrence(
                R, units, first=(0, 4), last=(3, 7),
                operands=lambda d, t: (gs[:, t, d, :], ks[:, t, :], vs[:, t, :], qT[:, t, :], kT[:, t, :]),
                o_acc=lambda t: o[:, t, :])
            n = len(units)

            @block.gpsimd
            def _(pool):
                load(pool, "pool", *R.tables(), (gain[:, :], a["gla_out_norm"][0:1, :].partition_broadcast(P)))
                pool.sem_inc(loads_ready.handle, 1)
                with pool.Fori(0, GH) as h:
                    pool_chain.enter(h, 1)
                    pool.wait_ge(S["rec_head_done"].handle, S["rec_head_done"].at(0) + h)
                    nc.gpsimd.tensor_copy(qs, A[:, :, bass.ds(h * GK + O_Q, GK)])
                    nc.gpsimd.tensor_copy(ks[:, :, :], A[:, :, bass.ds(h * GK + O_K, GK)])
                    for t in range(4):
                        nc.gpsimd.tensor_copy(gs[:, t, :, :], g[:, t, :, bass.ds(h * GK, GK)])
                    nc.gpsimd.tensor_copy(vs, A[:, :, bass.ds(h * GV + O_V, GV)])\
                        .then_inc(S["rec_staged"].handle, 1)
                    gpsimd(pool, h * n)
                    pool.wait_ge(S["rec_squares"].handle, S["rec_squares"].at(1) + h)
                    settle(pool)
                    link_g(nc.gpsimd.tensor_scalar(rstd[:, :], rstd[:, :], 1.0 / GV, EPS_RMS, ALU.mult, ALU.add))
                    nc.gpsimd.tensor_tensor(rstd[:, :], rstd[:, :], half_power.to_broadcast([P, 4]), ALU.pow)\
                        .then_inc(S["rec_rms"].handle, 1)
                pool_chain.leave(GH)

            @block.tensor
            def _(pe):
                pe.wait_ge(loads_ready.handle, loads_ready.at(1))
                with pe.Fori(0, GH) as h:
                    pe.wait_ge(S["rec_staged"].handle, S["rec_staged"].at(1) + h)
                    pe.wait_ge(S["rec_decays"].handle, S["rec_decays"].at(0) + h * n)
                    settle(pe)
                    for t in range(4):
                        nc.tensor.transpose(R.ps_sums[0:GK, t, :], qs[:, t, :], ident)
                    for t in range(4):
                        mm = nc.tensor.transpose(R.ps_sums[0:GK, 4 + t, :], ks[:, t, :], ident)
                    mm.then_inc(S["rec_qk_psum"].handle, 1)
                    pe.wait_ge(S["rec_qk_ready"].handle, S["rec_qk_ready"].at(1) + h)
                    tensor(pe, h * n)

            @block.scalar
            def _(act):
                with act.Fori(0, GH) as h:
                    act.wait_ge(S["rec_qk_psum"].handle, S["rec_qk_psum"].at(1) + h)
                    nc.scalar.activation(qT[:, :, :], R.ps_sums[0:GK, 0:4, :], ACT.Copy, scale=GK ** -0.5)
                    nc.scalar.activation(kT[:, :, :], R.ps_sums[0:GK, 4:8, :], ACT.Copy)\
                        .then_inc(S["rec_qk_ready"].handle, 1)
                    scalar(act, h * n)

            @block.vector
            def _(dve):
                dve.wait_ge(loads_ready.handle, loads_ready.at(1))
                with dve.Fori(0, GH) as h:
                    dve_chain.enter(h, 5)
                    vector(dve, h * n)
                    dve.wait_ge(S["rec_state"].handle, S["rec_state"].at(n) + h * n)
                    link_v(nc.vector.tensor_tensor(sq, o, o, ALU.mult))
                    link_v(nc.vector.tensor_reduce(rstd[:, :], sq[:, :, :], AX.X, ALU.add))
                    nc.vector.sem_inc(S["rec_squares"].handle, 1)
                    link_v(nc.vector.tensor_tensor(o[:, :, :], o[:, :, :], gain[:, :].unsqueeze(1).to_broadcast([P, 4, GV]),
                                                   ALU.mult))
                    dve.wait_ge(S["rec_rms"].handle, S["rec_rms"].at(1) + h)
                    link_v(nc.vector.tensor_tensor(o[:, :, :], o[:, :, :],
                                                   rstd[:, :].unsqueeze(2).to_broadcast([P, 4, GV]), ALU.mult))
                    og = A[:, :, bass.ds(h * GV + O_G, GV)]
                    link_v(nc.vector.tensor_tensor(og, o[:, :, :], og, ALU.mult))
                    nc.vector.sem_inc(S["rec_head_done"].handle, 1)
                dve_chain.leave(GH)
            for k in REC_PER_UNIT:
                S[k].passed(GH * n)
            for k in ("rec_staged", "rec_head_done", "rec_qk_psum", "rec_qk_ready", "rec_rms", "rec_squares"):
                S[k].passed(GH)
            loads_ready.passed(1)
            meet()

    s_att = {n: signal(n, o) for n, o in (
        ("att_kT_psum", "tensor"), ("att_kT_ready", "scalar"),
        ("att_staged", "gpsimd"), ("att_q_psum", "tensor"), ("att_q_ready", "scalar"),
        ("att_scores", "tensor"), ("att_max", "vector"), ("att_probs", "scalar"), ("att_turned", "tensor"),
        ("att_probs_T", "vector"), ("att_out", "tensor"), ("att_taken", "vector"))}

    def attend(A, q_col, k_col, v_col, kv_heads, group, q_tiles, mask=None, sinks=None, scale=1.0):
        tiles = [t for t, _ in q_tiles]
        t0, nt = tiles[0], len(tiles)
        nkt = max(k for _, ks in q_tiles for k in ks) + 1 - t0
        with ExitStack() as cx:
            qs = sb(cx, "att_qs", [P, nt, group * ATT_D])
            qT = sb(cx, "att_qT", [ATT_D, group, nt, P])
            kT = sb(cx, "att_kT", [ATT_D, kv_heads, nkt, P])
            probs = sb(cx, "att_probs_buf", [P, 2, nkt * P])
            probsT = sb(cx, "att_probsT_buf", [P, 2, nkt, P])
            scr = sb(cx, "att_masked", [P, 2, nkt * P]) if mask is not None else None
            stat = sb(cx, "att_stat", [P, 2, 4])
            ps_s = [pb(cx, f"ps_att_s{i}", [P, 512]) for i in range(2)]
            ps_t = [pb(cx, f"ps_att_t{i}", [P, 4, P]) for i in range(2)]
            ps_o = [pb(cx, f"ps_att_o{i}", [P, 512]) for i in range(2)]
            ps_q = [pb(cx, f"ps_att_q{i}", [P, 4, P]) for i in range(2)]
            S = s_att
            units = [(g, i) for g in range(group) for i in range(nt)]
            n = len(units)
            per_sink = 1 if sinks is not None else 0

            @block.gpsimd
            def _(pool):
                with pool.Fori(0, kv_heads) as kv:
                    pool.wait_ge(S["att_q_psum"].handle, S["att_q_psum"].at(0) + kv * group)
                    nc.gpsimd.tensor_copy(qs[:, :, :], A[:, t0:t0 + nt, bass.ds(kv * (group * ATT_D) + q_col, group * ATT_D)])\
                        .then_inc(S["att_staged"].handle, 1)

            @block.tensor
            def _(pe):
                for kv in range(kv_heads):
                    if kv >= 2:
                        pe.wait_ge(S["att_kT_ready"].handle, S["att_kT_ready"].at(kv - 1))
                    for i in range(nkt):
                        mm = nc.tensor.transpose(ps_q[kv % 2][0:ATT_D, i, :],
                                                 A[:, t0 + i, k_col + kv * ATT_D:k_col + (kv + 1) * ATT_D], ident)
                    mm.then_inc(S["att_kT_psum"].handle, 1)
                pe.wait_ge(S["att_kT_ready"].handle, S["att_kT_ready"].at(kv_heads))

                def scores(u, kv, i):
                    g, qi = units[i]
                    nk = len(q_tiles[qi][1]) * P
                    pe.wait_ge(S["att_probs"].handle, S["att_probs"].at(-1) + u)
                    settle(pe)
                    nc.tensor.matmul(ps_s[i % 2][:, 0:nk], qT[:, g, qi, :],
                                     kT[:, bass.ds(kv, 1), 0:nk // P, :].rearrange("k h t n -> k (h t n)"),
                                     start=True, stop=True).then_inc(S["att_scores"].handle, 1)

                def turned(u, i):
                    pe.wait_ge(S["att_probs"].handle, S["att_probs"].at(1) + u)
                    pe.wait_ge(S["att_probs_T"].handle, S["att_probs_T"].at(-1) + u)
                    for k in range(len(q_tiles[units[i][1]][1])):
                        mm = nc.tensor.transpose(ps_t[i % 2][:, k, :], probs[:, i % 2, k * P:(k + 1) * P], ident)
                    mm.then_inc(S["att_turned"].handle, 1)

                def output(u, kv, i):
                    keys = q_tiles[units[i][1]][1]
                    pe.wait_ge(S["att_probs_T"].handle, S["att_probs_T"].at(1) + u)
                    pe.wait_ge(S["att_taken"].handle, S["att_taken"].at(-1) + u)
                    for k, t in enumerate(keys):
                        mm = nc.tensor.matmul(ps_o[i % 2][:, 0:ATT_D], probsT[:, i % 2, k, :],
                                              A[:, t, bass.ds(kv * ATT_D + v_col, ATT_D)],
                                              start=k == 0, stop=k == len(keys) - 1)
                    mm.then_inc(S["att_out"].handle, 1)

                with pe.Fori(0, kv_heads) as kv:
                    pe.wait_ge(S["att_staged"].handle, S["att_staged"].at(1) + kv)
                    for g in range(group):
                        pe.wait_ge(S["att_q_ready"].handle, S["att_q_ready"].at(g - 1) + kv * group)
                        settle(pe)
                        for i in range(nt):
                            mm = nc.tensor.transpose(ps_q[g % 2][0:ATT_D, i, :], qs[:, i, g * ATT_D:(g + 1) * ATT_D],
                                                     ident)
                        mm.then_inc(S["att_q_psum"].handle, 1)
                    pe.wait_ge(S["att_q_ready"].handle, S["att_q_ready"].at(group) + kv * group)
                    for i in range(n + 2):
                        if i < n:
                            scores(kv * n + i, kv, i)
                        if 1 <= i <= n:
                            turned(kv * n + i - 1, i - 1)
                        if i >= 2:
                            output(kv * n + i - 2, kv, i - 2)

            @block.scalar
            def _(act):
                for kv in range(kv_heads):
                    act.wait_ge(S["att_kT_psum"].handle, S["att_kT_psum"].at(kv + 1))
                    nc.scalar.activation(kT[:, kv, :, :], ps_q[kv % 2][0:ATT_D, 0:nkt, :], ACT.Copy)\
                        .then_inc(S["att_kT_ready"].handle, 1)
                with act.Fori(0, kv_heads) as kv:
                    act.wait_ge(S["att_out"].handle, S["att_out"].at(0) + kv * n)
                    for g in range(group):
                        act.wait_ge(S["att_q_psum"].handle, S["att_q_psum"].at(g + 1) + kv * group)
                        nc.scalar.activation(qT[:, g, :, :], ps_q[g % 2][0:ATT_D, 0:nt, :], ACT.Copy, scale=scale)\
                            .then_inc(S["att_q_ready"].handle, 1)
                    for i in range(n):
                        u = kv * n + i
                        g, qi = units[i]
                        nk = len(q_tiles[qi][1]) * P
                        act.wait_ge(S["att_max"].handle, S["att_max"].at(1) + u)
                        act.wait_ge(S["att_turned"].handle, S["att_turned"].at(-1) + u)
                        src = ps_s[i % 2][:, 0:nk] if mask is None else scr[:, i % 2, 0:nk]
                        if sinks is not None:
                            settle(nc.scalar)
                            nc.scalar.activation(stat[:, i % 2, 3:4],
                                                 sinks[:, bass.ds(kv * group + g, 1)], ACT.Exp, bias=stat[:, i % 2, 0:1])
                        nc.scalar.activation(probs[:, i % 2, 0:nk], src, ACT.Exp, bias=stat[:, i % 2, 0:1],
                                             accum_out=stat[:, i % 2, 1:2]).then_inc(S["att_probs"].handle, 1)

            @block.vector
            def _(dve):
                links = n + (n if mask is not None else 0) + (3 * n if sinks is not None else 0)

                def maxima(u, kv, i):
                    g, qi = units[i]
                    nk = len(q_tiles[qi][1]) * P
                    dve.wait_ge(S["att_scores"].handle, S["att_scores"].at(1) + u)
                    dve.wait_ge(S["att_taken"].handle, S["att_taken"].at(-1) + u)
                    src = ps_s[i % 2][:, 0:nk]
                    if mask is not None:
                        link_v(nc.vector.tensor_tensor(scr[:, i % 2, 0:nk], src, mask[:, qi, 0:nk], ALU.add))
                        src = scr[:, i % 2, 0:nk]
                    if sinks is None:
                        nc.vector.tensor_reduce(stat[:, i % 2, 0:1], src, AX.X, ALU.max, negate=True)\
                            .then_inc(S["att_max"].handle, 1)
                    else:
                        link_v(nc.vector.tensor_reduce(stat[:, i % 2, 0:1], src, AX.X, ALU.max))
                        link_v(nc.vector.tensor_tensor(stat[:, i % 2, 0:1], stat[:, i % 2, 0:1],
                                                       sinks[:, bass.ds(kv * group + g, 1)], ALU.max))
                        nc.vector.tensor_scalar(stat[:, i % 2, 0:1], stat[:, i % 2, 0:1], -1.0, None, ALU.mult)\
                            .then_inc(S["att_max"].handle, 1)

                def turn_probs(u, i):
                    nk = len(q_tiles[units[i][1]][1])
                    dve.wait_ge(S["att_turned"].handle, S["att_turned"].at(1) + u)
                    dve.wait_ge(S["att_out"].handle, S["att_out"].at(-1) + u)
                    nc.vector.tensor_copy(probsT[:, i % 2, 0:nk, :], ps_t[i % 2][:, 0:nk, :])\
                        .then_inc(S["att_probs_T"].handle, 1)

                def divide(u, kv, i):
                    g, qi = units[i]
                    if sinks is not None:
                        link_v(nc.vector.tensor_tensor(stat[:, i % 2, 1:2], stat[:, i % 2, 1:2], stat[:, i % 2, 3:4],
                                                       ALU.add))
                    link_v(nc.vector.reciprocal(stat[:, i % 2, 2:3], stat[:, i % 2, 1:2]))
                    dve.wait_ge(S["att_out"].handle, S["att_out"].at(1) + u)
                    dst = A[:, t0 + qi, bass.ds(kv * (group * ATT_D) + (q_col + g * ATT_D), ATT_D)]
                    nc.vector.tensor_scalar(dst, ps_o[i % 2][:, 0:ATT_D], stat[:, i % 2, 2:3], None, ALU.mult)\
                        .then_inc(S["att_taken"].handle, 1)

                with dve.Fori(0, kv_heads) as kv:
                    dve_chain.enter(kv, links)
                    for i in range(n + 2):
                        if i >= 2:
                            divide(kv * n + i - 2, kv, i - 2)
                        if i < n:
                            maxima(kv * n + i, kv, i)
                        if 1 <= i <= n:
                            turn_probs(kv * n + i - 1, i - 1)
                dve_chain.leave(kv_heads)
            for k in ("att_scores", "att_max", "att_probs", "att_turned", "att_probs_T", "att_out", "att_taken"):
                S[k].passed(kv_heads * n)
            S["att_kT_psum"].passed(kv_heads), S["att_kT_ready"].passed(kv_heads), S["att_staged"].passed(kv_heads)
            S["att_q_psum"].passed(kv_heads * group), S["att_q_ready"].passed(kv_heads * group)
            meet()

    s_qk = {n: signal(n, o) for n, o in (("qk_squares", "vector"), ("qk_rstd", "gpsimd"))}

    def even_queries_keys(A):
        heads = (O_AV - O_AQ) // ATT_D
        with ExitStack() as cx:
            sq = sb(cx, "qk_sq", [P, 4, heads * ATT_D])
            rstd = sb(cx, "qk_rstd_buf", [P, 4, heads])
            gain = sb(cx, "qk_gain", [P, heads, ATT_D])
            grid = sb(cx, "qk_grid", [P, 2, 2, 32])
            S = s_qk

            @block.gpsimd
            def _(pool):
                load(pool, "pool", (grid[:, :, :, :].rearrange("p f t n -> p (f t n)"), a["table"][:, C_GRID:C_CAUSAL]),
                     *[(gain[:, h, :], a["att_q_norm" if h < 8 else "att_k_norm"][0:1, :].partition_broadcast(P))
                       for h in range(heads)])
                pool.sem_inc(loads_ready.handle, 1)
                pool.wait_ge(S["qk_squares"].handle, S["qk_squares"].at(1))
                link_g(nc.gpsimd.tensor_scalar(rstd[:, :, :], rstd[:, :, :], 1.0 / ATT_D, EPS_RMS, ALU.mult, ALU.add))
                r = rstd[:, :, :].rearrange("p t h -> p (t h)")
                nc.gpsimd.tensor_tensor(r, r, half_power.to_broadcast([P, 4 * heads]), ALU.pow)\
                    .then_inc(S["qk_rstd"].handle, 1)

            @block.vector
            def _(dve):
                qk = A[:, :, O_AQ:O_AV]
                by_head = qk.rearrange("p t (h e) -> p t h e", e=ATT_D)
                link_v(nc.vector.tensor_tensor(sq[:, :, :], qk, qk, ALU.mult))
                link_v(nc.vector.tensor_reduce(rstd[:, :, :], sq[:, :, :].rearrange("p t (h e) -> p t h e", e=ATT_D),
                                               AX.X, ALU.add))
                nc.vector.sem_inc(S["qk_squares"].handle, 1)
                dve.wait_ge(loads_ready.handle, loads_ready.at(1))
                link_v(nc.vector.tensor_scalar(gain[:, 0:8, :], gain[:, 0:8, :], ATT_D ** -0.5, None, ALU.mult))
                dve.wait_ge(S["qk_rstd"].handle, S["qk_rstd"].at(1))
                for t in range(4):
                    link_v(nc.vector.tensor_tensor(by_head[:, t], by_head[:, t],
                                                   rstd[:, t, :].unsqueeze(2).to_broadcast([P, heads, ATT_D]), ALU.mult))
                    link_v(nc.vector.tensor_tensor(by_head[:, t], by_head[:, t], gain[:, :, :], ALU.mult))
                for i, t in enumerate(LAT_TILES):
                    pair = by_head[:, t].rearrange("p h (e two) -> p two h e", two=2)
                    x0, x1 = pair[:, 0], pair[:, 1]
                    cos = grid[:, 0, i, :].unsqueeze(1).to_broadcast([P, heads, 32])
                    sin = grid[:, 1, i, :].unsqueeze(1).to_broadcast([P, heads, 32])
                    part = [sq[:, j, 0:heads * 32].rearrange("p (h e) -> p h e", e=32) for j in range(4)]
                    nc.vector.tensor_tensor(part[0], x0, cos, ALU.mult)
                    nc.vector.tensor_tensor(part[1], x1, sin, ALU.mult)
                    nc.vector.tensor_tensor(part[2], x0, sin, ALU.mult)
                    link_v(nc.vector.tensor_tensor(part[3], x1, cos, ALU.mult))
                    nc.vector.tensor_tensor(x0, part[0], part[1], ALU.subtract)
                    link_v(nc.vector.tensor_tensor(x1, part[2], part[3], ALU.add))
            S["qk_squares"].passed(1), S["qk_rstd"].passed(1), loads_ready.passed(1)
            meet()

    def first_layer_even(A, g, Y):
        normalise(0, ALL_TILES)
        linear(a["even_w_in"][0], ALL_TILES, lambda e, t, lo, hi, ps: copy_on(e, A[:, t, lo:hi], ps),
               [(0, 896, 448), (896, 1792, 448), (1792, O_END, 272)])
        silu_columns(A, O_G, O_Z)
        gla_gates(A, g)
        even_queries_keys(A)
        attend(A, O_AQ, O_AK, O_AV, 2, 4, [(0, (0, 1)), (1, (0, 1)), (2, (0, 1, 2, 3)), (3, (0, 1, 2, 3))])
        gla_heads(A, g)
        turn(lambda t, k: A[:, t, O_G + k * P:O_G + (k + 1) * P] if k < 4 else
             A[:, t, O_AQ + (k - 4) * P:O_AQ + (k - 3) * P], ALL_TILES)

    s_silu = signal("silu_done", "scalar")

    def silu_columns(A, lo, hi):
        @block.scalar
        def _(act):
            nc.scalar.activation(A[:, :, lo:hi], A[:, :, lo:hi], ACT.Silu).then_inc(s_silu.handle, 1)
            act.wait_ge(s_silu.handle, s_silu.at(1))
        s_silu.passed(1)
        meet()

    def finish(tiles):
        done = sem("out_written")

        @block.sync
        def _(sp):
            sp.wait_ge(met["tensor"][0], met["tensor"][1])
            sp.wait_ge(met["scalar"][0], met["scalar"][1])
            sp.wait_ge(met["vector"][0], met["vector"][1])
            sp.wait_ge(met["gpsimd"][0], met["gpsimd"][1])
            sp.dma_start(out.rearrange("o (t p) d -> p (o t) d", p=P), X[:, tiles[0]:tiles[-1] + 1, :])\
                .then_inc(done, 16)
            sp.wait_ge(done, 16)
        root.close()


    HH = 8
    odd_second = [sem(f"odd_second{j}") for j in range(2)]
    c_sig = {n: signal(n, o) for n, o in (
        ("ctx_sums", "tensor"), ("ctx_decay", "scalar"), ("ctx_k_end", "vector"), ("ctx_out", "tensor"),
        ("ctx_state", "vector"))}
    s_odd = {n: signal(n, o) for n, o in (
        ("bound_exp", "scalar"), ("bound_ready", "vector"),
        ("hg_lb_psum", "tensor"), ("hg_lb_ready", "vector"), ("hg_psum", "tensor"), ("hg_taken", "scalar"),
        ("hg_forget", "vector"), ("hg_log", "scalar"), ("hg_k", "vector"))}

    def odd_mixer(O):
        w = by_rows(a["odd_w_in"][0])
        col = lambda which, h: w[:, :, bass.ds(h * P + which * D, P)]
        Q, FF, FB, I, OG = range(5)
        with ExitStack() as cx:
            R = Recurrence(cx, P, 1.0)
            lb = sb(cx, "hg_lb", [2, D])
            lb1 = sb(cx, "hg_lb1", [2, D])
            lbb = sb(cx, "hg_lbb", [P, 2, 2, P])
            qs = sb(cx, "hg_q", [P, 2, P])
            og = sb(cx, "hg_og", [P, 2, P])
            vs = sb(cx, "hg_v", [P, 4, P])
            tanh = sb(cx, "hg_tanh", [P, 4, 2, P])
            ks = sb(cx, "hg_k_buf", [P, 4, 2, P])
            gs = sb(cx, "hg_g", [P, 4, 2, P])
            qT = sb(cx, "hg_qT", [P, 2, P])
            kT = sb(cx, "hg_kT", [P, 2, 2, P])
            o = sb(cx, "hg_o", [P, 2, P])
            rstd = sb(cx, "hg_rstd", [P, 2])
            gain = sb(cx, "hg_gain", [P, P])
            ctx_total = sb(cx, "hg_ctx_total", [P, 2])
            sq = R.masked[:, 0:2, :]
            S, Z = s_rec, s_odd
            ctx_units = [(0, 0), (0, 1), (1, 1), (1, 0)]
            lat_units = [[(0, 2), (0, 3)], [(1, 3), (1, 2)]]
            operands = lambda d, t: (gs[:, t, d, :], ks[:, t, d, :], vs[:, t, :], qT[:, t - 2, :], kT[:, d, t - 2, :])
            seqs = [recurrence(R, lat_units[d], first=(), last=(1,), operands=operands,
                               o_acc=lambda t: o[:, t - 2, :]) for d in range(2)]

            @block.sync
            def _(sp):
                with sp.Fori(0, HH) as h:
                    for j, parts in enumerate(((FF, FB), (I, Q), (OG,))):
                        sp.wait_ge(ring_free[ring.slot(j)].handle, START + ring.round(j) + h)
                        view = slot_view(j, KD, 256)
                        for i, which in enumerate(parts):
                            landed = ring_loaded[ring.slot(j)] if i == 0 else odd_second[j]
                            sp.dma_start(view[:, :, i * P:(i + 1) * P], col(which, h)).then_inc(landed, 16)

            @block.gpsimd
            def _(pool):
                load(pool, "pool", *R.tables(), (gain[:, :], a["hgrn_out_norm"][0:1, :].partition_broadcast(P)),
                     (lb[:, :], a["hgrn_lower_bounds"][:, 0, :]), (lb1[:, :], a["hgrn_lower_bounds"][:, 1, :]))
                pool.sem_inc(loads_ready.handle, 1)
                with pool.Fori(0, HH) as h:
                    pool_chain.enter(h, 1)
                    for d in range(2):
                        seqs[d][2](pool, h * 4 + d * 2)
                    pool.wait_ge(S["rec_squares"].handle, S["rec_squares"].at(1) + h)
                    settle(pool)
                    link_g(nc.gpsimd.tensor_scalar(rstd[:, :], rstd[:, :], 1.0 / P, EPS_RMS, ALU.mult, ALU.add))
                    nc.gpsimd.tensor_tensor(rstd[:, :], rstd[:, :], half_power.to_broadcast([P, 2]), ALU.pow)\
                        .then_inc(S["rec_rms"].handle, 1)
                pool_chain.leave(HH)

            def lower_bounds_vector(dve):
                top, b0, b1, inv = (tanh[0:2, :, :, :].rearrange("p t d n -> p (t d n)"),
                                    lb[:, :], lb1[:, :], gs[0:2, :, :, :].rearrange("p t d n -> p (t d n)"))
                dve.wait_ge(loads_ready.handle, loads_ready.at(1))
                link_v(nc.vector.tensor_tensor(top, b0, b1, ALU.max))
                link_v(nc.vector.tensor_tensor(b0, b0, top, ALU.subtract))
                link_v(nc.vector.tensor_tensor(b1, b1, top, ALU.subtract))
                nc.vector.sem_inc(Z["bound_ready"].handle, 1)
                dve.wait_ge(Z["bound_exp"].handle, Z["bound_exp"].at(1))
                link_v(nc.vector.tensor_tensor(top, b0, b1, ALU.add))
                link_v(nc.vector.reciprocal(inv, top))
                link_v(nc.vector.tensor_tensor(top, b1, inv, ALU.mult))
                link_v(nc.vector.tensor_tensor(b1, b0, inv, ALU.mult))
                link_v(nc.vector.tensor_copy(b0, top))
                nc.vector.sem_inc(Z["bound_ready"].handle, 1)

            def groups():
                for t in range(4):
                    yield t, "f"
                    yield t, "iq"
                    if t >= 2:
                        yield t, "og"
            GR = list(groups())
            NG = len(GR)

            @block.tensor
            def _(pe):
                pe.wait_ge(Z["bound_ready"].handle, Z["bound_ready"].at(2))
                with pe.Fori(0, HH) as h:
                    pe.wait_ge(S["rec_head_done"].handle, S["rec_head_done"].at(0) + h)
                    for x, src in enumerate((lb, lb1)):
                        for d in range(2):
                            mm = nc.tensor.matmul(R.ps_rest[:, (2 * x + d) * P:(2 * x + d + 1) * P], sel(d, 2),
                                                  src[:, bass.ds(h * P, P)], start=True, stop=True)
                    mm.then_inc(Z["hg_lb_psum"].handle, 1)
                    for j in range(3):
                        await_item(pe, j, h)
                        if j < 2:
                            pe.wait_ge(odd_second[j], 16 + 16 * h)
                    banks = [R.ps_scores[:, 0:4, :], R.ps_scores[:, 4:8, :], R.ps_sums[:, 0:4, :], R.ps_sums[:, 4:8, :]]
                    for n, (t, kind) in enumerate(GR):
                        pe.wait_ge(Z["hg_taken"].handle, Z["hg_taken"].at(n - 3) + h * NG)
                        view = slot_view({"f": 0, "iq": 1, "og": 2}[kind], KD, 256)
                        width = {"f": 256, "iq": 256 if t >= 2 else P, "og": P}[kind]
                        dst = banks[n % 4].rearrange("p l n -> p (l n)")[:, 0:width]
                        for k in range(KD):
                            mm = nc.tensor.matmul(dst, hT[:, k, t * P:(t + 1) * P], view[:, k, 0:width],
                                                  start=k == 0, stop=k == KD - 1)
                        mm.then_inc(Z["hg_psum"].handle, 1)
                    for j in range(3):
                        free_item(j)
                    pe.wait_ge(Z["hg_k"].handle, Z["hg_k"].at(1) + h)
                    pe.wait_ge(Z["hg_taken"].handle, Z["hg_taken"].at(NG) + h * NG)
                    for t in range(2):
                        nc.tensor.transpose(R.ps_sums[:, t, :], qs[:, t, :], ident)
                    for d in range(2):
                        for t in range(2):
                            mm = nc.tensor.transpose(R.ps_sums[:, 4 + 2 * d + t, :], ks[:, 2 + t, d, :], ident)
                    mm.then_inc(S["rec_qk_psum"].handle, 1)
                    pe.wait_ge(Z["hg_log"].handle, Z["hg_log"].at(1) + h)
                    for d in range(2):
                        for i, t in enumerate((0, 1) if d == 0 else (1, 0)):
                            u = h * 4 + d * 2 + i
                            pe.wait_ge(c_sig["ctx_decay"].handle, c_sig["ctx_decay"].at(0) + u)
                            if i == 0:
                                pe.wait_ge(S["rec_decays"].handle, S["rec_decays"].at(0) + h * 4 + d * 2)
                                pe.wait_ge(S["rec_state"].handle, S["rec_state"].at(0) + h * 4 + d * 2)
                            nc.tensor.matmul(R.ps_rest[:, 0:P], R.rest[:, d, :], gs[:, t, d, :], start=True, stop=True)
                            nc.tensor.matmul(R.ps_rest[:, P:P + 1], gs[:, t, d, :], ones[:, 0:1], start=True, stop=True)\
                                .then_inc(c_sig["ctx_sums"].handle, 1)
                            pe.wait_ge(c_sig["ctx_k_end"].handle, c_sig["ctx_k_end"].at(1) + u)
                            pe.wait_ge(c_sig["ctx_state"].handle, c_sig["ctx_state"].at(0) + u)
                            nc.tensor.matmul(R.ps_state[:, 0:P], R.k_end[:, i, :], vs[:, t, :], start=True, stop=True)\
                                .then_inc(c_sig["ctx_out"].handle, 1)
                        pe.wait_ge(c_sig["ctx_state"].handle, c_sig["ctx_state"].at(2) + h * 4 + d * 2)
                        if d == 0:
                            pe.wait_ge(S["rec_qk_ready"].handle, S["rec_qk_ready"].at(1) + h)
                        seqs[d][0](pe, h * 4 + d * 2)

            @block.scalar
            def _(act):
                nc.scalar.preload_act_table_set("natural_log_exp_and_others")
                act.wait_ge(Z["bound_ready"].handle, Z["bound_ready"].at(1))
                nc.scalar.activation(lb[:, :], lb[:, :], ACT.Exp)
                nc.scalar.activation(lb1[:, :], lb1[:, :], ACT.Exp).then_inc(Z["bound_exp"].handle, 1)
                with act.Fori(0, HH) as h:
                    banks = [R.ps_scores[:, 0:4, :], R.ps_scores[:, 4:8, :], R.ps_sums[:, 0:4, :], R.ps_sums[:, 4:8, :]]
                    nc.scalar.preload_act_table_set("silu_and_others")
                    act.wait_ge(S["rec_head_done"].handle, S["rec_head_done"].at(0) + h)
                    for n, (t, kind) in enumerate(GR):
                        act.wait_ge(Z["hg_psum"].handle, Z["hg_psum"].at(n + 1) + h * NG)
                        src = banks[n % 4].rearrange("p l n -> p (l n)")
                        if kind == "f":
                            last = nc.scalar.activation(tanh[:, t, :, :].rearrange("p d n -> p (d n)"), src[:, 0:256],
                                                        ACT.Tanh, scale=0.5)
                        elif kind == "iq":
                            last = nc.scalar.activation(vs[:, t, :], src[:, 0:P], ACT.Copy)
                            if t >= 2:
                                last = nc.scalar.activation(qs[:, t - 2, :], src[:, P:256], ACT.Silu)
                        else:
                            last = nc.scalar.activation(og[:, t - 2, :], src[:, 0:P], ACT.Silu)
                        last.then_inc(Z["hg_taken"].handle, 1)
                    nc.scalar.preload_act_table_set("natural_log_exp_and_others")
                    act.wait_ge(Z["hg_forget"].handle, Z["hg_forget"].at(1) + h)
                    nc.scalar.activation(gs[:, :, :, :], gs[:, :, :, :], ACT.Ln).then_inc(Z["hg_log"].handle, 1)
                    act.wait_ge(S["rec_qk_psum"].handle, S["rec_qk_psum"].at(1) + h)
                    nc.scalar.activation(qT[:, :, :], R.ps_sums[:, 0:2, :], ACT.Copy)
                    nc.scalar.activation(kT[:, :, :, :].rearrange("p d t n -> p (d t) n"), R.ps_sums[:, 4:8, :], ACT.Copy)\
                        .then_inc(S["rec_qk_ready"].handle, 1)
                    for d in range(2):
                        for i in range(2):
                            u = h * 4 + d * 2 + i
                            act.wait_ge(c_sig["ctx_sums"].handle, c_sig["ctx_sums"].at(1) + u)
                            act.wait_ge(c_sig["ctx_k_end"].handle, c_sig["ctx_k_end"].at(0) + u)
                            act.wait_ge(S["rec_q"].handle, S["rec_q"].at(0) + h * 4 + d * 2)
                            nc.scalar.activation(R.rest_decay[:, :], R.ps_rest[:, 0:P], ACT.Exp)
                            nc.scalar.activation(ctx_total[:, i:i + 1], R.ps_rest[:, P:P + 1], ACT.Exp)\
                                .then_inc(c_sig["ctx_decay"].handle, 1)
                        act.wait_ge(c_sig["ctx_k_end"].handle, c_sig["ctx_k_end"].at(2) + h * 4 + d * 2)
                        seqs[d][1](act, h * 4 + d * 2)

            @block.vector
            def _(dve):
                lower_bounds_vector(dve)
                with dve.Fori(0, HH) as h:
                    dve_chain.enter(h, 27)
                    dve.wait_ge(Z["hg_lb_psum"].handle, Z["hg_lb_psum"].at(1) + h)
                    link_v(nc.vector.tensor_copy(lbb[:, :, :, :].rearrange("p x d n -> p (x d n)"), R.ps_rest[:, :]))
                    for t in range(4):
                        dve.wait_ge(Z["hg_taken"].handle, Z["hg_taken"].at(GR.index((t, "f")) + 1) + h * NG)
                        link_v(nc.vector.tensor_scalar(ks[:, t, :, :], tanh[:, t, :, :], -0.5, 0.5, ALU.mult, ALU.add))
                        link_v(nc.vector.tensor_tensor(ks[:, t, :, :], ks[:, t, :, :], lbb[:, 1, :, :], ALU.mult))
                        link_v(nc.vector.tensor_scalar(gs[:, t, :, :], tanh[:, t, :, :], 0.5, 0.5, ALU.mult, ALU.add))
                        link_v(nc.vector.tensor_tensor(gs[:, t, :, :], gs[:, t, :, :], lbb[:, 1, :, :], ALU.mult))
                        link_v(nc.vector.tensor_tensor(gs[:, t, :, :], gs[:, t, :, :], lbb[:, 0, :, :], ALU.add))
                    nc.vector.sem_inc(Z["hg_k"].handle, 1)
                    link_v(nc.vector.tensor_scalar(gs[:, :, :, :].rearrange("p t d n -> p (t d n)"),
                                                   gs[:, :, :, :].rearrange("p t d n -> p (t d n)"), 1e-18, None, ALU.max))
                    nc.vector.sem_inc(Z["hg_forget"].handle, 1)
                    for d in range(2):
                        for i, t in enumerate((0, 1) if d == 0 else (1, 0)):
                            u = h * 4 + d * 2 + i
                            dve.wait_ge(c_sig["ctx_decay"].handle, c_sig["ctx_decay"].at(1) + u)
                            dve.wait_ge(c_sig["ctx_out"].handle, c_sig["ctx_out"].at(-1) + u)
                            dve.wait_ge(S["rec_out"].handle, S["rec_out"].at(0) + h * 4 + d * 2)
                            nc.vector.tensor_tensor(R.k_end[:, i, :], ks[:, t, d, :], R.rest_decay[:, :], ALU.mult)\
                                .then_inc(c_sig["ctx_k_end"].handle, 1)
                            dve.wait_ge(c_sig["ctx_out"].handle, c_sig["ctx_out"].at(1) + u)
                            if i == 0:
                                nc.vector.tensor_copy(R.state[:, :], R.ps_state[:, 0:P])\
                                    .then_inc(c_sig["ctx_state"].handle, 1)
                            else:
                                dve.wait_ge(c_sig["ctx_state"].handle, c_sig["ctx_state"].at(0) + u)
                                nc.vector.scalar_tensor_tensor(
                                    out=R.state[:, :], in0=R.state[:, :], scalar=ctx_total[:, i:i + 1],
                                    in1=R.ps_state[:, 0:P], op0=ALU.mult, op1=ALU.add)\
                                    .then_inc(c_sig["ctx_state"].handle, 1)
                        dve.wait_ge(c_sig["ctx_state"].handle, c_sig["ctx_state"].at(2) + h * 4 + d * 2)
                        seqs[d][3](dve, h * 4 + d * 2)
                    dve.wait_ge(S["rec_state"].handle, S["rec_state"].at(4) + h * 4)
                    link_v(nc.vector.tensor_tensor(sq, o[:, :, :], o[:, :, :], ALU.mult))
                    link_v(nc.vector.tensor_reduce(rstd[:, :], sq, AX.X, ALU.add))
                    nc.vector.sem_inc(S["rec_squares"].handle, 1)
                    link_v(nc.vector.tensor_tensor(o[:, :, :], o[:, :, :], gain[:, :].unsqueeze(1).to_broadcast([P, 2, P]),
                                                   ALU.mult))
                    link_v(nc.vector.tensor_tensor(o[:, :, :], o[:, :, :], og[:, :, :], ALU.mult))
                    dve.wait_ge(S["rec_rms"].handle, S["rec_rms"].at(1) + h)
                    link_v(nc.vector.tensor_tensor(O[:, :, bass.ds(h * P, P)], o[:, :, :],
                                                   rstd[:, :].unsqueeze(2).to_broadcast([P, 2, P]), ALU.mult))
                    nc.vector.sem_inc(S["rec_head_done"].handle, 1)
                dve_chain.leave(HH)
            for k in REC_PER_UNIT:
                S[k].passed(HH * 4)
            for k in c_sig:
                c_sig[k].passed(HH * 4)
            for k in ("rec_head_done", "rec_qk_psum", "rec_qk_ready", "rec_rms", "rec_squares"):
                S[k].passed(HH)
            for k in ("hg_psum", "hg_taken"):
                Z[k].passed(HH * NG)
            for k in ("hg_lb_psum", "hg_forget", "hg_log", "hg_k"):
                Z[k].passed(HH)
            Z["bound_exp"].passed(1), Z["bound_ready"].passed(2), loads_ready.passed(1)
            ring.pos += 3 * HH
            meet()

    ALPHA = (2.0 * 2) ** 0.25
    ROT = 8
    QKV, K2, V2 = 1536, 1024, 1280
    HID2, WIDTH2 = 3584, 896
    EXPERTS = 8
    TWO_PI = 2 * np.pi
    PI_HI = 6.28125
    PI_MID = float(np.float32(np.round((TWO_PI - PI_HI) * 2 ** 20) / 2 ** 20))
    PI_LO = float(TWO_PI - PI_HI - PI_MID)
    ROUND = 1.5 * 2 ** 23
    s_rot = {n: signal(n, o) for n, o in (("rot_angle", "vector"), ("rot_done", "scalar"))}

    def rotation_table(rot):
        with ExitStack() as cx:
            pos = sb(cx, "rot_pos", [P, 2], I32)
            posf = sb(cx, "rot_posf", [P, 2])
            freq = sb(cx, "rot_freq", [P, ROT])
            turns = sb(cx, "rot_turns", [P, 2, ROT])
            S = s_rot

            @block.gpsimd
            def _(pool):
                with nc.allow_non_contiguous_dma("one position a partition"):
                    load(pool, "pool", (pos[:, :], a["positions_2"].rearrange("o (t p) -> p (o t)", p=P)),
                         (freq[:, :], a["table"][:, C_INVF:C_ALL]))
                pool.sem_inc(loads_ready.handle, 1)

            @block.vector
            def _(dve):
                dve.wait_ge(loads_ready.handle, loads_ready.at(1))
                link_v(nc.vector.tensor_copy(posf[:, :], pos[:, :]))
                cos, sin = rot[:, 0, :, :], rot[:, 1, :, :]
                for t in range(2):
                    last = nc.vector.tensor_scalar(sin[:, t, :], freq[:, :], posf[:, t:t + 1], None, ALU.mult)
                link_v(last)
                link_v(nc.vector.tensor_scalar(turns[:, :, :], sin, 1.0 / TWO_PI, None, ALU.mult))
                link_v(nc.vector.tensor_scalar(turns[:, :, :], turns[:, :, :], ROUND, None, ALU.add))
                link_v(nc.vector.tensor_scalar(turns[:, :, :], turns[:, :, :], ROUND, None, ALU.subtract))
                for part in (PI_HI, PI_MID, PI_LO):
                    link_v(nc.vector.scalar_tensor_tensor(out=sin, in0=turns[:, :, :], scalar=-part, in1=sin,
                                                          op0=ALU.mult, op1=ALU.add))
                link_v(nc.vector.tensor_scalar(cos, sin, np.pi / 2, None, ALU.add))
                link_v(nc.vector.tensor_scalar(turns[:, :, :], cos, np.pi, -TWO_PI, ALU.is_gt, ALU.mult))
                link_v(nc.vector.tensor_tensor(cos, cos, turns[:, :, :], ALU.add))
                limit = 3.1415925
                link_v(nc.vector.tensor_scalar(rot[:, :, :, :], rot[:, :, :, :], limit, -limit, ALU.min, ALU.max))
                nc.vector.sem_inc(S["rot_angle"].handle, 1)

            @block.scalar
            def _(act):
                act.wait_ge(S["rot_angle"].handle, S["rot_angle"].at(1))
                nc.scalar.activation(rot[:, :, :, :], rot[:, :, :, :], ACT.Sin)
            S["rot_angle"].passed(1), loads_ready.passed(1)
            meet()

    def rotate_partly(B, rot):
        heads = V2 // ATT_D
        with ExitStack() as cx:
            part = sb(cx, "rot_parts", [P, 4, heads, ROT])

            @block.vector
            def _(dve):
                for t in range(2):
                    x = B[:, t, 0:V2].rearrange("p (h e) -> p h e", e=ATT_D)
                    x1, x2 = x[:, :, 0:ROT], x[:, :, ROT:2 * ROT]
                    cos = rot[:, 0, t, :].unsqueeze(1).to_broadcast([P, heads, ROT])
                    sin = rot[:, 1, t, :].unsqueeze(1).to_broadcast([P, heads, ROT])
                    nc.vector.tensor_tensor(part[:, 0], x1, cos, ALU.mult)
                    nc.vector.tensor_tensor(part[:, 1], x2, sin, ALU.mult)
                    nc.vector.tensor_tensor(part[:, 2], x2, cos, ALU.mult)
                    link_v(nc.vector.tensor_tensor(part[:, 3], x1, sin, ALU.mult))
                    nc.vector.tensor_tensor(x1, part[:, 0], part[:, 1], ALU.subtract)
                    link_v(nc.vector.tensor_tensor(x2, part[:, 2], part[:, 3], ALU.add))
            meet()

    s_ln = {n: signal(n, o) for n, o in (("ln_var", "vector"), ("ln_rstd", "gpsimd"))}

    def layer_norm(Y, gain_row, shift_row):
        with ExitStack() as cx:
            gain = sb(cx, "ln_gain", [P, D])
            shift = sb(cx, "ln_shift", [P, D])
            stats = sb(cx, "ln_stats", [P, 2, 2, 6])
            mv = sb(cx, "ln_mv", [P, 2, 2])
            S = s_ln

            @block.gpsimd
            def _(pool):
                load(pool, "pool", (gain[:, :], gain_row.partition_broadcast(P)),
                     (shift[:, :], shift_row.partition_broadcast(P)))
                pool.sem_inc(loads_ready.handle, 1)
                pool.wait_ge(S["ln_var"].handle, S["ln_var"].at(1))
                var = mv[:, :, 1]
                link_g(nc.gpsimd.tensor_scalar(var, var, 1.0, EPS_LN, ALU.mult, ALU.add))
                nc.gpsimd.tensor_tensor(var, var, half_power.to_broadcast([P, 2]), ALU.pow)\
                    .then_inc(S["ln_rstd"].handle, 1)

            @block.vector
            def _(dve):
                for i, t in enumerate(LAT_TILES):
                    link_v(nc.vector.scalar_tensor_tensor(out=X[:, t, :], in0=X[:, t, :], scalar=ALPHA, in1=Y[:, t, :],
                                                          op0=ALU.mult, op1=ALU.add))
                    for h in range(2):
                        last = nc.vector.bn_stats(stats[:, i, h, :], X[:, t, h * 512:(h + 1) * 512])
                    link_v(last)
                    link_v(nc.vector.bn_aggr(mv[:, i, :], stats[:, i, :, :]))
                nc.vector.sem_inc(S["ln_var"].handle, 1)
                dve.wait_ge(loads_ready.handle, loads_ready.at(1))
                dve.wait_ge(S["ln_rstd"].handle, S["ln_rstd"].at(1))
                for i, t in enumerate(LAT_TILES):
                    link_v(nc.vector.tensor_scalar(X[:, t, :], X[:, t, :], mv[:, i, 0:1], mv[:, i, 1:2],
                                                   ALU.subtract, ALU.mult))
                    link_v(nc.vector.tensor_tensor(X[:, t, :], X[:, t, :], gain[:, :], ALU.mult))
                    link_v(nc.vector.tensor_tensor(X[:, t, :], X[:, t, :], shift[:, :], ALU.add))
            S["ln_var"].passed(1), S["ln_rstd"].passed(1), loads_ready.passed(1)
            meet()

    s_ple = {n: signal(n, o) for n, o in (("ple_gate", "scalar"),)}

    def per_layer_input(layer, Y, turns=None):
        turn(lambda t, k: X[:, t, k * P:(k + 1) * P], LAT_TILES)
        with ExitStack() as cx:
            G = sb(cx, "ple_gate_buf", [P, 4, D])
            pin = sb(cx, "ple_in", [P, 4, 256])

            @block.scalar
            def _(act):
                load(act, "act", (pin[:, 2:4, :], a["p_2"][layer].rearrange("o (t p) d -> p (o t) d", p=P)))
            linear(a["w_ple_gate_2"][layer], LAT_TILES, lambda e, t, lo, hi, ps: copy_on(e, G[:, t, lo:hi], ps),
                   [(0, 512, 512), (512, 1024, 512)], turns=turns)

            @block.scalar
            def _(act):
                nc.scalar.activation(G[:, 2:4, :], G[:, 2:4, :], ACT.Sigmoid)
            turn(lambda t, k: pin[:, t, k * P:(k + 1) * P], LAT_TILES, 2)
            linear(a["w_ple_proj_2"][layer], LAT_TILES, lambda e, t, lo, hi, ps: copy_on(e, Y[:, t, lo:hi], ps),
                   [(0, 1024, 512)], parts=2, turns=turns)

            @block.vector
            def _(dve):
                link_v(nc.vector.tensor_tensor(G[:, 2:4, :], G[:, 2:4, :], Y[:, 2:4, :], ALU.mult))
                link_v(nc.vector.tensor_tensor(X[:, 2:4, :], X[:, 2:4, :], G[:, 2:4, :], ALU.add))
            meet()

    def second_attention(layer, rot, sinks):
        with ExitStack() as cx:
            B = sb(cx, "qkv", [P, 2, QKV])
            mask = sb(cx, "att_mask", [P, 2, 256])
            turn(lambda t, k: X[:, t, k * P:(k + 1) * P], LAT_TILES)

            @block.scalar
            def _(act):
                lo = C_CAUSAL + layer * 512
                load(act, "act", (mask[:, :, :].rearrange("p t n -> p (t n)"), a["table"][:, lo:lo + 512]))
            linear(a["w_qkv_2"][layer], LAT_TILES, lambda e, t, lo, hi, ps: copy_on(e, B[:, t - 2, lo:hi], ps),
                   [(0, 768, 384), (768, 1536, 384)])
            rotate_partly(B, rot)
            attend(B, 0, K2, V2, 4, 4, [(0, (0,)), (1, (0, 1))], mask=mask, sinks=sinks, scale=ATT_D ** -0.5)
            turn(lambda t, k: B[:, t - 2, k * P:(k + 1) * P], LAT_TILES)

    s_moe = {n: signal(n, o) for n, o in (
        ("moe_logits", "tensor"), ("moe_top", "vector"), ("moe_exp", "scalar"), ("moe_chosen", "vector"),
        ("moe_ranks", "tensor"), ("moe_table", "vector"), ("moe_sel", "vector"), ("moe_gather", "tensor"),
        ("moe_xg", "scalar"), ("moe_scatter", "tensor"), ("moe_added", "vector"))}
    ye_clear = signal("ye_clear", "vector")
    CHUNKS2 = HID2 // WIDTH2
    passes_of = {}

    def experts(Y):
        S = s_moe
        turn(lambda t, k: X[:, t, k * P:(k + 1) * P], LAT_TILES)
        with ExitStack() as cx:
            router = sb(cx, "moe_router", [P, KD, EXPERTS])
            lg = sb(cx, "moe_lg", [P, 2, EXPERTS])
            top = sb(cx, "moe_top_buf", [P, 2, 8])
            idx = sb(cx, "moe_idx", [P, 2, 8], U32)
            idf = sb(cx, "moe_idf", [P, 2, 8])
            e1 = sb(cx, "moe_e1", [P, 2])
            w01 = sb(cx, "moe_w01", [P, 2, 2])
            one = sb(cx, "moe_one", [P, 2, 2, EXPERTS])
            chosen = sb(cx, "moe_chosen_buf", [P, 2, EXPERTS])
            gates = sb(cx, "moe_gates", [P, 2, EXPERTS, 2])
            place = sb(cx, "moe_place", [P, 2, EXPERTS, 2])
            row = sb(cx, "moe_row", [1, 4, EXPERTS])
            grid = sb(cx, "moe_grid", [1, 4, 16, EXPERTS])
            table = sb(cx, "moe_table_buf", [1, 2, 16], I32)
            total = sb(cx, "moe_total", [1, 1], I32)
            totf = sb(cx, "moe_totf", [1, 1])
            tabf = sb(cx, "moe_tabf", [1, 2, 16])
            pick = sb(cx, "moe_pick", [P, 2, P])
            pick_g = sb(cx, "moe_pick_g", [P, 2, P])
            xg = sb(cx, "moe_xg_buf", [P, KD, P])
            back = sb(cx, "moe_back", [P, 2, P])
            ye = sb(cx, "moe_ye", [P, 1, D])
            H = Hidden(cx, WIDTH2)
            iota = const[:, C_IOTA:C_IOTA + P]
            tri = const[:, C_TRI:C_TRI + P]
            FS = s_ffn
            add = lambda y, ps: nc.vector.tensor_tensor(y, y, ps, ALU.add)
            pe_gate, pe_up, pe_turn, pe_down, act_silu, act_turned, dve_hidden, dve_add = ffn_steps(
                H, lambda k, t: xg[:, k, :], ye, add)

            @block.gpsimd
            def _(pool):
                load(pool, "pool", (router[:, :, :], a["w_router_2"][0].rearrange("(k p) e -> p k e", p=P)))
                pool.sem_inc(loads_ready.handle, 1)

            @block.tensor
            def _(pe):
                pe.wait_ge(loads_ready.handle, loads_ready.at(1))
                for i, t in enumerate(LAT_TILES):
                    for k in range(KD):
                        mm = nc.tensor.matmul(H.ps_g[:, i, 0:EXPERTS], hT[:, k, t * P:(t + 1) * P], router[:, k, :],
                                              start=k == 0, stop=k == KD - 1)
                mm.then_inc(S["moe_logits"].handle, 1)
                pe.wait_ge(S["moe_chosen"].handle, S["moe_chosen"].at(1))
                nc.tensor.matmul(H.ps_u[:, 0, 0:EXPERTS], tri, chosen[:, 0, :], start=True, stop=True)
                nc.tensor.matmul(H.ps_u[:, 1, 0:EXPERTS], ones, chosen[:, 0, :], start=True, stop=False)
                nc.tensor.matmul(H.ps_u[:, 1, 0:EXPERTS], tri, chosen[:, 1, :], start=False, stop=True)
                nc.tensor.matmul(H.ps_y[:, 0, 0:EXPERTS], ones, chosen[:, 0, :], start=True, stop=False)
                nc.tensor.matmul(H.ps_y[:, 0, 0:EXPERTS], ones, chosen[:, 1, :], start=False, stop=True)\
                    .then_inc(S["moe_ranks"].handle, 1)

            @block.scalar
            def _(act):
                act.wait_ge(S["moe_top"].handle, S["moe_top"].at(1))
                nc.scalar.activation(e1[:, :], e1[:, :], ACT.Exp).then_inc(S["moe_exp"].handle, 1)

            @block.vector
            def _(dve):
                dve.wait_ge(S["moe_logits"].handle, S["moe_logits"].at(1))
                link_v(nc.vector.tensor_copy(lg[:, :, :], H.ps_g[:, :, 0:EXPERTS]))
                for i in range(2):
                    link_v(nc.vector.max(top[:, i, :], lg[:, i, :]))
                    link_v(nc.vector.max_index(idx[:, i, :], top[:, i, :], lg[:, i, :]))
                link_v(nc.vector.tensor_copy(idf[:, :, :], idx[:, :, :]))
                link_v(nc.vector.tensor_tensor(e1[:, :], top[:, :, 1], top[:, :, 0], ALU.subtract))
                nc.vector.sem_inc(S["moe_top"].handle, 1)
                dve.wait_ge(S["moe_exp"].handle, S["moe_exp"].at(1))
                link_v(nc.vector.tensor_scalar(w01[:, :, 1], e1[:, :], 1.0, None, ALU.add))
                link_v(nc.vector.reciprocal(w01[:, :, 0], w01[:, :, 1]))
                link_v(nc.vector.tensor_tensor(w01[:, :, 1], e1[:, :], w01[:, :, 0], ALU.mult))
                for i in range(2):
                    for c in range(2):
                        link_v(nc.vector.tensor_scalar(one[:, i, c, :], iota[:, 0:EXPERTS], idf[:, i, c:c + 1], None,
                                                       ALU.is_equal))
                link_v(nc.vector.tensor_tensor(chosen[:, :, :], one[:, :, 0, :], one[:, :, 1, :], ALU.add))
                nc.vector.sem_inc(S["moe_chosen"].handle, 1)
                for i in range(2):
                    link_v(nc.vector.tensor_scalar(gates[:, i, :, 0], one[:, i, 0, :], w01[:, i, 0:1], None, ALU.mult))
                    link_v(nc.vector.scalar_tensor_tensor(out=gates[:, i, :, 0], in0=one[:, i, 1, :],
                                                          scalar=w01[:, i, 1:2], in1=gates[:, i, :, 0],
                                                          op0=ALU.mult, op1=ALU.add))
                link_v(nc.vector.tensor_copy(gates[:, :, :, 1], gates[:, :, :, 0]))
                dve.wait_ge(S["moe_ranks"].handle, S["moe_ranks"].at(1))
                link_v(nc.vector.scalar_tensor_tensor(out=place[:, :, :, 0], in0=H.ps_u[:, :, 0:EXPERTS], scalar=1000.0,
                                                      in1=chosen[:, :, :], op0=ALU.add, op1=ALU.mult))
                link_v(nc.vector.tensor_scalar(place[:, :, :, 0], place[:, :, :, 0], 1000.0, None, ALU.subtract))
                link_v(nc.vector.tensor_scalar(place[:, :, :, 1], place[:, :, :, 0], float(P), None, ALU.subtract))
                cnt, start_, run, two = row[:, 0, :], row[:, 1, :], row[:, 2, :], row[:, 3, :]
                link_v(nc.vector.tensor_copy(run, H.ps_y[0:1, 0, 0:EXPERTS]))
                link_v(nc.vector.tensor_scalar(cnt, run, 0.5, None, ALU.is_gt))
                link_v(nc.vector.tensor_scalar(two, run, P + 0.5, None, ALU.is_gt))
                link_v(nc.vector.tensor_tensor(cnt, cnt, two, ALU.add))
                link_v(nc.vector.tensor_tensor_scan(run, ones[0:1, 0:EXPERTS], cnt, 0.0, ALU.mult, ALU.add))
                link_v(nc.vector.tensor_tensor(start_, run, cnt, ALU.subtract))
                link_v(nc.vector.tensor_copy(total[:, :], run[:, EXPERTS - 1:EXPERTS]))
                twice_e = const[0:1, C_MISC + 8:C_MISC + 16]
                number = const[0:1, C_MISC + 16:C_MISC + 32]
                rows = lambda r: r.unsqueeze(1).to_broadcast([1, 16, EXPERTS])
                off, inside, low, val = (grid[:, j, :, :] for j in range(4))
                link_v(nc.vector.tensor_tensor(off, number.unsqueeze(2).to_broadcast([1, 16, EXPERTS]), rows(start_),
                                               ALU.subtract))
                link_v(nc.vector.tensor_tensor(inside, off, rows(cnt), ALU.is_lt))
                link_v(nc.vector.tensor_scalar(low, off, 0.0, None, ALU.is_ge))
                link_v(nc.vector.tensor_tensor(inside, inside, low, ALU.mult))
                link_v(nc.vector.tensor_tensor(low, inside, rows(twice_e), ALU.mult))
                link_v(nc.vector.tensor_tensor(off, inside, off, ALU.mult))
                link_v(nc.vector.tensor_tensor(val, low, off, ALU.add))
                link_v(nc.vector.tensor_reduce(tabf[:, 0, :], val, AX.X, ALU.add))
                link_v(nc.vector.tensor_reduce(tabf[:, 1, :], low, AX.X, ALU.add))
                link_v(nc.vector.tensor_scalar(tabf[:, 1, :], tabf[:, 1, :], 0.5, None, ALU.mult))
                link_v(nc.vector.tensor_copy(table[:, :, :], tabf[:, :, :]))
                nc.vector.sem_inc(S["moe_table"].handle, 1)
                link_v(nc.vector.memset(Y[:, 2:4, :], 0.0))

            def passes(eng, name):
                eng.wait_ge(S["moe_table"].handle, S["moe_table"].at(1))
                n = eng.value_load(total[0:1, 0:1], min_val=1, max_val=11)
                passes_of[name] = n
                return n

            @block.sync
            def _(sp):
                with sp.Fori(0, passes(sp, "sync")) as p:
                    e = sp.value_load(table[0:1, 1, bass.ds(p, 1)], min_val=0, max_val=EXPERTS - 1)
                    for c in range(CHUNKS2):
                        for j, w in ((3 * c, "w_exp_gate_2"), (3 * c + 1, "w_exp_up_2")):
                            src = a[w][0][bass.ds(e, 1)].rearrange("o (k p) n -> p (o k) n", p=P)
                            stream(sp, j, src[:, :, c * WIDTH2:(c + 1) * WIDTH2], p * CHUNKS2)
                        src = a["w_exp_down_2"][0][bass.ds(e, 1), c * WIDTH2:(c + 1) * WIDTH2, :]
                        stream(sp, 3 * c + 2, src.rearrange("o (k p) n -> p (o k) n", p=P), p * CHUNKS2)

            @block.tensor
            def _(pe):
                with pe.Fori(0, passes(pe, "tensor")) as p:
                    n0 = p * CHUNKS2
                    pe.wait_ge(S["moe_sel"].handle, S["moe_sel"].at(1) + p)
                    pe.wait_ge(FS["ffn_turned_taken"].handle, FS["ffn_turned_taken"].at(0) + n0)
                    pe.wait_ge(FS["ffn_silu"].handle, FS["ffn_silu"].at(0) + n0)
                    for k in range(KD):
                        for i in range(2):
                            nc.tensor.matmul(H.ps_t[:, k, :], X[:, 2 + i, k * P:(k + 1) * P], pick[:, i, :],
                                             start=i == 0, stop=i == 1)
                    for i in range(2):
                        mm = nc.tensor.transpose(H.ps_g[:, 0, i * P:(i + 1) * P], pick_g[:, i, :], ident)
                    mm.then_inc(S["moe_gather"].handle, 1)
                    pe.wait_ge(S["moe_xg"].handle, S["moe_xg"].at(1) + p)
                    views = [(slot_view(3 * c, KD, WIDTH2), slot_view(3 * c + 1, KD, WIDTH2),
                              down_view(3 * c + 2, WIDTH2)) for c in range(CHUNKS2)]
                    await_item(pe, 0, n0)
                    pe_gate(pe, n0, views[0][0], 0)
                    await_item(pe, 1, n0)
                    pe_up(pe, n0, views[0][1], 0)
                    for c in range(CHUNKS2):
                        free_item(3 * c)
                        free_item(3 * c + 1)
                        if c + 1 < CHUNKS2:
                            await_item(pe, 3 * c + 3, n0)
                            pe_gate(pe, n0 + c + 1, views[c + 1][0], 0)
                        pe_turn(pe, n0 + c)
                        if c + 1 < CHUNKS2:
                            await_item(pe, 3 * c + 4, n0)
                            pe_up(pe, n0 + c + 1, views[c + 1][1], 0)
                        await_item(pe, 3 * c + 2, n0)
                        pe_down(pe, n0 + c, views[c][2])
                        free_item(3 * c + 2)
                    pe.wait_ge(FS["ffn_added"].handle, FS["ffn_added"].at(CHUNKS2) + n0)
                    for i in range(2):
                        pe.wait_ge(S["moe_added"].handle, S["moe_added"].at(i) + p * 2)
                        for h in range(2):
                            mm = nc.tensor.matmul(H.ps_y[:, h, :], back[:, i, :], ye[:, 0, h * 512:(h + 1) * 512],
                                                  start=True, stop=True)
                        mm.then_inc(S["moe_scatter"].handle, 1)

            @block.scalar
            def _(act):
                nc.scalar.preload_act_table_set("silu_and_others")
                with act.Fori(0, passes(act, "scalar")) as p:
                    n0 = p * CHUNKS2
                    act.wait_ge(S["moe_gather"].handle, S["moe_gather"].at(1) + p)
                    act.wait_ge(S["moe_scatter"].handle, S["moe_scatter"].at(0) + p * 2)
                    nc.scalar.activation(xg[:, :, :], H.ps_t[:, :, :], ACT.Copy)
                    nc.scalar.activation(back[:, :, :].rearrange("p t n -> p (t n)"), H.ps_g[:, 0, 0:256], ACT.Copy)\
                        .then_inc(S["moe_xg"].handle, 1)
                    act_silu(act, n0)
                    for c in range(CHUNKS2):
                        if c + 1 < CHUNKS2:
                            act_silu(act, n0 + c + 1)
                        act_turned(act, n0 + c)

            @block.vector
            def _(dve):
                with dve.Fori(0, passes(dve, "vector")) as p:
                    n0 = p * CHUNKS2
                    code = dve.value_load(table[0:1, 0, bass.ds(p, 1)], min_val=0, max_val=2 * EXPERTS - 1)
                    flat = lambda x, i: x[:, i, :, :].rearrange("p e h -> p (e h)")[:, bass.ds(code, 1)]
                    dve.wait_ge(S["moe_gather"].handle, S["moe_gather"].at(0) + p)
                    for i in range(2):
                        nc.vector.tensor_scalar(pick[:, i, :], iota, flat(place, i), None, ALU.is_equal)
                        last = nc.vector.tensor_scalar(pick_g[:, i, :], iota, flat(place, i), flat(gates, i),
                                                       ALU.is_equal, ALU.mult)
                    last.then_inc(S["moe_sel"].handle, 1)
                    dve.wait_ge(S["moe_scatter"].handle, S["moe_scatter"].at(0) + p * 2)
                    nc.vector.memset(ye[:, :, :], 0.0).then_inc(ye_clear.handle, 1)
                    dve.wait_ge(ye_clear.handle, ye_clear.at(1) + p)
                    dve_hidden(dve, n0)
                    for c in range(CHUNKS2):
                        if c + 1 < CHUNKS2:
                            dve_hidden(dve, n0 + c + 1)
                        dve_add(dve, n0 + c, 0)
                    for i in range(2):
                        dve.wait_ge(S["moe_scatter"].handle, S["moe_scatter"].at(i + 1) + p * 2)
                        dve.wait_ge(S["moe_added"].handle, S["moe_added"].at(0) + p * 2)
                        add(Y[:, 2 + i, :], H.ps_y[:, :, :].rearrange("p h n -> p (h n)"))\
                            .then_inc(S["moe_added"].handle, 1)
            loads_ready.passed(1)
            meet()


    def rest():
        modulate(1)
        normalise(0, ALL_TILES)
        O = X[:, 0:2, :]
        odd_mixer(O)
        turn(lambda t, k: O[:, t - 2, k * P:(k + 1) * P], LAT_TILES)
        with ExitStack() as cx:
            Y = sb(cx, "Y2", [P, 4, D])
            linear(a["odd_w_out"][0], LAT_TILES, lambda e, t, lo, hi, ps: copy_on(e, Y[:, t, lo:hi], ps),
                   [(0, 512, 512), (512, 1024, 512)])
            add_gated(0, Y, LAT_TILES)
            normalise(1, LAT_TILES)
            feed_forward(a["ffn_w_gate"][1], a["ffn_w_up"][1], a["ffn_w_down"][1], 704, LAT_TILES, Y)
            add_gated(1, Y, LAT_TILES)
        with ExitStack() as cx:
            rot = sb(cx, "rot", [P, 2, 2, ROT])
            sinks = sb(cx, "sinks", [P, 16])
            Y = sb(cx, "Y3", [P, 4, D])
            rotation_table(rot)

            @block.scalar
            def _(act):
                load(act, "act", (sinks[:, :], a["sinks_2"][0:1, :].partition_broadcast(P)))
            for layer in range(2):
                second_attention(layer, rot, sinks if layer == 1 else None)
                linear(a["w_o_2"][layer], LAT_TILES, lambda e, t, lo, hi, ps: copy_on(e, Y[:, t, lo:hi], ps),
                       [(0, 512, 512), (512, 1024, 512)])
                layer_norm(Y, a["ln_mix_g_2"][layer:layer + 1, :], a["ln_mix_b_2"][layer:layer + 1, :])
                if layer == 0:
                    turn(lambda t, k: X[:, t, k * P:(k + 1) * P], LAT_TILES)
                    feed_forward(a["w_ffn_gate_2"][0], a["w_ffn_up_2"][0], a["w_ffn_down_2"][0], WIDTH2, LAT_TILES, Y)
                else:
                    experts(Y)
                layer_norm(Y, a["ln_ffn_g_2"][layer:layer + 1, :], a["ln_ffn_b_2"][layer:layer + 1, :])
                per_layer_input(layer, Y, passes_of if layer == 1 else None)
        finish(LAT_TILES)
    start()
    modulate(0)
    with ExitStack() as cx:
        A = sb(cx, "even_A", [P, 4, O_END])
        with ExitStack() as cy:
            g = sb(cy, "even_g", [P, 4, 2, GH * GK])
            first_layer_even(A, g, None)
        Y = A[:, :, 0:D]
        linear(a["even_w_out"][0], ALL_TILES, lambda e, t, lo, hi, ps: copy_on(e, Y[:, t, lo:hi], ps),
               [(0, 512, 512), (512, 1024, 512)])
        add_gated(0, Y, ALL_TILES)
    with ExitStack() as cx:
        Y = sb(cx, "Y", [P, 4, D])
        normalise(1, ALL_TILES)
        feed_forward(a["ffn_w_gate"][0], a["ffn_w_up"][0], a["ffn_w_down"][0], 704, ALL_TILES, Y)
        add_gated(1, Y, ALL_TILES)
    rest()


_INS = ["x", "c", "ctx", "c_ctx", "mod_w", "mod_b", "norm_pre_mix", "norm_post_mix", "norm_pre_ffn", "norm_post_ffn",
        "even_w_in", "gla_w_gate", "gla_b_gate", "gla_out_norm", "att_q_norm", "att_k_norm", "even_w_out",
        "odd_w_in", "hgrn_lower_bounds", "hgrn_out_norm", "odd_w_out", "ffn_w_gate", "ffn_w_up", "ffn_w_down",
        "p_2", "positions_2", "w_qkv_2", "w_o_2", "ln_mix_g_2", "ln_mix_b_2", "ln_ffn_g_2", "ln_ffn_b_2", "sinks_2",
        "w_ffn_gate_2", "w_ffn_up_2", "w_ffn_down_2", "w_router_2", "w_exp_gate_2", "w_exp_up_2", "w_exp_down_2",
        "w_ple_proj_2", "w_ple_gate_2"]


def kernel(**inputs):
    import concourse.bacc as bacc
    from concourse.bass_utils import run_bass_kernel_spmd

    nc = bacc.Bacc("TRN2", target_bir_lowering=False, num_devices=1)
    arrays, access = {}, {}
    inputs["table"] = constants()
    for name in _INS + ["table"]:
        x = np.ascontiguousarray(inputs[name])
        arrays[f"in_{name}_dram"] = x
        access[name] = nc.dram_tensor(f"in_{name}_dram", x.shape, mybir.dt.from_np(x.dtype),
                                      kind="ExternalInput").ap()
    out = nc.dram_tensor("out_0_dram", (1, 256, 1024), F32, kind="ExternalOutput").ap()
    program(nc, access, out)
    r = run_bass_kernel_spmd(nc, [arrays], core_ids=[0])
    return r.results[0]["out_0_dram"]
```

```python
from contextlib import ExitStack

import numpy as np
import concourse.bass as bass
from concourse import mybir

F32 = mybir.dt.float32
I32 = mybir.dt.int32
U32 = mybir.dt.uint32
ALU = mybir.AluOpType
ACT = mybir.ActivationFunctionType
AX = mybir.AxisListType

P = 128
D = 1024
KD = D // P
CTX_TILES = (0, 1)
LAT_TILES = (2, 3)
ALL_TILES = CTX_TILES + LAT_TILES
START = 4
SLOTS = 3
SLOT = 7168
EPS_RMS = 1e-6
EPS_LN = 1e-5
LEVELS = (64, 32, 16, 8, 4, 2, 1)
NL = 1 + len(LEVELS)
ATT_D = 64
NEG = -1e30

C_IDENT = 0
C_ONES = C_IDENT + P
C_SEL = C_ONES + P
C_IOTA = C_SEL + 4 * P
C_TRI = C_IOTA + P
C_MISC = C_TRI + P
C_BASE = C_MISC + P
C_SUM = C_BASE
C_REST = C_SUM + 2 * NL * P
C_MASK = C_REST + 2 * P
C_GRID = C_MASK + 2 * NL * P
C_CAUSAL = C_GRID + 2 * 2 * 32
C_INVF = C_CAUSAL + 2 * 2 * 256
C_ALL = C_INVF + 8


def constants():
    c = np.zeros((P, C_ALL), np.float32)
    i = np.arange(P)
    c[:, C_IDENT:C_IDENT + P] = np.eye(P)
    c[:, C_ONES:C_ONES + P] = 1
    for r in range(4):
        c[r, C_SEL + r * P:C_SEL + (r + 1) * P] = 1
    c[:, C_IOTA:C_IOTA + P] = i[None, :]
    c[:, C_TRI:C_TRI + P] = i[:, None] < i[None, :]
    c[:, C_MISC] = -0.5
    c[0, C_MISC + 8:C_MISC + 16] = 2 * np.arange(8)
    c[0, C_MISC + 16:C_MISC + 32] = np.arange(16)
    t, x = i[:, None], i[None, :]
    for d in range(2):
        sums = np.zeros((NL, P, P), np.float32)
        masks = np.zeros((NL, P, P), np.float32)
        sums[0] = (t <= x) if d == 0 else (t >= x)
        for n, h in enumerate(LEVELS):
            mid = x // (2 * h) * (2 * h) + h
            upper = x >= mid
            if d == 0:
                sums[n + 1] = np.where(upper, (t >= mid) & (t <= x), (t > x) & (t < mid))
            else:
                sums[n + 1] = np.where(upper, (t >= mid) & (t < x), (t >= x) & (t < mid))
            same = t // (2 * h) == x // (2 * h)
            late, early = (x, t) if d == 0 else (t, x)
            masks[n] = same & (late % (2 * h) >= h) & (early % (2 * h) < h)
        masks[NL - 1] = np.eye(P)
        c[:, C_SUM + d * NL * P:C_SUM + (d + 1) * NL * P] = sums.transpose(1, 0, 2).reshape(P, -1)
        c[:, C_MASK + d * NL * P:C_MASK + (d + 1) * NL * P] = masks.transpose(1, 0, 2).reshape(P, -1)
        c[:, C_REST + d * P:C_REST + (d + 1) * P] = (t > x) if d == 0 else (t < x)
    grid_w, axis, theta = 64, 32, 10000.0
    inv = theta ** (-np.arange(0, axis, 2, dtype=np.float32) / axis)
    tok = np.arange(2 * P)
    ang = np.concatenate([(tok // grid_w).astype(np.float32)[:, None] * inv,
                          (tok % grid_w).astype(np.float32)[:, None] * inv], axis=-1).astype(np.float32)
    for n, f in enumerate((np.cos(ang), np.sin(ang))):
        c[:, C_GRID + n * 64:C_GRID + (n + 1) * 64] = f.reshape(2, P, 32).transpose(1, 0, 2).reshape(P, 64)
    q, k = np.arange(2 * P)[:, None], np.arange(2 * P)[None, :]
    for n, ok in enumerate((k <= q, (k <= q) & (k > q - P))):
        m = np.where(ok, 0.0, NEG).astype(np.float32)
        c[:, C_CAUSAL + n * 512:C_CAUSAL + (n + 1) * 512] = m.reshape(2, P, 256).transpose(1, 0, 2).reshape(P, 512)
    c[:, C_INVF:C_INVF + 8] = 1.0 / (500000.0 ** (np.arange(0, 16, 2, dtype=np.float32) / 16))
    return c


class Signal:

    def __init__(self, handle, owner):
        self.handle, self.owner, self.base = handle, owner, START

    def at(self, n):
        return self.base + n

    def passed(self, n):
        self.base += n


class Chain:

    def __init__(self, handle):
        self.handle, self.base, self.n, self.extra, self.per = handle, 0, 0, 0, 0

    def link(self, eng, ins):
        self.n += 1
        ins.then_inc(self.handle, 1)
        eng.wait_ge(self.handle, self.base + self.n + self.extra)

    def enter(self, index, per):
        self.base, self.n, self.per = self.base + self.n, 0, per
        self.extra = index * per

    def leave(self, times):
        assert self.n == self.per, (self.n, self.per)
        self.base, self.n, self.extra = self.base + self.per * times, 0, 0


class Ring:

    def __init__(self, loaded, free):
        self.loaded, self.free, self.pos = loaded, free, 0

    def slot(self, j):
        return (self.pos + j) % SLOTS

    def round(self, j):
        return (self.pos + j) // SLOTS


def program(nc, a, out):
    root = ExitStack()
    uses = {}

    def unique(name):
        uses[name] = uses.get(name, 0) + 1
        return name if uses[name] == 1 else f"{name}_{uses[name]}"

    def sb(cx, name, shape, dt=F32):
        return cx.enter_context(nc.sbuf_tensor(unique(name), shape, dt))

    def pb(cx, name, shape, dt=F32):
        return cx.enter_context(nc.psum_tensor(unique(name), shape, dt))

    sem = lambda name: root.enter_context(nc.semaphore(name))
    signals = []

    def signal(name, owner):
        s = Signal(sem(name), owner)
        signals.append(s)
        return s

    ring_loaded = [sem(f"ring_loaded{s}") for s in range(SLOTS)]
    ring_free = [signal(f"ring_free{s}", "tensor") for s in range(SLOTS)]
    ring = Ring(ring_loaded, ring_free)
    loads = {q: [[sem(f"loads_{q}{k}"), 0] for k in range(5)] for q in ("act", "pool")}
    act_chain, dve_chain, pool_chain = Chain(sem("act_chain")), Chain(sem("dve_chain")), Chain(sem("pool_chain"))
    loads_ready = signal("loads_ready", "gpsimd")
    met = {e: [sem(f"met_{e}"), 0] for e in ("tensor", "scalar", "vector", "gpsimd")}

    ring_buf = sb(root, "ring_buf", [P, SLOTS, SLOT])
    X = sb(root, "X", [P, 4, D])
    hT = sb(root, "hT", [P, KD, 4 * P])
    const = sb(root, "const", [P, C_BASE])
    scT = sb(root, "scT", [P, KD, 2])
    mod_gain = sb(root, "mod_gain", [P, 2, KD, 2])
    mod_shift = sb(root, "mod_shift", [P, 2, KD, 2])
    gate_row = sb(root, "gate_row", [2, 2, D])
    ident = const[:, C_IDENT:C_IDENT + P]
    ones = const[:, C_ONES:C_ONES + P]
    sel = lambda r, n: const[0:n, C_SEL + r * P:C_SEL + (r + 1) * P]
    half_power = const[:, C_MISC:C_MISC + 1]

    block = root.enter_context(nc.Block())
    link_a = lambda ins: act_chain.link(nc.scalar, ins)
    link_v = lambda ins: dve_chain.link(nc.vector, ins)
    link_g = lambda ins: pool_chain.link(nc.gpsimd, ins)

    def load(eng, queue, *pairs):
        for n in range(0, len(pairs), 5):
            under_way = list(zip(loads[queue], pairs[n:n + 5]))
            for s, (dst, src) in under_way:
                s[1] += 16
                eng.dma_start(dst, src).then_inc(s[0], 16)
            for s, _ in under_way:
                eng.wait_ge(s[0], s[1])

    waited = {e: sem(f"waited_{e}") for e in ("tensor", "scalar", "gpsimd")}

    def settle(eng):
        eng.sem_inc(waited["tensor" if eng is nc.tensor else "scalar" if eng is nc.scalar else "gpsimd"], 1)

    def meet():
        for e in met:
            met[e][1] += 1

        def body(name):
            def _(eng):
                eng.drain().then_inc(met[name][0], 1)
                for other in met:
                    if other != name:
                        eng.wait_ge(met[other][0], met[other][1])
            return _
        for e in met:
            on_engine[e](body(e))

    on_engine = {"tensor": block.tensor, "scalar": block.scalar, "vector": block.vector,
                     "gpsimd": block.gpsimd}

    def slot_view(j, rows, width):
        return ring_buf[:, ring.slot(j), 0:rows * width].rearrange("p (k n) -> p k n", k=rows)

    def stream(sp, j, src, turn=0):
        rows, width = src.shape[1], src.shape[2]
        sp.wait_ge(ring_free[ring.slot(j)].handle, START + ring.round(j) + turn)
        sp.dma_start(slot_view(j, rows, width), src).then_inc(ring_loaded[ring.slot(j)], 16)

    def await_item(pe, j, turn=0):
        pe.wait_ge(ring_loaded[ring.slot(j)], 16 * (ring.round(j) + 1) + 16 * turn)

    def free_item(j):
        nc.tensor.drain().then_inc(ring_free[ring.slot(j)].handle, 1)

    def by_rows(w):
        return w.rearrange("(k p) n -> p k n", p=P)

    s_start = {n: signal(n, o) for n, o in (
        ("cond_silu", "scalar"), ("cond_psum", "tensor"))}

    def start():
        with ExitStack() as cx:
            cond = sb(cx, "cond", [16, P])
            ps = pb(cx, "ps_cond", [P, 16])
            S = s_start

            def counters(owner):
                def _(eng):
                    for s in signals:
                        if s.owner == owner:
                            eng.sem_inc(s.handle, START)
                return _
            for e in met:
                on_engine[e](counters(e))

            @block.scalar
            def _(act):
                load(act, "act", (const[:, :], a["table"][:, 0:C_BASE]),
                     (cond[0:8, :], a["c"].rearrange("o (k p) -> (o k) p", p=P)),
                     (cond[8:16, :], a["c_ctx"].rearrange("(k p) -> k p", p=P)))
                nc.scalar.activation(cond[:, :], cond[:, :], ACT.Silu).then_inc(S["cond_silu"].handle, 1)

            @block.gpsimd
            def _(pool):
                load(pool, "pool", (X[:, 0:2, :], a["ctx"].rearrange("o (t p) d -> p (o t) d", p=P)),
                     (X[:, 2:4, :], a["x"].rearrange("o (t p) d -> p (o t) d", p=P)))

            @block.tensor
            def _(pe):
                pe.wait_ge(S["cond_silu"].handle, S["cond_silu"].at(1))
                nc.tensor.transpose(ps[:, :], cond[:, :], ident[0:16, 0:16]).then_inc(S["cond_psum"].handle, 1)

            @block.vector
            def _(dve):
                dve.wait_ge(S["cond_psum"].handle, S["cond_psum"].at(1))
                link_v(nc.vector.tensor_copy(scT[:, :, :], ps[:, :].rearrange("p (w k) -> p k w", w=2)))
            for s in S.values():
                s.passed(1)
            meet()

    s_mod = {n: signal(n, o) for n, o in (
        ("mod_psum", "tensor"), ("mod_taken", "vector"), ("mod_rows", "vector"), ("mod_cols", "tensor"),
        ("mod_cols_taken", "vector"))}

    def modulate(layer):
        items = 6
        with ExitStack() as cx:
            rows = sb(cx, "mod_rows_buf", [2, 4, 512])
            bias = sb(cx, "mod_bias", [2, 2, items, 512])
            gains = sb(cx, "mod_gains", [2, 2, 2, D])
            tmp = sb(cx, "mod_tmp", [2, 2, 512])
            ps_row = [pb(cx, f"ps_row{i}", [P, 512]) for i in range(2)]
            ps_col = pb(cx, "ps_col", [P, 4, 4, 2])
            S = s_mod

            @block.sync
            def _(sp):
                with sp.Fori(0, 2) as site:
                    for q in range(items):
                        w = by_rows(a["mod_w"][layer])[:, :, bass.ds(site * (items * 512) + q * 512, 512)]
                        stream(sp, q, w, site * (items // SLOTS))

            @block.tensor
            def _(pe):
                with pe.Fori(0, 2) as site:
                    for q in range(items):
                        n = site * items + q
                        await_item(pe, q, site * (items // SLOTS))
                        pe.wait_ge(S["mod_taken"].handle, S["mod_taken"].at(-1) + n)
                        w = slot_view(q, KD, 512)
                        for k in range(KD):
                            mm = nc.tensor.matmul(ps_row[q % 2][0:2, :], scT[:, k, :], w[:, k, :],
                                                  start=k == 0, stop=k == KD - 1)
                        mm.then_inc(S["mod_psum"].handle, 1)
                        free_item(q)
                    pe.wait_ge(S["mod_rows"].handle, S["mod_rows"].at(1) + site)
                    pe.wait_ge(S["mod_cols_taken"].handle, S["mod_cols_taken"].at(0) + site)
                    settle(pe)
                    for q in range(4):
                        for c in range(4):
                            mm = nc.tensor.transpose(ps_col[:, q, c, :], rows[:, q, c * P:(c + 1) * P],
                                                     ident[0:2, 0:2])
                    mm.then_inc(S["mod_cols"].handle, 1)

            @block.gpsimd
            def _(pool):
                names = (("norm_pre_mix", "norm_post_mix"), ("norm_pre_ffn", "norm_post_ffn"))
                load(pool, "pool", (bias[:, :, :, :].rearrange("w s q n -> w (s q n)"),
                                    a["mod_b"][layer:layer + 1, :].partition_broadcast(2)),
                     *[(gains[:, s, i, :], a[names[s][i]][layer:layer + 1, :].partition_broadcast(2))
                       for s in range(2) for i in range(2)])
                pool.sem_inc(loads_ready.handle, 1)

            @block.vector
            def _(dve):
                dve.wait_ge(loads_ready.handle, loads_ready.at(1))
                per = items + 4
                with dve.Fori(0, 2) as site:
                    dve_chain.enter(site, per)
                    dve.wait_ge(S["mod_cols"].handle, S["mod_cols"].at(0) + site)
                    for q in range(items):
                        n = site * items + q
                        half = (q % 2) * 512
                        b = bias[:, bass.ds(site, 1), q, :].rearrange("w s n -> w (s n)")
                        pre = gains[:, bass.ds(site, 1), 0, half:half + 512].rearrange("w s n -> w (s n)")
                        post = gains[:, bass.ds(site, 1), 1, half:half + 512].rearrange("w s n -> w (s n)")
                        dve.wait_ge(S["mod_psum"].handle, S["mod_psum"].at(1) + n)
                        dst = rows[:, q, :] if q < 2 else tmp[:, q % 2, :]
                        link_v(nc.vector.tensor_tensor(dst, ps_row[q % 2][0:2, :], b, ALU.add))
                        nc.vector.sem_inc(S["mod_taken"].handle, 1)
                        if 2 <= q < 4:
                            link_v(nc.vector.scalar_tensor_tensor(
                                out=rows[:, q, :], in0=tmp[:, q % 2, :], scalar=1.0, in1=pre,
                                op0=ALU.add, op1=ALU.mult))
                        if q == 3:
                            nc.vector.sem_inc(S["mod_rows"].handle, 1)
                        if q >= 4:
                            g = gate_row[:, bass.ds(site, 1), half:half + 512].rearrange("w s n -> w (s n)")
                            link_v(nc.vector.tensor_tensor(g, tmp[:, q % 2, :], post, ALU.mult))
                    dve.wait_ge(S["mod_cols"].handle, S["mod_cols"].at(1) + site)
                    for dst, q in ((mod_shift, 0), (mod_gain, 2)):
                        last = nc.vector.tensor_copy(
                            dst[:, bass.ds(site, 1), :, :].rearrange("p s k w -> p (s k w)"),
                            ps_col[:, q:q + 2, :, :].rearrange("p q c w -> p (q c w)"))
                    last.then_inc(S["mod_cols_taken"].handle, 1)
                dve_chain.leave(2)
            loads_ready.passed(1)
            ring.pos += 2 * items
            S["mod_psum"].passed(12), S["mod_taken"].passed(12)
            for n in ("mod_rows", "mod_cols", "mod_cols_taken"):
                S[n].passed(2)
            normalise(0, ALL_TILES)

    s_norm = {n: signal(n, o) for n, o in (
        ("norm_sums", "scalar"), ("norm_rstd", "gpsimd"), ("norm_scaled", "vector"), ("norm_psum", "tensor"),
        ("norm_out_v", "vector"), ("norm_out_a", "scalar"))}

    def normalise(site, tiles):
        with ExitStack() as cx:
            junk = sb(cx, "norm_junk", [P, D])
            sums = sb(cx, "norm_sums_buf", [P, 4])
            rstd = sb(cx, "norm_rstd_buf", [P, 4])
            xn = sb(cx, "norm_xn", [P, 2, D])
            ps = [pb(cx, f"ps_norm{i}", [P, KD, P]) for i in range(2)]
            S = s_norm
            nt = len(tiles)

            @block.scalar
            def _(act):
                for i, t in enumerate(tiles):
                    nc.scalar.activation(junk[:, :], X[:, t, :], ACT.Square, accum_out=sums[:, i:i + 1])\
                        .then_inc(S["norm_sums"].handle, 1)
                    act.wait_ge(S["norm_sums"].handle, S["norm_sums"].at(i + 1))
                act.wait_ge(s_mod["mod_cols_taken"].handle, s_mod["mod_cols_taken"].at(0))
                for i, t in enumerate(tiles):
                    act.wait_ge(S["norm_psum"].handle, S["norm_psum"].at(i + 1))
                    w = 0 if t in LAT_TILES else 1
                    for k in range(KD // 2):
                        last = nc.scalar.activation(hT[:, k, t * P:(t + 1) * P], ps[i % 2][:, k, :], ACT.Identity,
                                                    bias=mod_shift[:, site, k, w:w + 1],
                                                    scale=mod_gain[:, site, k, w:w + 1])
                    last.then_inc(S["norm_out_a"].handle, 1)

            @block.gpsimd
            def _(pool):
                pool.wait_ge(S["norm_sums"].handle, S["norm_sums"].at(nt))
                link_g(nc.gpsimd.tensor_scalar(rstd[:, 0:nt], sums[:, 0:nt], 1.0 / D, EPS_RMS, ALU.mult, ALU.add))
                nc.gpsimd.tensor_tensor(rstd[:, 0:nt], rstd[:, 0:nt], half_power.to_broadcast([P, nt]), ALU.pow)\
                    .then_inc(S["norm_rstd"].handle, 1)

            @block.vector
            def _(dve):
                dve.wait_ge(S["norm_rstd"].handle, S["norm_rstd"].at(1))
                dve.wait_ge(s_mod["mod_cols_taken"].handle, s_mod["mod_cols_taken"].at(0))
                for i, t in enumerate(tiles):
                    if i >= 2:
                        dve.wait_ge(S["norm_psum"].handle, S["norm_psum"].at(i - 1))
                    nc.vector.tensor_scalar(xn[:, i % 2, :], X[:, t, :], rstd[:, i:i + 1], None, ALU.mult)\
                        .then_inc(S["norm_scaled"].handle, 1)
                    dve.wait_ge(S["norm_psum"].handle, S["norm_psum"].at(i + 1))
                    w = 0 if t in LAT_TILES else 1
                    for k in range(KD // 2, KD):
                        last = nc.vector.tensor_scalar(hT[:, k, t * P:(t + 1) * P], ps[i % 2][:, k, :],
                                                       mod_gain[:, site, k, w:w + 1],
                                                       mod_shift[:, site, k, w:w + 1], ALU.mult, ALU.add)
                    last.then_inc(S["norm_out_v"].handle, 1)

            @block.tensor
            def _(pe):
                for i, t in enumerate(tiles):
                    pe.wait_ge(S["norm_scaled"].handle, S["norm_scaled"].at(i + 1))
                    if i >= 2:
                        pe.wait_ge(S["norm_out_v"].handle, S["norm_out_v"].at(i - 1))
                        pe.wait_ge(S["norm_out_a"].handle, S["norm_out_a"].at(i - 1))
                    for k in range(KD):
                        mm = nc.tensor.transpose(ps[i % 2][:, k, :], xn[:, i % 2, k * P:(k + 1) * P], ident)
                    mm.then_inc(S["norm_psum"].handle, 1)
            for n in S:
                S[n].passed(1 if n == "norm_rstd" else nt)
            meet()

    s_tr = {n: signal(n, o) for n, o in (
        ("turn_psum", "tensor"), ("turn_taken", "scalar"))}

    def turn(src, tiles, parts=KD):
        with ExitStack() as cx:
            ps = [pb(cx, f"ps_turn{i}", [P, KD, P]) for i in range(2)]
            S = s_tr

            @block.tensor
            def _(pe):
                for i, t in enumerate(tiles):
                    pe.wait_ge(S["turn_taken"].handle, S["turn_taken"].at(i - 1))
                    for k in range(parts):
                        mm = nc.tensor.transpose(ps[i % 2][:, k, :], src(t, k), ident)
                    mm.then_inc(S["turn_psum"].handle, 1)

            @block.scalar
            def _(act):
                for i, t in enumerate(tiles):
                    act.wait_ge(S["turn_psum"].handle, S["turn_psum"].at(i + 1))
                    nc.scalar.activation(hT[:, 0:parts, t * P:(t + 1) * P], ps[i % 2][:, 0:parts, :], ACT.Copy)\
                        .then_inc(S["turn_taken"].handle, 1)
            for s in S.values():
                s.passed(len(tiles))
            meet()

    s_lin = {n: signal(n, o) for n, o in (
        ("lin_psum", "tensor"), ("lin_taken_a", "scalar"), ("lin_taken_v", "vector"))}

    def linear(w, tiles, take, cuts, parts=KD, turns=None):
        with ExitStack() as cx:
            ps = [pb(cx, f"ps_lin{i}", [P, 512]) for i in range(4)]
            S = s_lin
            groups = [(j, t, lo + o, min(lo + o + step, hi), o) for j, (lo, hi, step) in enumerate(cuts)
                      for t in tiles for o in range(0, hi - lo, step)]

            @block.sync
            def _(sp):
                for j, (lo, hi, step) in enumerate(cuts):
                    stream(sp, j, by_rows(w)[:, :, lo:hi], turns["sync"] * CHUNKS2 if turns else 0)

            @block.tensor
            def _(pe):
                for n, (j, t, lo, hi, o) in enumerate(groups):
                    if n == 0 or groups[n - 1][0] != j:
                        await_item(pe, j, turns["tensor"] * CHUNKS2 if turns else 0)
                    reader = S["lin_taken_a"] if n % 2 == 0 else S["lin_taken_v"]
                    pe.wait_ge(reader.handle, reader.at(n // 2 - 1))
                    view = slot_view(j, parts, cuts[j][1] - cuts[j][0])
                    for k in range(parts):
                        mm = nc.tensor.matmul(ps[n % 4][:, 0:hi - lo], hT[:, k, t * P:(t + 1) * P],
                                              view[:, k, o:o + hi - lo], start=k == 0, stop=k == parts - 1)
                    mm.then_inc(S["lin_psum"].handle, 1)
                    if n + 1 == len(groups) or groups[n + 1][0] != j:
                        free_item(j)

            @block.scalar
            def _(act):
                for n, (j, t, lo, hi, o) in enumerate(groups):
                    if n % 2 == 0:
                        act.wait_ge(S["lin_psum"].handle, S["lin_psum"].at(n + 1))
                        take(nc.scalar, t, lo, hi, ps[n % 4][:, 0:hi - lo]).then_inc(S["lin_taken_a"].handle, 1)

            @block.vector
            def _(dve):
                for n, (j, t, lo, hi, o) in enumerate(groups):
                    if n % 2 == 1:
                        dve.wait_ge(S["lin_psum"].handle, S["lin_psum"].at(n + 1))
                        take(nc.vector, t, lo, hi, ps[n % 4][:, 0:hi - lo]).then_inc(S["lin_taken_v"].handle, 1)
            S["lin_psum"].passed(len(groups))
            S["lin_taken_a"].passed((len(groups) + 1) // 2)
            S["lin_taken_v"].passed(len(groups) // 2)
            ring.pos += len(cuts)
            meet()

    def copy_on(eng, dst, src):
        return nc.scalar.activation(dst, src, ACT.Copy) if eng is nc.scalar else nc.vector.tensor_copy(dst, src)

    s_post = {n: signal(n, o) for n, o in (
        ("post_sums", "scalar"), ("post_rstd", "gpsimd"), ("post_gate", "tensor"))}

    def add_gated(site, Y, tiles):
        with ExitStack() as cx:
            junk = sb(cx, "post_junk", [P, D])
            sums = sb(cx, "post_sums_buf", [P, 4])
            rstd = sb(cx, "post_rstd_buf", [P, 4])
            term = sb(cx, "post_term", [P, D])
            ps = [pb(cx, f"ps_gate{i}", [P, D]) for i in range(2)]
            S = s_post
            nt = len(tiles)

            @block.tensor
            def _(pe):
                for w in range(2):
                    for h in range(2):
                        mm = nc.tensor.matmul(ps[w][:, h * 512:(h + 1) * 512], sel(w, 2),
                                              gate_row[:, site, h * 512:(h + 1) * 512], start=True, stop=True)
                mm.then_inc(S["post_gate"].handle, 1)

            @block.scalar
            def _(act):
                for i, t in enumerate(tiles):
                    nc.scalar.activation(junk[:, :], Y[:, t, :], ACT.Square, accum_out=sums[:, i:i + 1])\
                        .then_inc(S["post_sums"].handle, 1)
                    act.wait_ge(S["post_sums"].handle, S["post_sums"].at(i + 1))

            @block.gpsimd
            def _(pool):
                pool.wait_ge(S["post_sums"].handle, S["post_sums"].at(nt))
                link_g(nc.gpsimd.tensor_scalar(rstd[:, 0:nt], sums[:, 0:nt], 1.0 / D, EPS_RMS, ALU.mult, ALU.add))
                nc.gpsimd.tensor_tensor(rstd[:, 0:nt], rstd[:, 0:nt], half_power.to_broadcast([P, nt]), ALU.pow)\
                    .then_inc(S["post_rstd"].handle, 1)

            @block.vector
            def _(dve):
                dve.wait_ge(S["post_rstd"].handle, S["post_rstd"].at(1))
                dve.wait_ge(S["post_gate"].handle, S["post_gate"].at(1))
                for i, t in enumerate(tiles):
                    w = 0 if t in LAT_TILES else 1
                    link_v(nc.vector.scalar_tensor_tensor(out=term[:, :], in0=Y[:, t, :], scalar=rstd[:, i:i + 1],
                                                          in1=ps[w][:, :], op0=ALU.mult, op1=ALU.mult))
                    link_v(nc.vector.tensor_tensor(X[:, t, :], X[:, t, :], term[:, :], ALU.add))
            S["post_sums"].passed(nt), S["post_rstd"].passed(1), S["post_gate"].passed(1)
            meet()

    s_ffn = {n: signal(n, o) for n, o in (
        ("ffn_gate", "tensor"), ("ffn_up", "tensor"), ("ffn_silu", "scalar"), ("ffn_hidden", "vector"),
        ("ffn_turned", "tensor"), ("ffn_turned_taken", "scalar"), ("ffn_down", "tensor"), ("ffn_added", "vector"))}

    class Hidden:

        def __init__(self, cx, width):
            self.width, self.half = width, width // 2
            self.parts = [(o, min(P, width - o)) for o in range(0, width, P)]
            self.silu = sb(cx, "ffn_silu_buf", [P, width])
            self.hid = sb(cx, "ffn_hidden_buf", [P, width])
            self.hidT = sb(cx, "ffn_hiddenT", [P, len(self.parts), P])
            self.ps_g = pb(cx, "ps_ffn_gate", [P, 2, 512])
            self.ps_u = pb(cx, "ps_ffn_up", [P, 2, 512])
            self.ps_t = pb(cx, "ps_ffn_turn", [P, 8, P])
            self.ps_y = pb(cx, "ps_ffn_down", [P, 2, 512])

    def ffn_steps(H, act_tile, Y, add):
        S, hw = s_ffn, H.half

        def used(eng, item):
            if item is not None:
                eng.sem_inc(ring_free[ring.slot(item)].handle, 1)

        def product(pe, ps, n, view, t, taken, ready):
            pe.wait_ge(taken.handle, taken.at(0) + n)
            for h in range(2):
                for k in range(KD):
                    mm = nc.tensor.matmul(ps[:, h, 0:hw], act_tile(k, t), view[:, k, h * hw:(h + 1) * hw],
                                          start=k == 0, stop=k == KD - 1)
            mm.then_inc(ready.handle, 1)

        def pe_gate(pe, n, view, t):
            product(pe, H.ps_g, n, view, t, S["ffn_silu"], S["ffn_gate"])

        def pe_up(pe, n, view, t):
            product(pe, H.ps_u, n, view, t, S["ffn_hidden"], S["ffn_up"])

        def pe_turn(pe, n):
            pe.wait_ge(S["ffn_hidden"].handle, S["ffn_hidden"].at(1) + n)
            pe.wait_ge(S["ffn_turned_taken"].handle, S["ffn_turned_taken"].at(0) + n)
            settle(pe)
            for i, (o, m) in enumerate(H.parts):
                mm = nc.tensor.transpose(H.ps_t[0:m, i, :], H.hid[:, o:o + m], ident)
            mm.then_inc(S["ffn_turned"].handle, 1)

        def pe_down(pe, n, view):
            pe.wait_ge(S["ffn_turned_taken"].handle, S["ffn_turned_taken"].at(1) + n)
            pe.wait_ge(S["ffn_added"].handle, S["ffn_added"].at(0) + n)
            for h in range(2):
                for i, (o, m) in enumerate(H.parts):
                    mm = nc.tensor.matmul(H.ps_y[:, h, :], H.hidT[0:m, i, :], view[0:m, i, h * 512:(h + 1) * 512],
                                          start=i == 0, stop=i == len(H.parts) - 1)
            mm.then_inc(S["ffn_down"].handle, 1)

        def act_silu(act, n, freed=None):
            act.wait_ge(S["ffn_gate"].handle, S["ffn_gate"].at(1) + n)
            used(nc.scalar, freed)
            act.wait_ge(S["ffn_hidden"].handle, S["ffn_hidden"].at(0) + n)
            nc.scalar.activation(H.silu[:, :].rearrange("p (h n) -> p h n", h=2), H.ps_g[:, :, 0:hw], ACT.Silu)\
                .then_inc(S["ffn_silu"].handle, 1)

        def act_turned(act, n):
            act.wait_ge(S["ffn_turned"].handle, S["ffn_turned"].at(1) + n)
            act.wait_ge(S["ffn_down"].handle, S["ffn_down"].at(0) + n)
            full = H.width // P
            last = nc.scalar.activation(H.hidT[:, 0:full, :], H.ps_t[:, 0:full, :], ACT.Copy)
            if H.width % P:
                m = H.width % P
                last = nc.scalar.activation(H.hidT[0:m, full, :], H.ps_t[0:m, full, :], ACT.Copy)
            last.then_inc(S["ffn_turned_taken"].handle, 1)

        def dve_hidden(dve, n, freed=None):
            dve.wait_ge(S["ffn_silu"].handle, S["ffn_silu"].at(1) + n)
            dve.wait_ge(S["ffn_up"].handle, S["ffn_up"].at(1) + n)
            used(nc.vector, freed)
            dve.wait_ge(S["ffn_turned"].handle, S["ffn_turned"].at(0) + n)
            nc.vector.tensor_tensor(H.hid[:, :].rearrange("p (h n) -> p h n", h=2),
                                    H.silu[:, :].rearrange("p (h n) -> p h n", h=2), H.ps_u[:, :, 0:hw],
                                    ALU.mult).then_inc(S["ffn_hidden"].handle, 1)

        def dve_add(dve, n, t, freed=None):
            dve.wait_ge(S["ffn_down"].handle, S["ffn_down"].at(1) + n)
            used(nc.vector, freed)
            dve.wait_ge(S["ffn_added"].handle, S["ffn_added"].at(0) + n)
            add(Y[:, t, :], H.ps_y[:, :, :].rearrange("p h n -> p (h n)")).then_inc(S["ffn_added"].handle, 1)

        return pe_gate, pe_up, pe_turn, pe_down, act_silu, act_turned, dve_hidden, dve_add

    def down_view(j, width):
        return ring_buf[:, ring.slot(j), 0:(width + P - 1) // P * D].rearrange("p (k n) -> p k n", n=D)

    def stream_down(sp, j, w, row, width, turn=0):
        full, rest = width // P, width % P
        view = down_view(j, width)
        sp.wait_ge(ring_free[ring.slot(j)].handle, START + ring.round(j) + turn)
        h = ring_loaded[ring.slot(j)]
        if rest:
            sp.dma_start(view[0:rest, full, :], w[bass.ds(row + full * P, rest), :]).then_inc(down_rest, 16)
        sp.dma_start(view[:, 0:full, :], w[bass.ds(row, full * P), :].rearrange("(k p) n -> p k n", p=P))\
            .then_inc(h, 16)

    down_rest = sem("down_rest_loaded")
    down_rest_count = [0]

    def feed_forward(w_gate, w_up, w_down, width, tiles, Y):
        hidden = w_gate.shape[1]
        chunks, nt = hidden // width, len(tiles)
        assert chunks * width == hidden
        rest = width % P != 0
        with ExitStack() as cx:
            H = Hidden(cx, width)
            S = s_ffn
            add = lambda y, ps: nc.vector.tensor_tensor(y, y, ps, ALU.add)
            pe_gate, pe_up, pe_turn, pe_down, act_silu, act_turned, dve_hidden, dve_add = ffn_steps(
                H, lambda k, t: hT[:, k, t * P:(t + 1) * P], Y, add)
            view_g, view_u, view_d = slot_view(0, KD, width), slot_view(1, KD, width), down_view(2, width)
            rests = down_rest_count[0]

            @block.sync
            def _(sp):
                with sp.Fori(0, chunks) as c:
                    stream(sp, 0, by_rows(w_gate)[:, :, bass.ds(c * width, width)], c)
                    stream(sp, 1, by_rows(w_up)[:, :, bass.ds(c * width, width)], c)
                    stream_down(sp, 2, w_down, c * width, width, c)

            @block.vector
            def _(dve):
                link_v(nc.vector.memset(Y[:, tiles[0]:tiles[-1] + 1, :], 0.0))
                dve_hidden(dve, 0)

                def chunk(c, last):
                    for i, t in enumerate(tiles):
                        n = c * nt + i
                        if not (last and i == nt - 1):
                            dve_hidden(dve, n + 1)
                        dve_add(dve, n, t)
                with dve.Fori(0, chunks - 1) as c:
                    chunk(c, False)
                chunk(chunks - 1, True)

            @block.scalar
            def _(act):
                act_silu(act, 0)

                def chunk(c, last):
                    for i in range(nt):
                        n = c * nt + i
                        if not (last and i == nt - 1):
                            act_silu(act, n + 1)
                        act_turned(act, n)
                with act.Fori(0, chunks - 1) as c:
                    chunk(c, False)
                chunk(chunks - 1, True)

            @block.tensor
            def _(pe):
                await_item(pe, 0)
                pe_gate(pe, 0, view_g, tiles[0])
                await_item(pe, 1)
                pe_up(pe, 0, view_u, tiles[0])

                def chunk(c, last):
                    for i in range(nt):
                        n = c * nt + i
                        wrap = i == nt - 1
                        nxt = tiles[(i + 1) % nt]
                        go = not (last and wrap)
                        if go:
                            if wrap:
                                await_item(pe, 0, c + 1)
                            pe_gate(pe, n + 1, view_g, nxt)
                        if i == nt - 2:
                            free_item(0)
                        pe_turn(pe, n)
                        if go:
                            if wrap:
                                await_item(pe, 1, c + 1)
                            pe_up(pe, n + 1, view_u, nxt)
                        if i == nt - 2:
                            free_item(1)
                        if i == 0:
                            await_item(pe, 2, c)
                            if rest:
                                pe.wait_ge(down_rest, 16 * (rests + 1) + 16 * c)
                        pe_down(pe, n, view_d)
                    free_item(2)
                with pe.Fori(0, chunks - 1) as c:
                    chunk(c, False)
                chunk(chunks - 1, True)
            for s in S.values():
                s.passed(chunks * nt)
            if rest:
                down_rest_count[0] += chunks
            ring.pos += 3 * chunks
            meet()

    s_rec = {n: signal(n, o) for n, o in (
        ("rec_staged", "scalar"), ("rec_head_done", "vector"), ("rec_qk_psum", "tensor"), ("rec_qk_ready", "scalar"),
        ("rec_sums", "tensor"), ("rec_decays", "scalar"), ("rec_q", "vector"), ("rec_k", "gpsimd"),
        ("rec_scores", "tensor"), ("rec_masked", "vector"), ("rec_out", "tensor"), ("rec_state", "vector"),
        ("rec_rms", "gpsimd"), ("rec_squares", "vector"))}

    class Recurrence:

        def __init__(self, cx, width, scale, room=None):
            self.width, self.scale = width, scale
            K = width
            self.sums = sb(cx, "rec_sum_table", [P, 2, NL, P])
            self.rest = sb(cx, "rec_rest_table", [P, 2, P])
            self.mask = sb(cx, "rec_mask_table", [P, 2, NL, P])
            self.decay = ring_buf[0:K, ring.slot(0), KD * 512:KD * 512 + 2 * NL * P]\
                .rearrange("k (b l n) -> k b l n", b=2, l=NL)
            self.rest_decay = sb(cx, "rec_rest_decay", [P, 2, K])
            self.total = sb(cx, "rec_total", [K, 2])
            if room is None:
                room = sb(cx, "rec_room", [P, 2 * (2 * NL - 1) * P])
            nq, nk = 2 * NL * P, 2 * (NL - 1) * P
            self.qd = room[0:K, 0:nq].rearrange("k (b l n) -> k b l n", b=2, l=NL)
            self.kd = room[0:K, nq:nq + nk].rearrange("k (b l n) -> k b l n", b=2, l=NL - 1)
            self.k_end = sb(cx, "rec_k_end", [P, 2, K])
            self.masked = sb(cx, "rec_masked_buf", [P, NL, P])
            self.state = sb(cx, "rec_state_buf", [K, 2, P])
            self.ps_sums = pb(cx, "ps_rec_sums", [P, NL, P])
            self.ps_scores = pb(cx, "ps_rec_scores", [P, NL, P])
            self.ps_out = [pb(cx, f"ps_rec_out{i}", [P, 512]) for i in range(2)]
            self.ps_state = pb(cx, "ps_rec_state", [P, 512])
            self.ps_rest = pb(cx, "ps_rec_rest", [P, 512])

        def tables(self):
            return ((self.sums[:, :, :, :].rearrange("p d l n -> p (d l n)"), a["table"][:, C_SUM:C_REST]),
                    (self.rest[:, :, :].rearrange("p d n -> p (d n)"), a["table"][:, C_REST:C_MASK]),
                    (self.mask[:, :, :, :].rearrange("p d l n -> p (d l n)"), a["table"][:, C_MASK:C_GRID]))

    def recurrence(R, units, first, last, operands, o_acc):
        S, K = s_rec, R.width

        def pe_sums(pe, u, i):
            d, t = units[i]
            g = operands(d, t)[0]
            pe.wait_ge(S["rec_decays"].handle, S["rec_decays"].at(0) + u)
            for h in range(2):
                nc.tensor.matmul(R.ps_sums[0:K, h * 4:h * 4 + 4, :], g, R.sums[:, d, h * 4:h * 4 + 4, :],
                                 start=True, stop=True)
            nc.tensor.matmul(R.ps_rest[:, 0:K], R.rest[:, d, :], g, start=True, stop=True)\
                .then_inc(S["rec_sums"].handle, 1)

        def pe_scores(pe, u, i):
            d, t = units[i]
            _, _, _, qT, kT = operands(d, t)
            pe.wait_ge(S["rec_q"].handle, S["rec_q"].at(1) + u)
            pe.wait_ge(S["rec_k"].handle, S["rec_k"].at(1) + u)
            pe.wait_ge(S["rec_masked"].handle, S["rec_masked"].at(0) + u)
            for l in range(NL - 1):
                nc.tensor.matmul(R.ps_scores[:, l, :], R.kd[:, i % 2, l, :], R.qd[:, i % 2, l + 1, :],
                                 start=True, stop=True)
            nc.tensor.matmul(R.ps_scores[:, NL - 1, :], kT, qT, start=True, stop=True)\
                .then_inc(S["rec_scores"].handle, 1)

        def pe_out(pe, u, i):
            d, t = units[i]
            _, _, v, _, _ = operands(d, t)
            pe.wait_ge(S["rec_masked"].handle, S["rec_masked"].at(1) + u)
            pe.wait_ge(S["rec_state"].handle, S["rec_state"].at(-1) + u)
            if i not in first:
                nc.tensor.matmul(R.ps_out[i % 2][:, 0:P], R.qd[:, i % 2, 0, :], R.state[:, d, :], start=True, stop=False)
            for l in range(NL):
                mm = nc.tensor.matmul(R.ps_out[i % 2][:, 0:P], R.masked[:, l, :], v,
                                      start=l == 0 and i in first, stop=l == NL - 1)
            if i not in last:
                pe.wait_ge(S["rec_state"].handle, S["rec_state"].at(0) + u)
                mm = nc.tensor.matmul(R.ps_state[0:K, 0:P], R.k_end[:, i % 2, :], v, start=True, stop=True)
            mm.then_inc(S["rec_out"].handle, 1)

        def act_decays(act, u, i):
            act.wait_ge(S["rec_sums"].handle, S["rec_sums"].at(1) + u)
            act.wait_ge(S["rec_q"].handle, S["rec_q"].at(-1) + u)
            act.wait_ge(S["rec_k"].handle, S["rec_k"].at(-1) + u)
            nc.scalar.activation(R.decay[:, i % 2, :, :], R.ps_sums[0:K, :, :], ACT.Exp, scale=R.scale)
            nc.scalar.activation(R.rest_decay[:, i % 2, :], R.ps_rest[:, 0:K], ACT.Exp, scale=R.scale)\
                .then_inc(S["rec_decays"].handle, 1)

        def dve_q(dve, u, i):
            d, t = units[i]
            _, k, _, qT, _ = operands(d, t)
            dve.wait_ge(S["rec_decays"].handle, S["rec_decays"].at(1) + u)
            dve.wait_ge(S["rec_out"].handle, S["rec_out"].at(-1) + u)
            dve.wait_ge(S["rec_state"].handle, S["rec_state"].at(-1) + u)
            end = P - 1 if d == 0 else 0
            nc.vector.tensor_copy(R.total[:, i % 2:i % 2 + 1], R.decay[:, i % 2, 0, end:end + 1])
            nc.vector.tensor_tensor(R.k_end[:, i % 2, :], k, R.rest_decay[:, i % 2, :], ALU.mult)
            nc.vector.tensor_tensor(R.qd[:, i % 2, :, :], R.decay[:, i % 2, :, :],
                                    qT.unsqueeze(1).to_broadcast([K, NL, P]), ALU.mult)\
                .then_inc(S["rec_q"].handle, 1)

        def pool_k(pool, u, i):
            d, t = units[i]
            kT = operands(d, t)[4]
            pool.wait_ge(S["rec_decays"].handle, S["rec_decays"].at(1) + u)
            pool.wait_ge(S["rec_scores"].handle, S["rec_scores"].at(-1) + u)
            nc.gpsimd.tensor_tensor(R.kd[:, i % 2, :, :], R.decay[:, i % 2, 1:NL, :],
                                    kT.unsqueeze(1).to_broadcast([K, NL - 1, P]), ALU.mult)\
                .then_inc(S["rec_k"].handle, 1)

        def dve_mask(dve, u, i):
            d, t = units[i]
            dve.wait_ge(S["rec_scores"].handle, S["rec_scores"].at(1) + u)
            dve.wait_ge(S["rec_out"].handle, S["rec_out"].at(0) + u)
            nc.vector.tensor_tensor(R.masked[:, :, :], R.ps_scores[:, :, :], R.mask[:, d, :, :], ALU.mult)\
                .then_inc(S["rec_masked"].handle, 1)

        def dve_state(dve, u, i):
            d, t = units[i]
            dve.wait_ge(S["rec_out"].handle, S["rec_out"].at(1) + u)
            if t not in [other for _, other in units[:i]]:
                nc.vector.tensor_copy(o_acc(t), R.ps_out[i % 2][:, 0:P])
            else:
                nc.vector.tensor_tensor(o_acc(t), o_acc(t), R.ps_out[i % 2][:, 0:P], ALU.add)
            if i in last:
                nc.vector.engine_nop().then_inc(S["rec_state"].handle, 1)
            elif i in first:
                nc.vector.tensor_copy(R.state[:, d, :], R.ps_state[0:K, 0:P]).then_inc(S["rec_state"].handle, 1)
            else:
                nc.vector.scalar_tensor_tensor(out=R.state[:, d, :], in0=R.state[:, d, :], scalar=R.total[:, i % 2:i % 2 + 1],
                                               in1=R.ps_state[0:K, 0:P], op0=ALU.mult, op1=ALU.add)\
                    .then_inc(S["rec_state"].handle, 1)

        n = len(units)

        def tensor(pe, u, after_first=lambda: None, before_scores=lambda: None):
            pe_sums(pe, u, 0)
            after_first()
            pe_sums(pe, u + 1, 1)
            before_scores()
            for i in range(n):
                pe_scores(pe, u + i, i)
                if i + 2 < n:
                    pe_sums(pe, u + i + 2, i + 2)
                pe_out(pe, u + i, i)

        def scalar(act, u):
            for i in range(n):
                act_decays(act, u + i, i)

        def gpsimd(pool, u):
            for i in range(n):
                pool_k(pool, u + i, i)

        def vector(dve, u):
            dve_q(dve, u, 0)
            for i in range(n):
                dve_mask(dve, u + i, i)
                if i + 1 < n:
                    dve_q(dve, u + i + 1, i + 1)
                dve_state(dve, u + i, i)
        return tensor, scalar, gpsimd, vector

    REC_PER_UNIT = ("rec_sums", "rec_decays", "rec_q", "rec_k", "rec_scores", "rec_masked", "rec_out", "rec_state")

    GH, GK, GV, RANK = 4, 64, 128, 16
    O_Q, O_K, O_V, O_G, O_Z = 0, 256, 512, 1024, 1536
    O_AQ, O_AK, O_AV, O_END = 1568, 2080, 2208, 2336
    s_gate = {n: signal(n, o) for n, o in (
        ("z_psum", "tensor"), ("z_ready", "scalar"), ("logit_psum", "tensor"), ("logit_low", "vector"),
        ("logit_log", "scalar"))}

    def gla_gates(A, g, meanwhile):
        with ExitStack() as cx:
            w = sb(cx, "gla_w", [RANK, 2, GH * GK])
            b = sb(cx, "gla_b", [1, 2, GH * GK])
            zT = hT[0:RANK, 6:8, :].rearrange("r k n -> r (k n)").rearrange("r (t d n) -> r t d n", t=4, d=2)
            low = sb(cx, "gla_low", [P, 4, 512])
            mag = sb(cx, "gla_mag", [P, 4, 512])
            ps_z = [pb(cx, f"ps_z{i}", [P, 4, P]) for i in range(2)]
            ps_l = [pb(cx, f"ps_logit{i}", [P, 512]) for i in range(4)]
            S = s_gate

            @block.gpsimd
            def _(pool):
                load(pool, "pool", (w[:, :, :], a["gla_w_gate"][0].rearrange("d r n -> r d n")),
                     (b[:, :, :], a["gla_b_gate"][0:1]))
                pool.sem_inc(loads_ready.handle, 1)

            @block.tensor
            def _(pe):
                for d in range(2):
                    for t in range(4):
                        mm = nc.tensor.transpose(ps_z[d][0:RANK, t, :],
                                                 A[:, t, O_Z + d * RANK:O_Z + (d + 1) * RANK], ident)
                mm.then_inc(S["z_psum"].handle, 1)
                pe.wait_ge(S["z_ready"].handle, S["z_ready"].at(1))
                pe.wait_ge(loads_ready.handle, loads_ready.at(1))
                for t in range(4):
                    for d in range(2):
                        dst = ps_l[t][:, d * 256:(d + 1) * 256]
                        nc.tensor.matmul(dst, zT[:, t, d, :], w[:, d, :], start=True, stop=False)
                        mm = nc.tensor.matmul(dst, ones[0:1, :], b[:, d, :], start=False, stop=True)
                    mm.then_inc(S["logit_psum"].handle, 1)

            @block.scalar
            def _(act):
                act.wait_ge(S["z_psum"].handle, S["z_psum"].at(1))
                for d in range(2):
                    last = nc.scalar.activation(zT[:, :, d, :], ps_z[d][0:RANK, :, :], ACT.Copy)
                last.then_inc(S["z_ready"].handle, 1)
                nc.scalar.preload_act_table_set("natural_log_exp_and_others")
                for t in range(4):
                    act.wait_ge(S["logit_low"].handle, S["logit_low"].at(t + 1))
                    link_a(nc.scalar.activation(mag[:, t, :], ps_l[t][:, :], ACT.Abs))
                    link_a(nc.scalar.activation(mag[:, t, :], mag[:, t, :], ACT.Exp, scale=-1.0))
                    nc.scalar.activation(mag[:, t, :], mag[:, t, :], ACT.Ln, bias=1.0)\
                        .then_inc(S["logit_log"].handle, 1)

            @block.vector
            def _(dve):
                for t in range(4):
                    dve.wait_ge(S["logit_psum"].handle, S["logit_psum"].at(t + 1))
                    nc.vector.tensor_scalar(low[:, t, :], ps_l[t][:, :], 0.0, None, ALU.min)\
                        .then_inc(S["logit_low"].handle, 1)
            loads_ready.passed(1)
            meanwhile()

            @block.vector
            def _(dve):
                for t in range(4):
                    dve.wait_ge(S["logit_log"].handle, S["logit_log"].at(t + 1))
                    link_v(nc.vector.tensor_tensor(g[:, t, :, :].rearrange("p d n -> p (d n)"), low[:, t, :],
                                                   mag[:, t, :], ALU.subtract))
            S["z_psum"].passed(1), S["z_ready"].passed(1)
            for k in ("logit_psum", "logit_low", "logit_log"):
                S[k].passed(4)
            meet()

    def gla_heads(A, g):
        with ExitStack() as cx:
            R = Recurrence(cx, GK, 1.0 / 16.0, hT[:, :, :].rearrange("p k n -> p (k n)"))
            qs = hT[:, KD - 1, 256:512].rearrange("p (t n) -> p t n", t=4)
            vs = A[:, :, O_AK:O_AV]
            o = A[:, :, O_AV:O_END]
            ks = sb(cx, "gla_k", [P, 4, GK])
            gs = sb(cx, "gla_g", [P, 4, 2, GK])
            qT = sb(cx, "gla_qT", [GK, 4, P])
            kT = sb(cx, "gla_kT", [GK, 4, P])
            sq = R.masked[:, 0:4, :]
            rstd = sb(cx, "gla_rstd", [P, 4])
            gain = sb(cx, "gla_gain", [P, GV])
            S = s_rec
            units = [(0, 0), (1, 1), (0, 1), (1, 0), (0, 2), (1, 3), (0, 3), (1, 2)]
            tensor, scalar, gpsimd, vector = recurrence(
                R, units, first=(0, 1), last=(6, 7),
                operands=lambda d, t: (gs[:, t, d, :], ks[:, t, :], vs[:, t, :], qT[:, t, :], kT[:, t, :]),
                o_acc=lambda t: o[:, t, :])
            n = len(units)

            @block.gpsimd
            def _(pool):
                load(pool, "pool", *R.tables(), (gain[:, :], a["gla_out_norm"][0:1, :].partition_broadcast(P)))
                pool.sem_inc(loads_ready.handle, 1)
                with pool.Fori(0, GH) as h:
                    pool_chain.enter(h, 1)
                    gpsimd(pool, h * n)
                    pool.wait_ge(S["rec_squares"].handle, S["rec_squares"].at(1) + h)
                    settle(pool)
                    link_g(nc.gpsimd.tensor_scalar(rstd[:, :], rstd[:, :], 1.0 / GV, EPS_RMS, ALU.mult, ALU.add))
                    nc.gpsimd.tensor_tensor(rstd[:, :], rstd[:, :], half_power.to_broadcast([P, 4]), ALU.pow)\
                        .then_inc(S["rec_rms"].handle, 1)
                pool_chain.leave(GH)

            @block.tensor
            def _(pe):
                pe.wait_ge(loads_ready.handle, loads_ready.at(1))
                with pe.Fori(0, GH) as h:
                    pe.wait_ge(S["rec_staged"].handle, S["rec_staged"].at(1) + h)
                    pe.wait_ge(S["rec_decays"].handle, S["rec_decays"].at(0) + h * n)
                    settle(pe)
                    for t in range(4):
                        nc.tensor.transpose(R.ps_sums[0:GK, t, :], qs[:, t, :], ident)
                    for t in range(4):
                        mm = nc.tensor.transpose(R.ps_sums[0:GK, 4 + t, :], ks[:, t, :], ident)
                    mm.then_inc(S["rec_qk_psum"].handle, 1)
                    pe.wait_ge(S["rec_qk_ready"].handle, S["rec_qk_ready"].at(1) + h)
                    tensor(pe, h * n)

            @block.scalar
            def _(act):
                with act.Fori(0, GH) as h:
                    act.wait_ge(S["rec_out"].handle, S["rec_out"].at(0) + h * n)
                    settle(nc.scalar)
                    nc.scalar.activation(qs, A[:, :, bass.ds(h * GK + O_Q, GK)], ACT.Copy)
                    nc.scalar.activation(ks[:, :, :], A[:, :, bass.ds(h * GK + O_K, GK)], ACT.Copy)
                    for t in range(4):
                        nc.scalar.activation(gs[:, t, :, :], g[:, t, :, bass.ds(h * GK, GK)], ACT.Copy)
                    nc.scalar.activation(vs, A[:, :, bass.ds(h * GV + O_V, GV)], ACT.Copy)\
                        .then_inc(S["rec_staged"].handle, 1)
                    act.wait_ge(S["rec_qk_psum"].handle, S["rec_qk_psum"].at(1) + h)
                    nc.scalar.activation(qT[:, :, :], R.ps_sums[0:GK, 0:4, :], ACT.Copy, scale=GK ** -0.5)
                    nc.scalar.activation(kT[:, :, :], R.ps_sums[0:GK, 4:8, :], ACT.Copy)\
                        .then_inc(S["rec_qk_ready"].handle, 1)
                    scalar(act, h * n)

            @block.vector
            def _(dve):
                dve.wait_ge(loads_ready.handle, loads_ready.at(1))
                with dve.Fori(0, GH) as h:
                    dve_chain.enter(h, 5)
                    vector(dve, h * n)
                    dve.wait_ge(S["rec_state"].handle, S["rec_state"].at(n) + h * n)
                    link_v(nc.vector.tensor_tensor(sq, o, o, ALU.mult))
                    link_v(nc.vector.tensor_reduce(rstd[:, :], sq[:, :, :], AX.X, ALU.add))
                    nc.vector.sem_inc(S["rec_squares"].handle, 1)
                    link_v(nc.vector.tensor_tensor(o[:, :, :], o[:, :, :], gain[:, :].unsqueeze(1).to_broadcast([P, 4, GV]),
                                                   ALU.mult))
                    dve.wait_ge(S["rec_rms"].handle, S["rec_rms"].at(1) + h)
                    link_v(nc.vector.tensor_tensor(o[:, :, :], o[:, :, :],
                                                   rstd[:, :].unsqueeze(2).to_broadcast([P, 4, GV]), ALU.mult))
                    og = A[:, :, bass.ds(h * GV + O_G, GV)]
                    link_v(nc.vector.tensor_tensor(og, o[:, :, :], og, ALU.mult))
                    nc.vector.sem_inc(S["rec_head_done"].handle, 1)
                dve_chain.leave(GH)
            for k in REC_PER_UNIT:
                S[k].passed(GH * n)
            for k in ("rec_staged", "rec_head_done", "rec_qk_psum", "rec_qk_ready", "rec_rms", "rec_squares"):
                S[k].passed(GH)
            loads_ready.passed(1)
            meet()

    s_att = {n: signal(n, o) for n, o in (
        ("att_kT_psum", "tensor"), ("att_kT_ready", "scalar"),
        ("att_staged", "gpsimd"), ("att_q_psum", "tensor"), ("att_q_ready_a", "scalar"), ("att_q_ready_v", "vector"),
        ("att_scores", "tensor"), ("att_max", "vector"), ("att_probs", "scalar"), ("att_turned", "tensor"),
        ("att_probs_T", "scalar"), ("att_out", "tensor"), ("att_taken", "vector"))}

    def attend(A, q_col, k_col, v_col, kv_heads, q_tiles, heads, mask=None, sinks=None, scale=1.0):
        group, E = 4, ATT_D
        tiles = [t for t, _ in q_tiles]
        t0, nt = tiles[0], len(tiles)
        nkt = max(k for _, ks in q_tiles for k in ks) + 1 - t0
        wide = nkt * P
        assert heads * wide == 1024
        turned_q, turned_p = hT[:, 0:4, :], hT[:, 4:8, :]
        qT = turned_q[0:E]
        flat_p = turned_p.rearrange("p k n -> p (k n)").rearrange("p (b n) -> p b n", b=2)
        probsT = flat_p.rearrange("p b (h t n) -> p b h t n", h=heads, t=nkt)
        with ExitStack() as cx:
            qs = sb(cx, "att_qs", [P, nt, group * E])
            kT = sb(cx, "att_kT", [E, kv_heads, nkt * P])
            probs = sb(cx, "att_probs_buf", [P, 2, heads, wide])
            masked = sb(cx, "att_masked", [P, 2, heads, wide]) if mask is not None else None
            stat = sb(cx, "att_stat", [P, 4, 4, heads])
            ps_s = [pb(cx, f"ps_att_s{i}", [P, heads, wide]) for i in range(2)]
            ps_t = pb(cx, "ps_att_t", [P, heads, nkt, P])
            ps_o = [pb(cx, f"ps_att_o{i}", [P, 512]) for i in range(2)]
            S = s_att
            ps_q = [p[0:E, :, :].rearrange("p h n -> p (h n)").rearrange("p (b n) -> p b n", b=2) for p in ps_s]
            units = [(qi, g) for qi in range(nt) for g in range(0, group, heads)]
            n = len(units)
            assert n % 2 == 0
            keys_of = lambda i: q_tiles[units[i][0]][1]

            @block.gpsimd
            def _(pool):
                with pool.Fori(0, kv_heads) as kv:
                    pool.wait_ge(S["att_q_psum"].handle, S["att_q_psum"].at(0) + kv)
                    nc.gpsimd.tensor_copy(qs[:, :, :], A[:, t0:t0 + nt, bass.ds(kv * (group * E) + q_col, group * E)])\
                        .then_inc(S["att_staged"].handle, 1)

            @block.tensor
            def _(pe):
                for kv in range(kv_heads):
                    if kv >= 2:
                        pe.wait_ge(S["att_kT_ready"].handle, S["att_kT_ready"].at(kv - 1))
                    for i in range(nkt):
                        mm = nc.tensor.transpose(ps_q[kv % 2][:, 0, i * P:(i + 1) * P],
                                                 A[:, t0 + i, k_col + kv * E:k_col + (kv + 1) * E], ident)
                    mm.then_inc(S["att_kT_psum"].handle, 1)
                pe.wait_ge(S["att_kT_ready"].handle, S["att_kT_ready"].at(kv_heads))

                def scores(u, kv, i):
                    qi, g = units[i]
                    nk = len(keys_of(i)) * P
                    pe.wait_ge(S["att_probs"].handle, S["att_probs"].at(-1) + u)
                    settle(pe)
                    for h in range(heads):
                        mm = nc.tensor.matmul(ps_s[i % 2][:, h, 0:nk], qT[:, g + h, qi * P:(qi + 1) * P],
                                              kT[:, bass.ds(kv, 1), 0:nk].rearrange("k h n -> k (h n)"),
                                              start=True, stop=True)
                    mm.then_inc(S["att_scores"].handle, 1)

                def turned(u, i):
                    pe.wait_ge(S["att_probs"].handle, S["att_probs"].at(1) + u)
                    pe.wait_ge(S["att_probs_T"].handle, S["att_probs_T"].at(0) + u)
                    for h in range(heads):
                        for k in range(len(keys_of(i))):
                            mm = nc.tensor.transpose(ps_t[:, h, k, :], probs[:, i % 2, h, k * P:(k + 1) * P], ident)
                    mm.then_inc(S["att_turned"].handle, 1)

                def output(u, kv, i):
                    keys = keys_of(i)
                    pe.wait_ge(S["att_probs_T"].handle, S["att_probs_T"].at(1) + u)
                    pe.wait_ge(S["att_taken"].handle, S["att_taken"].at(-1) + u)
                    for h in range(heads):
                        for k, t in enumerate(keys):
                            mm = nc.tensor.matmul(ps_o[i % 2][:, h * E:(h + 1) * E], probsT[:, i % 2, h, k, :],
                                                  A[:, t0 + k, bass.ds(kv * E + v_col, E)],
                                                  start=k == 0, stop=k == len(keys) - 1)
                    mm.then_inc(S["att_out"].handle, 1)

                with pe.Fori(0, kv_heads) as kv:
                    pe.wait_ge(S["att_staged"].handle, S["att_staged"].at(1) + kv)
                    pe.wait_ge(S["att_probs"].handle, S["att_probs"].at(0) + kv * n)
                    settle(pe)
                    for g in range(group):
                        for i in range(nt):
                            mm = nc.tensor.transpose(ps_q[g // 2][:, g % 2, i * P:(i + 1) * P],
                                                     qs[:, i, g * E:(g + 1) * E], ident)
                    mm.then_inc(S["att_q_psum"].handle, 1)
                    pe.wait_ge(S["att_q_ready_a"].handle, S["att_q_ready_a"].at(1) + kv)
                    pe.wait_ge(S["att_q_ready_v"].handle, S["att_q_ready_v"].at(1) + kv)
                    for i in range(n + 2):
                        if i < n:
                            scores(kv * n + i, kv, i)
                        if 1 <= i <= n:
                            turned(kv * n + i - 1, i - 1)
                        if i >= 2:
                            output(kv * n + i - 2, kv, i - 2)

            @block.scalar
            def _(act):
                for kv in range(kv_heads):
                    act.wait_ge(S["att_kT_psum"].handle, S["att_kT_psum"].at(kv + 1))
                    nc.scalar.activation(kT[:, kv, :], ps_q[kv % 2][:, 0, 0:nkt * P], ACT.Copy)\
                        .then_inc(S["att_kT_ready"].handle, 1)

                def softmax(u, i):
                    nk = len(keys_of(i)) * P
                    act.wait_ge(S["att_max"].handle, S["att_max"].at(1) + u)
                    act.wait_ge(S["att_turned"].handle, S["att_turned"].at(-1) + u)
                    src = ps_s[i % 2] if mask is None else masked[:, i % 2, :, :]
                    if sinks is not None:
                        nc.scalar.activation(stat[:, i % 4, 3, :], stat[:, i % 4, 3, :], ACT.Exp)
                    for h in range(heads):
                        last = nc.scalar.activation(probs[:, i % 2, h, 0:nk], src[:, h, 0:nk], ACT.Exp,
                                                    bias=stat[:, i % 4, 0, h:h + 1],
                                                    accum_out=stat[:, i % 4, 1, h:h + 1])
                    last.then_inc(S["att_probs"].handle, 1)

                def take_turned(u, i):
                    nk = len(keys_of(i))
                    act.wait_ge(S["att_turned"].handle, S["att_turned"].at(1) + u)
                    act.wait_ge(S["att_out"].handle, S["att_out"].at(-1) + u)
                    nc.scalar.activation(probsT[:, i % 2, :, 0:nk, :], ps_t[:, :, 0:nk, :], ACT.Copy)\
                        .then_inc(S["att_probs_T"].handle, 1)

                with act.Fori(0, kv_heads) as kv:
                    act.wait_ge(S["att_q_psum"].handle, S["att_q_psum"].at(1) + kv)
                    nc.scalar.activation(qT[:, 0:2, 0:nt * P], ps_q[0][:, :, 0:nt * P], ACT.Copy, scale=scale)\
                        .then_inc(S["att_q_ready_a"].handle, 1)
                    for i in range(n + 1):
                        if i >= 1:
                            take_turned(kv * n + i - 1, i - 1)
                        if i < n:
                            softmax(kv * n + i, i)

            @block.vector
            def _(dve):
                links = n * (1 + (mask is not None) + 4 * (sinks is not None))

                def maxima(u, kv, i):
                    qi, g = units[i]
                    nk = len(keys_of(i)) * P
                    dve.wait_ge(S["att_scores"].handle, S["att_scores"].at(1) + u)
                    src = ps_s[i % 2][:, :, 0:nk]
                    top = stat[:, i % 4, 0, :]
                    if mask is not None:
                        link_v(nc.vector.tensor_tensor(masked[:, i % 2, :, 0:nk], src,
                                                       mask[:, qi, 0:nk].unsqueeze(1).to_broadcast([P, heads, nk]),
                                                       ALU.add))
                        src = masked[:, i % 2, :, 0:nk]
                    if sinks is None:
                        nc.vector.tensor_reduce(top, src, AX.X, ALU.max, negate=True)\
                            .then_inc(S["att_max"].handle, 1)
                    else:
                        own = sinks[:, bass.ds(kv * group + g, heads)]
                        link_v(nc.vector.tensor_reduce(top, src, AX.X, ALU.max))
                        link_v(nc.vector.tensor_tensor(top, top, own, ALU.max))
                        link_v(nc.vector.tensor_scalar(top, top, -1.0, None, ALU.mult))
                        nc.vector.tensor_tensor(stat[:, i % 4, 3, :], top, own, ALU.add)\
                            .then_inc(S["att_max"].handle, 1)

                def divide(u, kv, i):
                    qi, g = units[i]
                    total, inverse = stat[:, i % 4, 1, :], stat[:, i % 4, 2, :]
                    dve.wait_ge(S["att_out"].handle, S["att_out"].at(1) + u)
                    if sinks is not None:
                        link_v(nc.vector.tensor_tensor(total, total, stat[:, i % 4, 3, :], ALU.add))
                    link_v(nc.vector.reciprocal(inverse, total))
                    dst = A[:, t0 + qi, bass.ds(kv * (group * E) + (q_col + g * E), heads * E)]
                    nc.vector.tensor_tensor(dst.rearrange("p (h e) -> p h e", e=E),
                                            ps_o[i % 2][:, 0:heads * E].rearrange("p (h e) -> p h e", e=E),
                                            inverse.unsqueeze(2).to_broadcast([P, heads, E]), ALU.mult)\
                        .then_inc(S["att_taken"].handle, 1)

                with dve.Fori(0, kv_heads) as kv:
                    dve_chain.enter(kv, links)
                    dve.wait_ge(S["att_q_psum"].handle, S["att_q_psum"].at(1) + kv)
                    nc.vector.tensor_scalar(qT[:, 2:4, 0:nt * P], ps_q[1][:, :, 0:nt * P], scale, None, ALU.mult)\
                        .then_inc(S["att_q_ready_v"].handle, 1)
                    for i in range(n + 2):
                        if i < n:
                            maxima(kv * n + i, kv, i)
                        if i >= 2:
                            divide(kv * n + i - 2, kv, i - 2)
                dve_chain.leave(kv_heads)
            for k in ("att_scores", "att_max", "att_probs", "att_turned", "att_probs_T", "att_out", "att_taken"):
                S[k].passed(kv_heads * n)
            for k in ("att_kT_psum", "att_kT_ready", "att_staged", "att_q_psum", "att_q_ready_a", "att_q_ready_v"):
                S[k].passed(kv_heads)
            meet()


    s_qk = {n: signal(n, o) for n, o in (("qk_squares", "vector"), ("qk_rstd", "gpsimd"))}

    def even_queries_keys(A):
        heads = (O_AV - O_AQ) // ATT_D
        with ExitStack() as cx:
            sq = hT[:, 0:5, :].rearrange("p k n -> p (k n)").rearrange("p (t n) -> p t n", t=4)
            rstd = sb(cx, "qk_rstd_buf", [P, 4, heads])
            gain = sb(cx, "qk_gain", [P, 2, ATT_D])
            grid = sb(cx, "qk_grid", [P, 2, 2, 32])
            S = s_qk

            @block.gpsimd
            def _(pool):
                load(pool, "pool", (grid[:, :, :, :].rearrange("p f t n -> p (f t n)"), a["table"][:, C_GRID:C_CAUSAL]),
                     (gain[:, 0, :], a["att_q_norm"][0:1, :].partition_broadcast(P)),
                     (gain[:, 1, :], a["att_k_norm"][0:1, :].partition_broadcast(P)))
                pool.sem_inc(loads_ready.handle, 1)
                pool.wait_ge(S["qk_squares"].handle, S["qk_squares"].at(1))
                link_g(nc.gpsimd.tensor_scalar(rstd[:, :, :], rstd[:, :, :], 1.0 / ATT_D, EPS_RMS, ALU.mult, ALU.add))
                r = rstd[:, :, :].rearrange("p t h -> p (t h)")
                nc.gpsimd.tensor_tensor(r, r, half_power.to_broadcast([P, 4 * heads]), ALU.pow)\
                    .then_inc(S["qk_rstd"].handle, 1)

            @block.vector
            def _(dve):
                qk = A[:, :, O_AQ:O_AV]
                by_head = qk.rearrange("p t (h e) -> p t h e", e=ATT_D)
                link_v(nc.vector.tensor_tensor(sq[:, :, :], qk, qk, ALU.mult))
                link_v(nc.vector.tensor_reduce(rstd[:, :, :], sq[:, :, :].rearrange("p t (h e) -> p t h e", e=ATT_D),
                                               AX.X, ALU.add))
                nc.vector.sem_inc(S["qk_squares"].handle, 1)
                dve.wait_ge(loads_ready.handle, loads_ready.at(1))
                link_v(nc.vector.tensor_scalar(gain[:, 0, :], gain[:, 0, :], ATT_D ** -0.5, None, ALU.mult))
                dve.wait_ge(S["qk_rstd"].handle, S["qk_rstd"].at(1))
                for t in range(4):
                    link_v(nc.vector.tensor_tensor(by_head[:, t], by_head[:, t],
                                                   rstd[:, t, :].unsqueeze(2).to_broadcast([P, heads, ATT_D]), ALU.mult))
                    for which, lo, hi in ((0, 0, 8), (1, 8, heads)):
                        last = nc.vector.tensor_tensor(
                            by_head[:, t, lo:hi], by_head[:, t, lo:hi],
                            gain[:, which, :].unsqueeze(1).to_broadcast([P, hi - lo, ATT_D]), ALU.mult)
                    link_v(last)
                for i, t in enumerate(LAT_TILES):
                    pair = by_head[:, t].rearrange("p h (e two) -> p two h e", two=2)
                    x0, x1 = pair[:, 0], pair[:, 1]
                    cos = grid[:, 0, i, :].unsqueeze(1).to_broadcast([P, heads, 32])
                    sin = grid[:, 1, i, :].unsqueeze(1).to_broadcast([P, heads, 32])
                    part = [sq[:, j, 0:heads * 32].rearrange("p (h e) -> p h e", e=32) for j in range(4)]
                    nc.vector.tensor_tensor(part[0], x0, cos, ALU.mult)
                    nc.vector.tensor_tensor(part[1], x1, sin, ALU.mult)
                    nc.vector.tensor_tensor(part[2], x0, sin, ALU.mult)
                    link_v(nc.vector.tensor_tensor(part[3], x1, cos, ALU.mult))
                    nc.vector.tensor_tensor(x0, part[0], part[1], ALU.subtract)
                    link_v(nc.vector.tensor_tensor(x1, part[2], part[3], ALU.add))
            S["qk_squares"].passed(1), S["qk_rstd"].passed(1), loads_ready.passed(1)

    def first_layer_even(A, g):
        linear(a["even_w_in"][0], ALL_TILES, lambda e, t, lo, hi, ps: copy_on(e, A[:, t, lo:hi], ps),
               [(0, 896, 448), (896, 1792, 448), (1792, O_END, 272)])
        silu_columns(A, O_G, O_Z)
        gla_gates(A, g, lambda: even_queries_keys(A))
        attend(A, O_AQ, O_AK, O_AV, 2, [(0, (0, 1)), (1, (0, 1)), (2, (0, 1, 2, 3)), (3, (0, 1, 2, 3))], 2)
        gla_heads(A, g)
        turn(lambda t, k: A[:, t, O_G + k * P:O_G + (k + 1) * P] if k < 4 else
             A[:, t, O_AQ + (k - 4) * P:O_AQ + (k - 3) * P], ALL_TILES)

    s_silu = signal("silu_done", "scalar")

    def silu_columns(A, lo, hi):
        @block.scalar
        def _(act):
            nc.scalar.activation(A[:, :, lo:hi], A[:, :, lo:hi], ACT.Silu).then_inc(s_silu.handle, 1)
            act.wait_ge(s_silu.handle, s_silu.at(1))
        s_silu.passed(1)
        meet()

    def finish(tiles):
        done = sem("out_written")

        @block.sync
        def _(sp):
            sp.wait_ge(met["tensor"][0], met["tensor"][1])
            sp.wait_ge(met["scalar"][0], met["scalar"][1])
            sp.wait_ge(met["vector"][0], met["vector"][1])
            sp.wait_ge(met["gpsimd"][0], met["gpsimd"][1])
            sp.dma_start(out.rearrange("o (t p) d -> p (o t) d", p=P), X[:, tiles[0]:tiles[-1] + 1, :])\
                .then_inc(done, 16)
            sp.wait_ge(done, 16)
        root.close()


    HH = 8
    odd_second = [sem(f"odd_second{j}") for j in range(2)]
    c_sig = {n: signal(n, o) for n, o in (
        ("ctx_sums", "tensor"), ("ctx_decay", "scalar"), ("ctx_k_end", "vector"), ("ctx_out", "tensor"),
        ("ctx_state", "vector"))}
    s_odd = {n: signal(n, o) for n, o in (
        ("bound_exp", "scalar"), ("bound_ready", "vector"),
        ("hg_lb_psum", "tensor"), ("hg_psum", "tensor"), ("hg_taken", "scalar"),
        ("hg_forget", "vector"), ("hg_log", "scalar"), ("hg_k", "vector"))}

    def odd_mixer(O):
        w = by_rows(a["odd_w_in"][0])
        col = lambda which, h: w[:, :, bass.ds(h * P + which * D, P)]
        Q, FF, FB, I, OG = range(5)
        with ExitStack() as cx:
            R = Recurrence(cx, P, 1.0)
            lb = sb(cx, "hg_lb", [2, D])
            lb1 = sb(cx, "hg_lb1", [2, D])
            lbb = sb(cx, "hg_lbb", [P, 2, 2, P])
            qs = sb(cx, "hg_q", [P, 2, P])
            og = sb(cx, "hg_og", [P, 2, P])
            vs = sb(cx, "hg_v", [P, 4, P])
            tanh = sb(cx, "hg_tanh", [P, 4, 2, P])
            ks = sb(cx, "hg_k_buf", [P, 4, 2, P])
            gs = sb(cx, "hg_g", [P, 4, 2, P])
            qT = sb(cx, "hg_qT", [P, 2, P])
            kT = sb(cx, "hg_kT", [P, 2, 2, P])
            o = sb(cx, "hg_o", [P, 2, P])
            rstd = sb(cx, "hg_rstd", [P, 2])
            gain = sb(cx, "hg_gain", [P, P])
            ctx_k = sb(cx, "hg_ctx_k", [P, 4, P])
            sq = R.masked[:, 0:2, :]
            S, Z = s_rec, s_odd
            seq_tensor, seq_scalar, seq_gpsimd, seq_vector = recurrence(
                R, [(0, 2), (1, 3), (0, 3), (1, 2)], first=(), last=(2, 3),
                operands=lambda d, t: (gs[:, t, d, :], ks[:, t, d, :], vs[:, t, :], qT[:, t - 2, :], kT[:, d, t - 2, :]),
                o_acc=lambda t: o[:, t - 2, :])
            C = c_sig

            @block.sync
            def _(sp):
                with sp.Fori(0, HH) as h:
                    for j, parts in enumerate(((FF, FB), (I, Q), (OG,))):
                        sp.wait_ge(ring_free[ring.slot(j)].handle, START + ring.round(j) + h)
                        view = slot_view(j, KD, 256)
                        for i, which in enumerate(parts):
                            landed = ring_loaded[ring.slot(j)] if i == 0 else odd_second[j]
                            sp.dma_start(view[:, :, i * P:(i + 1) * P], col(which, h)).then_inc(landed, 16)

            @block.gpsimd
            def _(pool):
                load(pool, "pool", (lb[:, :], a["hgrn_lower_bounds"][:, 0, :]),
                     (lb1[:, :], a["hgrn_lower_bounds"][:, 1, :]))
                pool.sem_inc(loads_ready.handle, 1)
                load(pool, "pool", *R.tables(), (gain[:, :], a["hgrn_out_norm"][0:1, :].partition_broadcast(P)))
                pool.sem_inc(loads_ready.handle, 1)
                with pool.Fori(0, HH) as h:
                    pool_chain.enter(h, 1)
                    seq_gpsimd(pool, h * 4)
                    pool.wait_ge(S["rec_squares"].handle, S["rec_squares"].at(1) + h)
                    settle(pool)
                    link_g(nc.gpsimd.tensor_scalar(rstd[:, :], rstd[:, :], 1.0 / P, EPS_RMS, ALU.mult, ALU.add))
                    nc.gpsimd.tensor_tensor(rstd[:, :], rstd[:, :], half_power.to_broadcast([P, 2]), ALU.pow)\
                        .then_inc(S["rec_rms"].handle, 1)
                pool_chain.leave(HH)

            def lower_bounds_vector(dve):
                top, b0, b1, inv = (R.masked[0:2, :, :].rearrange("p l n -> p (l n)"), lb[:, :], lb1[:, :],
                                    R.qd[0:2, 0, :, :].rearrange("p l n -> p (l n)"))
                dve.wait_ge(loads_ready.handle, loads_ready.at(1))
                link_v(nc.vector.tensor_tensor(top, b0, b1, ALU.max))
                link_v(nc.vector.tensor_tensor(b0, b0, top, ALU.subtract))
                link_v(nc.vector.tensor_tensor(b1, b1, top, ALU.subtract))
                nc.vector.sem_inc(Z["bound_ready"].handle, 1)
                dve.wait_ge(Z["bound_exp"].handle, Z["bound_exp"].at(1))
                link_v(nc.vector.tensor_tensor(top, b0, b1, ALU.add))
                link_v(nc.vector.reciprocal(inv, top))
                link_v(nc.vector.tensor_tensor(top, b1, inv, ALU.mult))
                link_v(nc.vector.tensor_tensor(b1, b0, inv, ALU.mult))
                link_v(nc.vector.tensor_copy(b0, top))
                nc.vector.sem_inc(Z["bound_ready"].handle, 1)

            def groups():
                for t in range(4):
                    yield t, "f"
                    yield t, "iq"
                    if t >= 2:
                        yield t, "og"
            GR = list(groups())
            NG = len(GR)

            @block.tensor
            def _(pe):
                with pe.Fori(0, HH) as h:
                    pe.wait_ge(S["rec_masked"].handle, S["rec_masked"].at(0) + h * 4)
                    pe.wait_ge(S["rec_decays"].handle, S["rec_decays"].at(0) + h * 4)
                    for j in range(3):
                        await_item(pe, j, h)
                        if j < 2:
                            pe.wait_ge(odd_second[j], 16 + 16 * h)
                    banks = [R.ps_scores[:, 0:4, :], R.ps_scores[:, 4:8, :], R.ps_sums[:, 0:4, :], R.ps_sums[:, 4:8, :]]
                    for n, (t, kind) in enumerate(GR):
                        if n == 4:
                            pe.wait_ge(Z["bound_ready"].handle, Z["bound_ready"].at(2))
                            for x, src in enumerate((lb, lb1)):
                                for d in range(2):
                                    mm = nc.tensor.matmul(R.ps_rest[:, (2 * x + d) * P:(2 * x + d + 1) * P],
                                                          sel(d, 2), src[:, bass.ds(h * P, P)], start=True, stop=True)
                            mm.then_inc(Z["hg_lb_psum"].handle, 1)
                        pe.wait_ge(Z["hg_taken"].handle, Z["hg_taken"].at(n - 3) + h * NG)
                        view = slot_view({"f": 0, "iq": 1, "og": 2}[kind], KD, 256)
                        width = {"f": 256, "iq": 256 if t >= 2 else P, "og": P}[kind]
                        dst = banks[n % 4].rearrange("p l n -> p (l n)")[:, 0:width]
                        for k in range(KD):
                            mm = nc.tensor.matmul(dst, hT[:, k, t * P:(t + 1) * P], view[:, k, 0:width],
                                                  start=k == 0, stop=k == KD - 1)
                        mm.then_inc(Z["hg_psum"].handle, 1)
                    for j in range(3):
                        free_item(j)
                    pe.wait_ge(Z["hg_k"].handle, Z["hg_k"].at(1) + h)
                    pe.wait_ge(Z["hg_taken"].handle, Z["hg_taken"].at(NG) + h * NG)
                    for t in range(2):
                        nc.tensor.transpose(R.ps_sums[:, t, :], qs[:, t, :], ident)
                    for d in range(2):
                        for t in range(2):
                            mm = nc.tensor.transpose(R.ps_sums[:, 4 + 2 * d + t, :], ks[:, 2 + t, d, :], ident)
                    mm.then_inc(S["rec_qk_psum"].handle, 1)
                    pe.wait_ge(Z["hg_log"].handle, Z["hg_log"].at(1) + h)
                    pe.wait_ge(loads_ready.handle, loads_ready.at(2))
                    for t in range(2):
                        for d in range(2):
                            dst = R.ps_out[1][:, (2 * t + d) * P:(2 * t + d + 1) * P]
                            early = t == d
                            mm = nc.tensor.matmul(dst, R.rest[:, d, :], gs[:, t, d, :], start=True, stop=not early)
                            if early:
                                mm = nc.tensor.matmul(dst, ones, gs[:, 1 - t, d, :], start=False, stop=True)
                    mm.then_inc(C["ctx_sums"].handle, 1)
                    pe.wait_ge(S["rec_qk_ready"].handle, S["rec_qk_ready"].at(1) + h)

                    def context_state():
                        pe.wait_ge(C["ctx_k_end"].handle, C["ctx_k_end"].at(1) + h)
                        for d in range(2):
                            for t in range(2):
                                mm = nc.tensor.matmul(R.ps_state[:, d * P:(d + 1) * P], ctx_k[:, 2 * t + d, :],
                                                      vs[:, t, :], start=t == 0, stop=t == 1)
                        mm.then_inc(C["ctx_out"].handle, 1)

                    def state_ready():
                        pe.wait_ge(C["ctx_state"].handle, C["ctx_state"].at(1) + h)
                    seq_tensor(pe, h * 4, context_state, state_ready)

            @block.scalar
            def _(act):
                nc.scalar.preload_act_table_set("natural_log_exp_and_others")
                act.wait_ge(Z["bound_ready"].handle, Z["bound_ready"].at(1))
                nc.scalar.activation(lb[:, :], lb[:, :], ACT.Exp)
                nc.scalar.activation(lb1[:, :], lb1[:, :], ACT.Exp).then_inc(Z["bound_exp"].handle, 1)
                with act.Fori(0, HH) as h:
                    banks = [R.ps_scores[:, 0:4, :], R.ps_scores[:, 4:8, :], R.ps_sums[:, 0:4, :], R.ps_sums[:, 4:8, :]]
                    nc.scalar.preload_act_table_set("silu_and_others")
                    act.wait_ge(S["rec_head_done"].handle, S["rec_head_done"].at(0) + h)
                    for n, (t, kind) in enumerate(GR):
                        act.wait_ge(Z["hg_psum"].handle, Z["hg_psum"].at(n + 1) + h * NG)
                        src = banks[n % 4].rearrange("p l n -> p (l n)")
                        if kind == "f":
                            last = nc.scalar.activation(tanh[:, t, :, :].rearrange("p d n -> p (d n)"), src[:, 0:256],
                                                        ACT.Tanh, scale=0.5)
                        elif kind == "iq":
                            last = nc.scalar.activation(vs[:, t, :], src[:, 0:P], ACT.Copy)
                            if t >= 2:
                                last = nc.scalar.activation(qs[:, t - 2, :], src[:, P:256], ACT.Silu)
                        else:
                            last = nc.scalar.activation(og[:, t - 2, :], src[:, 0:P], ACT.Silu)
                        last.then_inc(Z["hg_taken"].handle, 1)
                    nc.scalar.preload_act_table_set("natural_log_exp_and_others")
                    act.wait_ge(Z["hg_forget"].handle, Z["hg_forget"].at(1) + h)
                    nc.scalar.activation(gs[:, :, :, :], gs[:, :, :, :], ACT.Ln).then_inc(Z["hg_log"].handle, 1)
                    act.wait_ge(S["rec_qk_psum"].handle, S["rec_qk_psum"].at(1) + h)
                    nc.scalar.activation(qT[:, :, :], R.ps_sums[:, 0:2, :], ACT.Copy)
                    nc.scalar.activation(kT[:, :, :, :].rearrange("p d t n -> p (d t) n"), R.ps_sums[:, 4:8, :], ACT.Copy)\
                        .then_inc(S["rec_qk_ready"].handle, 1)
                    act.wait_ge(C["ctx_sums"].handle, C["ctx_sums"].at(1) + h)
                    act.wait_ge(C["ctx_out"].handle, C["ctx_out"].at(0) + h)
                    nc.scalar.activation(ctx_k[:, :, :].rearrange("p t n -> p (t n)"), R.ps_out[1][:, :], ACT.Exp)\
                        .then_inc(C["ctx_decay"].handle, 1)
                    seq_scalar(act, h * 4)

            @block.vector
            def _(dve):
                lower_bounds_vector(dve)
                dve.wait_ge(loads_ready.handle, loads_ready.at(2))
                with dve.Fori(0, HH) as h:
                    dve_chain.enter(h, 27)
                    dve.wait_ge(Z["hg_lb_psum"].handle, Z["hg_lb_psum"].at(1) + h)
                    link_v(nc.vector.tensor_copy(lbb[:, :, :, :].rearrange("p x d n -> p (x d n)"), R.ps_rest[:, :]))
                    for t in range(4):
                        dve.wait_ge(Z["hg_taken"].handle, Z["hg_taken"].at(GR.index((t, "f")) + 1) + h * NG)
                        link_v(nc.vector.tensor_scalar(ks[:, t, :, :], tanh[:, t, :, :], -0.5, 0.5, ALU.mult, ALU.add))
                        link_v(nc.vector.tensor_tensor(ks[:, t, :, :], ks[:, t, :, :], lbb[:, 1, :, :], ALU.mult))
                        link_v(nc.vector.tensor_scalar(gs[:, t, :, :], tanh[:, t, :, :], 0.5, 0.5, ALU.mult, ALU.add))
                        link_v(nc.vector.tensor_tensor(gs[:, t, :, :], gs[:, t, :, :], lbb[:, 1, :, :], ALU.mult))
                        link_v(nc.vector.tensor_tensor(gs[:, t, :, :], gs[:, t, :, :], lbb[:, 0, :, :], ALU.add))
                    nc.vector.sem_inc(Z["hg_k"].handle, 1)
                    link_v(nc.vector.tensor_scalar(gs[:, :, :, :].rearrange("p t d n -> p (t d n)"),
                                                   gs[:, :, :, :].rearrange("p t d n -> p (t d n)"), 1e-18, None, ALU.max))
                    nc.vector.sem_inc(Z["hg_forget"].handle, 1)
                    dve.wait_ge(C["ctx_decay"].handle, C["ctx_decay"].at(1) + h)
                    nc.vector.tensor_tensor(ctx_k[:, :, :], ctx_k[:, :, :],
                                            ks[:, 0:2, :, :].rearrange("p t d n -> p (t d) n"), ALU.mult)\
                        .then_inc(C["ctx_k_end"].handle, 1)
                    dve.wait_ge(C["ctx_out"].handle, C["ctx_out"].at(1) + h)
                    nc.vector.tensor_copy(R.state[:, :, :].rearrange("p d n -> p (d n)"), R.ps_state[:, 0:2 * P])\
                        .then_inc(C["ctx_state"].handle, 1)
                    seq_vector(dve, h * 4)
                    dve.wait_ge(S["rec_state"].handle, S["rec_state"].at(4) + h * 4)
                    link_v(nc.vector.tensor_tensor(sq, o[:, :, :], o[:, :, :], ALU.mult))
                    link_v(nc.vector.tensor_reduce(rstd[:, :], sq, AX.X, ALU.add))
                    nc.vector.sem_inc(S["rec_squares"].handle, 1)
                    link_v(nc.vector.tensor_tensor(o[:, :, :], o[:, :, :], gain[:, :].unsqueeze(1).to_broadcast([P, 2, P]),
                                                   ALU.mult))
                    link_v(nc.vector.tensor_tensor(o[:, :, :], o[:, :, :], og[:, :, :], ALU.mult))
                    dve.wait_ge(S["rec_rms"].handle, S["rec_rms"].at(1) + h)
                    link_v(nc.vector.tensor_tensor(O[:, :, bass.ds(h * P, P)], o[:, :, :],
                                                   rstd[:, :].unsqueeze(2).to_broadcast([P, 2, P]), ALU.mult))
                    nc.vector.sem_inc(S["rec_head_done"].handle, 1)
                dve_chain.leave(HH)
            for k in REC_PER_UNIT:
                S[k].passed(HH * 4)
            for k in c_sig:
                c_sig[k].passed(HH)
            for k in ("rec_head_done", "rec_qk_psum", "rec_qk_ready", "rec_rms", "rec_squares"):
                S[k].passed(HH)
            for k in ("hg_psum", "hg_taken"):
                Z[k].passed(HH * NG)
            for k in ("hg_lb_psum", "hg_forget", "hg_log", "hg_k"):
                Z[k].passed(HH)
            Z["bound_exp"].passed(1), Z["bound_ready"].passed(2), loads_ready.passed(2)
            ring.pos += 3 * HH
            meet()

    ALPHA = (2.0 * 2) ** 0.25
    ROT = 8
    QKV, K2, V2 = 1536, 1024, 1280
    HID2, WIDTH2 = 3584, 896
    EXPERTS = 8
    TWO_PI = 2 * np.pi
    PI_HI = 6.28125
    PI_MID = float(np.float32(np.round((TWO_PI - PI_HI) * 2 ** 20) / 2 ** 20))
    PI_LO = float(TWO_PI - PI_HI - PI_MID)
    ROUND = 1.5 * 2 ** 23
    s_rot = {n: signal(n, o) for n, o in (("rot_angle", "vector"),)}

    def rotation_table(rot):
        with ExitStack() as cx:
            pos = sb(cx, "rot_pos", [P, 2], I32)
            posf = sb(cx, "rot_posf", [P, 2])
            freq = sb(cx, "rot_freq", [P, ROT])
            turns = sb(cx, "rot_turns", [P, 2, ROT])
            S = s_rot

            @block.gpsimd
            def _(pool):
                with nc.allow_non_contiguous_dma("one position a partition"):
                    load(pool, "pool", (pos[:, :], a["positions_2"].rearrange("o (t p) -> p (o t)", p=P)),
                         (freq[:, :], a["table"][:, C_INVF:C_ALL]))
                pool.sem_inc(loads_ready.handle, 1)

            @block.vector
            def _(dve):
                dve.wait_ge(loads_ready.handle, loads_ready.at(1))
                link_v(nc.vector.tensor_copy(posf[:, :], pos[:, :]))
                cos, sin = rot[:, 0, :, :], rot[:, 1, :, :]
                for t in range(2):
                    last = nc.vector.tensor_scalar(sin[:, t, :], freq[:, :], posf[:, t:t + 1], None, ALU.mult)
                link_v(last)
                link_v(nc.vector.tensor_scalar(turns[:, :, :], sin, 1.0 / TWO_PI, None, ALU.mult))
                link_v(nc.vector.tensor_scalar(turns[:, :, :], turns[:, :, :], ROUND, None, ALU.add))
                link_v(nc.vector.tensor_scalar(turns[:, :, :], turns[:, :, :], ROUND, None, ALU.subtract))
                for part in (PI_HI, PI_MID, PI_LO):
                    link_v(nc.vector.scalar_tensor_tensor(out=sin, in0=turns[:, :, :], scalar=-part, in1=sin,
                                                          op0=ALU.mult, op1=ALU.add))
                link_v(nc.vector.tensor_scalar(cos, sin, np.pi / 2, None, ALU.add))
                link_v(nc.vector.tensor_scalar(turns[:, :, :], cos, np.pi, -TWO_PI, ALU.is_gt, ALU.mult))
                link_v(nc.vector.tensor_tensor(cos, cos, turns[:, :, :], ALU.add))
                limit = 3.1415925
                link_v(nc.vector.tensor_scalar(rot[:, :, :, :], rot[:, :, :, :], limit, -limit, ALU.min, ALU.max))
                nc.vector.sem_inc(S["rot_angle"].handle, 1)

            @block.scalar
            def _(act):
                act.wait_ge(S["rot_angle"].handle, S["rot_angle"].at(1))
                nc.scalar.activation(rot[:, :, :, :], rot[:, :, :, :], ACT.Sin)
            S["rot_angle"].passed(1), loads_ready.passed(1)
            meet()

    def rotate_partly(B, rot):
        heads = V2 // ATT_D
        with ExitStack() as cx:
            part = sb(cx, "rot_parts", [P, 4, heads, ROT])

            @block.vector
            def _(dve):
                for t in range(2):
                    x = B[:, t, 0:V2].rearrange("p (h e) -> p h e", e=ATT_D)
                    x1, x2 = x[:, :, 0:ROT], x[:, :, ROT:2 * ROT]
                    cos = rot[:, 0, t, :].unsqueeze(1).to_broadcast([P, heads, ROT])
                    sin = rot[:, 1, t, :].unsqueeze(1).to_broadcast([P, heads, ROT])
                    nc.vector.tensor_tensor(part[:, 0], x1, cos, ALU.mult)
                    nc.vector.tensor_tensor(part[:, 1], x2, sin, ALU.mult)
                    nc.vector.tensor_tensor(part[:, 2], x2, cos, ALU.mult)
                    link_v(nc.vector.tensor_tensor(part[:, 3], x1, sin, ALU.mult))
                    nc.vector.tensor_tensor(x1, part[:, 0], part[:, 1], ALU.subtract)
                    link_v(nc.vector.tensor_tensor(x2, part[:, 2], part[:, 3], ALU.add))
            meet()

    s_ln = {n: signal(n, o) for n, o in (("ln_var", "vector"), ("ln_rstd", "gpsimd"))}

    def layer_norm(Y, gain_row, shift_row):
        with ExitStack() as cx:
            gain = sb(cx, "ln_gain", [P, D])
            shift = sb(cx, "ln_shift", [P, D])
            stats = sb(cx, "ln_stats", [P, 2, 2, 6])
            mv = sb(cx, "ln_mv", [P, 2, 2])
            S = s_ln

            @block.gpsimd
            def _(pool):
                load(pool, "pool", (gain[:, :], gain_row.partition_broadcast(P)),
                     (shift[:, :], shift_row.partition_broadcast(P)))
                pool.sem_inc(loads_ready.handle, 1)
                pool.wait_ge(S["ln_var"].handle, S["ln_var"].at(1))
                var = mv[:, :, 1]
                link_g(nc.gpsimd.tensor_scalar(var, var, 1.0, EPS_LN, ALU.mult, ALU.add))
                nc.gpsimd.tensor_tensor(var, var, half_power.to_broadcast([P, 2]), ALU.pow)\
                    .then_inc(S["ln_rstd"].handle, 1)

            @block.vector
            def _(dve):
                for i, t in enumerate(LAT_TILES):
                    link_v(nc.vector.scalar_tensor_tensor(out=X[:, t, :], in0=X[:, t, :], scalar=ALPHA, in1=Y[:, t, :],
                                                          op0=ALU.mult, op1=ALU.add))
                    for h in range(2):
                        last = nc.vector.bn_stats(stats[:, i, h, :], X[:, t, h * 512:(h + 1) * 512])
                    link_v(last)
                    link_v(nc.vector.bn_aggr(mv[:, i, :], stats[:, i, :, :]))
                nc.vector.sem_inc(S["ln_var"].handle, 1)
                dve.wait_ge(loads_ready.handle, loads_ready.at(1))
                dve.wait_ge(S["ln_rstd"].handle, S["ln_rstd"].at(1))
                for i, t in enumerate(LAT_TILES):
                    link_v(nc.vector.tensor_scalar(X[:, t, :], X[:, t, :], mv[:, i, 0:1], mv[:, i, 1:2],
                                                   ALU.subtract, ALU.mult))
                    link_v(nc.vector.tensor_tensor(X[:, t, :], X[:, t, :], gain[:, :], ALU.mult))
                    link_v(nc.vector.tensor_tensor(X[:, t, :], X[:, t, :], shift[:, :], ALU.add))
            S["ln_var"].passed(1), S["ln_rstd"].passed(1), loads_ready.passed(1)
            meet()


    def per_layer_input(layer, Y, turns=None):
        turn(lambda t, k: X[:, t, k * P:(k + 1) * P], LAT_TILES)
        with ExitStack() as cx:
            G = sb(cx, "ple_gate_buf", [P, 4, D])
            pin = sb(cx, "ple_in", [P, 4, 256])

            @block.scalar
            def _(act):
                load(act, "act", (pin[:, 2:4, :], a["p_2"][layer].rearrange("o (t p) d -> p (o t) d", p=P)))
            linear(a["w_ple_gate_2"][layer], LAT_TILES, lambda e, t, lo, hi, ps: copy_on(e, G[:, t, lo:hi], ps),
                   [(0, 512, 512), (512, 1024, 512)], turns=turns)

            @block.scalar
            def _(act):
                nc.scalar.activation(G[:, 2:4, :], G[:, 2:4, :], ACT.Sigmoid)
            turn(lambda t, k: pin[:, t, k * P:(k + 1) * P], LAT_TILES, 2)
            linear(a["w_ple_proj_2"][layer], LAT_TILES, lambda e, t, lo, hi, ps: copy_on(e, Y[:, t, lo:hi], ps),
                   [(0, 1024, 512)], parts=2, turns=turns)

            @block.vector
            def _(dve):
                link_v(nc.vector.tensor_tensor(G[:, 2:4, :], G[:, 2:4, :], Y[:, 2:4, :], ALU.mult))
                link_v(nc.vector.tensor_tensor(X[:, 2:4, :], X[:, 2:4, :], G[:, 2:4, :], ALU.add))
            meet()

    def second_attention(layer, rot, sinks):
        with ExitStack() as cx:
            B = sb(cx, "qkv", [P, 2, QKV])
            mask = sb(cx, "att_mask", [P, 2, 256])
            turn(lambda t, k: X[:, t, k * P:(k + 1) * P], LAT_TILES)

            @block.scalar
            def _(act):
                lo = C_CAUSAL + layer * 512
                load(act, "act", (mask[:, :, :].rearrange("p t n -> p (t n)"), a["table"][:, lo:lo + 512]))
            linear(a["w_qkv_2"][layer], LAT_TILES, lambda e, t, lo, hi, ps: copy_on(e, B[:, t - 2, lo:hi], ps),
                   [(0, 768, 384), (768, 1536, 384)])
            rotate_partly(B, rot)
            attend(B, 0, K2, V2, 4, [(0, (0,)), (1, (0, 1))], 4, mask=mask, sinks=sinks, scale=ATT_D ** -0.5)
            turn(lambda t, k: B[:, t - 2, k * P:(k + 1) * P], LAT_TILES)

    s_moe = {n: signal(n, o) for n, o in (
        ("moe_logits", "tensor"), ("moe_top", "vector"), ("moe_exp", "scalar"), ("moe_chosen", "vector"),
        ("moe_ranks", "tensor"), ("moe_table", "vector"), ("moe_sel", "vector"), ("moe_gather", "tensor"),
        ("moe_xg", "scalar"), ("moe_scatter", "tensor"), ("moe_added", "vector"))}
    ye_clear = signal("ye_clear", "vector")
    CHUNKS2 = HID2 // WIDTH2
    GATE_ITEM = [0] + [3 * c - 1 for c in range(1, CHUNKS2)]
    UP_ITEM = [1] + [3 * c for c in range(1, CHUNKS2)]
    DOWN_ITEM = [3 * c + 4 for c in range(CHUNKS2 - 1)] + [3 * CHUNKS2 - 1]
    passes_of = {}

    def experts(Y):
        S = s_moe
        turn(lambda t, k: X[:, t, k * P:(k + 1) * P], LAT_TILES)
        with ExitStack() as cx:
            router = sb(cx, "moe_router", [P, KD, EXPERTS])
            lg = sb(cx, "moe_lg", [P, 2, EXPERTS])
            top = sb(cx, "moe_top_buf", [P, 2, 8])
            idx = sb(cx, "moe_idx", [P, 2, 8], U32)
            idf = sb(cx, "moe_idf", [P, 2, 8])
            e1 = sb(cx, "moe_e1", [P, 2])
            w01 = sb(cx, "moe_w01", [P, 2, 2])
            one = sb(cx, "moe_one", [P, 2, 2, EXPERTS])
            chosen = sb(cx, "moe_chosen_buf", [P, 2, EXPERTS])
            gates = sb(cx, "moe_gates", [P, 2, EXPERTS, 2])
            place = sb(cx, "moe_place", [P, 2, EXPERTS, 2])
            row = sb(cx, "moe_row", [1, 4, EXPERTS])
            grid = sb(cx, "moe_grid", [1, 4, 16, EXPERTS])
            table = sb(cx, "moe_table_buf", [1, 2, 16], I32)
            total = sb(cx, "moe_total", [1, 1], I32)
            totf = sb(cx, "moe_totf", [1, 1])
            tabf = sb(cx, "moe_tabf", [1, 2, 16])
            pick = sb(cx, "moe_pick", [P, 2, P])
            pick_g = sb(cx, "moe_pick_g", [P, 2, P])
            xg = sb(cx, "moe_xg_buf", [P, KD, P])
            back = sb(cx, "moe_back", [P, 2, P])
            ye = sb(cx, "moe_ye", [P, 1, D])
            H = Hidden(cx, WIDTH2)
            iota = const[:, C_IOTA:C_IOTA + P]
            tri = const[:, C_TRI:C_TRI + P]
            FS = s_ffn
            add = lambda y, ps: nc.vector.tensor_tensor(y, y, ps, ALU.add)
            pe_gate, pe_up, pe_turn, pe_down, act_silu, act_turned, dve_hidden, dve_add = ffn_steps(
                H, lambda k, t: xg[:, k, :], ye, add)

            @block.gpsimd
            def _(pool):
                load(pool, "pool", (router[:, :, :], a["w_router_2"][0].rearrange("(k p) e -> p k e", p=P)))
                pool.sem_inc(loads_ready.handle, 1)

            @block.tensor
            def _(pe):
                pe.wait_ge(loads_ready.handle, loads_ready.at(1))
                for i, t in enumerate(LAT_TILES):
                    for k in range(KD):
                        mm = nc.tensor.matmul(H.ps_g[:, i, 0:EXPERTS], hT[:, k, t * P:(t + 1) * P], router[:, k, :],
                                              start=k == 0, stop=k == KD - 1)
                mm.then_inc(S["moe_logits"].handle, 1)
                pe.wait_ge(S["moe_chosen"].handle, S["moe_chosen"].at(1))
                nc.tensor.matmul(H.ps_u[:, 0, 0:EXPERTS], tri, chosen[:, 0, :], start=True, stop=True)
                nc.tensor.matmul(H.ps_u[:, 1, 0:EXPERTS], ones, chosen[:, 0, :], start=True, stop=False)
                nc.tensor.matmul(H.ps_u[:, 1, 0:EXPERTS], tri, chosen[:, 1, :], start=False, stop=True)
                nc.tensor.matmul(H.ps_y[:, 0, 0:EXPERTS], ones, chosen[:, 0, :], start=True, stop=False)
                nc.tensor.matmul(H.ps_y[:, 0, 0:EXPERTS], ones, chosen[:, 1, :], start=False, stop=True)\
                    .then_inc(S["moe_ranks"].handle, 1)

            @block.scalar
            def _(act):
                act.wait_ge(S["moe_top"].handle, S["moe_top"].at(1))
                nc.scalar.activation(e1[:, :], e1[:, :], ACT.Exp).then_inc(S["moe_exp"].handle, 1)

            @block.vector
            def _(dve):
                dve.wait_ge(S["moe_logits"].handle, S["moe_logits"].at(1))
                link_v(nc.vector.tensor_copy(lg[:, :, :], H.ps_g[:, :, 0:EXPERTS]))
                for i in range(2):
                    link_v(nc.vector.max(top[:, i, :], lg[:, i, :]))
                    link_v(nc.vector.max_index(idx[:, i, :], top[:, i, :], lg[:, i, :]))
                link_v(nc.vector.tensor_copy(idf[:, :, :], idx[:, :, :]))
                link_v(nc.vector.tensor_tensor(e1[:, :], top[:, :, 1], top[:, :, 0], ALU.subtract))
                nc.vector.sem_inc(S["moe_top"].handle, 1)
                dve.wait_ge(S["moe_exp"].handle, S["moe_exp"].at(1))
                link_v(nc.vector.tensor_scalar(w01[:, :, 1], e1[:, :], 1.0, None, ALU.add))
                link_v(nc.vector.reciprocal(w01[:, :, 0], w01[:, :, 1]))
                link_v(nc.vector.tensor_tensor(w01[:, :, 1], e1[:, :], w01[:, :, 0], ALU.mult))
                for i in range(2):
                    for c in range(2):
                        link_v(nc.vector.tensor_scalar(one[:, i, c, :], iota[:, 0:EXPERTS], idf[:, i, c:c + 1], None,
                                                       ALU.is_equal))
                link_v(nc.vector.tensor_tensor(chosen[:, :, :], one[:, :, 0, :], one[:, :, 1, :], ALU.add))
                nc.vector.sem_inc(S["moe_chosen"].handle, 1)
                for i in range(2):
                    link_v(nc.vector.tensor_scalar(gates[:, i, :, 0], one[:, i, 0, :], w01[:, i, 0:1], None, ALU.mult))
                    link_v(nc.vector.scalar_tensor_tensor(out=gates[:, i, :, 0], in0=one[:, i, 1, :],
                                                          scalar=w01[:, i, 1:2], in1=gates[:, i, :, 0],
                                                          op0=ALU.mult, op1=ALU.add))
                link_v(nc.vector.tensor_copy(gates[:, :, :, 1], gates[:, :, :, 0]))
                dve.wait_ge(S["moe_ranks"].handle, S["moe_ranks"].at(1))
                link_v(nc.vector.scalar_tensor_tensor(out=place[:, :, :, 0], in0=H.ps_u[:, :, 0:EXPERTS], scalar=1000.0,
                                                      in1=chosen[:, :, :], op0=ALU.add, op1=ALU.mult))
                link_v(nc.vector.tensor_scalar(place[:, :, :, 0], place[:, :, :, 0], 1000.0, None, ALU.subtract))
                link_v(nc.vector.tensor_scalar(place[:, :, :, 1], place[:, :, :, 0], float(P), None, ALU.subtract))
                cnt, start_, run, two = row[:, 0, :], row[:, 1, :], row[:, 2, :], row[:, 3, :]
                link_v(nc.vector.tensor_copy(run, H.ps_y[0:1, 0, 0:EXPERTS]))
                link_v(nc.vector.tensor_scalar(cnt, run, 0.5, None, ALU.is_gt))
                link_v(nc.vector.tensor_scalar(two, run, P + 0.5, None, ALU.is_gt))
                link_v(nc.vector.tensor_tensor(cnt, cnt, two, ALU.add))
                link_v(nc.vector.tensor_tensor_scan(run, ones[0:1, 0:EXPERTS], cnt, 0.0, ALU.mult, ALU.add))
                link_v(nc.vector.tensor_tensor(start_, run, cnt, ALU.subtract))
                link_v(nc.vector.tensor_copy(total[:, :], run[:, EXPERTS - 1:EXPERTS]))
                twice_e = const[0:1, C_MISC + 8:C_MISC + 16]
                number = const[0:1, C_MISC + 16:C_MISC + 32]
                rows = lambda r: r.unsqueeze(1).to_broadcast([1, 16, EXPERTS])
                off, inside, low, val = (grid[:, j, :, :] for j in range(4))
                link_v(nc.vector.tensor_tensor(off, number.unsqueeze(2).to_broadcast([1, 16, EXPERTS]), rows(start_),
                                               ALU.subtract))
                link_v(nc.vector.tensor_tensor(inside, off, rows(cnt), ALU.is_lt))
                link_v(nc.vector.tensor_scalar(low, off, 0.0, None, ALU.is_ge))
                link_v(nc.vector.tensor_tensor(inside, inside, low, ALU.mult))
                link_v(nc.vector.tensor_tensor(low, inside, rows(twice_e), ALU.mult))
                link_v(nc.vector.tensor_tensor(off, inside, off, ALU.mult))
                link_v(nc.vector.tensor_tensor(val, low, off, ALU.add))
                link_v(nc.vector.tensor_reduce(tabf[:, 0, :], val, AX.X, ALU.add))
                link_v(nc.vector.tensor_reduce(tabf[:, 1, :], low, AX.X, ALU.add))
                link_v(nc.vector.tensor_scalar(tabf[:, 1, :], tabf[:, 1, :], 0.5, None, ALU.mult))
                link_v(nc.vector.tensor_copy(table[:, :, :], tabf[:, :, :]))
                nc.vector.sem_inc(S["moe_table"].handle, 1)
                link_v(nc.vector.memset(Y[:, 2:4, :], 0.0))

            def passes(eng, name):
                eng.wait_ge(S["moe_table"].handle, S["moe_table"].at(1))
                n = eng.value_load(total[0:1, 0:1], min_val=1, max_val=11)
                passes_of[name] = n
                return n

            @block.sync
            def _(sp):
                with sp.Fori(0, passes(sp, "sync")) as p:
                    e = sp.value_load(table[0:1, 1, bass.ds(p, 1)], min_val=0, max_val=EXPERTS - 1)

                    def across(item, w, c):
                        src = a[w][0][bass.ds(e, 1)].rearrange("o (k p) n -> p (o k) n", p=P)
                        stream(sp, item[c], src[:, :, c * WIDTH2:(c + 1) * WIDTH2], p * CHUNKS2)

                    for c in range(CHUNKS2 + 1):
                        if c < CHUNKS2:
                            across(GATE_ITEM, "w_exp_gate_2", c)
                            across(UP_ITEM, "w_exp_up_2", c)
                        if c > 0:
                            src = a["w_exp_down_2"][0][bass.ds(e, 1), (c - 1) * WIDTH2:c * WIDTH2, :]
                            stream(sp, DOWN_ITEM[c - 1], src.rearrange("o (k p) n -> p (o k) n", p=P), p * CHUNKS2)

            @block.tensor
            def _(pe):
                with pe.Fori(0, passes(pe, "tensor")) as p:
                    n0 = p * CHUNKS2
                    pe.wait_ge(S["moe_sel"].handle, S["moe_sel"].at(1) + p)
                    pe.wait_ge(FS["ffn_turned_taken"].handle, FS["ffn_turned_taken"].at(0) + n0)
                    pe.wait_ge(FS["ffn_silu"].handle, FS["ffn_silu"].at(0) + n0)
                    for k in range(KD):
                        for i in range(2):
                            nc.tensor.matmul(H.ps_t[:, k, :], X[:, 2 + i, k * P:(k + 1) * P], pick[:, i, :],
                                             start=i == 0, stop=i == 1)
                    for i in range(2):
                        mm = nc.tensor.transpose(H.ps_g[:, 0, i * P:(i + 1) * P], pick_g[:, i, :], ident)
                    mm.then_inc(S["moe_gather"].handle, 1)
                    pe.wait_ge(S["moe_xg"].handle, S["moe_xg"].at(1) + p)
                    views = [(slot_view(GATE_ITEM[c], KD, WIDTH2), slot_view(UP_ITEM[c], KD, WIDTH2),
                              down_view(DOWN_ITEM[c], WIDTH2)) for c in range(CHUNKS2)]
                    await_item(pe, 0, n0)
                    pe_gate(pe, n0, views[0][0], 0)
                    await_item(pe, 1, n0)
                    pe.wait_ge(S["moe_added"].handle, S["moe_added"].at(0) + p * 2)
                    pe_up(pe, n0, views[0][1], 0)
                    for c in range(CHUNKS2):
                        if c + 1 < CHUNKS2:
                            await_item(pe, GATE_ITEM[c + 1], n0)
                            pe_gate(pe, n0 + c + 1, views[c + 1][0], 0)
                        pe_turn(pe, n0 + c)
                        if c + 1 < CHUNKS2:
                            await_item(pe, UP_ITEM[c + 1], n0)
                            pe_up(pe, n0 + c + 1, views[c + 1][1], 0)
                        await_item(pe, DOWN_ITEM[c], n0)
                        pe_down(pe, n0 + c, views[c][2])
                    pe.wait_ge(FS["ffn_added"].handle, FS["ffn_added"].at(CHUNKS2) + n0)
                    for i in range(2):
                        for h in range(2):
                            mm = nc.tensor.matmul((H.ps_y, H.ps_u)[i][:, h, :], back[:, i, :], ye[:, 0, h * 512:(h + 1) * 512],
                                                  start=True, stop=True)
                        mm.then_inc(S["moe_scatter"].handle, 1)

            @block.scalar
            def _(act):
                nc.scalar.preload_act_table_set("silu_and_others")
                with act.Fori(0, passes(act, "scalar")) as p:
                    n0 = p * CHUNKS2
                    act.wait_ge(S["moe_gather"].handle, S["moe_gather"].at(1) + p)
                    act.wait_ge(S["moe_scatter"].handle, S["moe_scatter"].at(0) + p * 2)
                    nc.scalar.activation(xg[:, :, :], H.ps_t[:, :, :], ACT.Copy)
                    nc.scalar.activation(back[:, :, :].rearrange("p t n -> p (t n)"), H.ps_g[:, 0, 0:256], ACT.Copy)\
                        .then_inc(S["moe_xg"].handle, 1)
                    act_silu(act, n0, GATE_ITEM[0])
                    for c in range(CHUNKS2):
                        if c + 1 < CHUNKS2:
                            act_silu(act, n0 + c + 1, GATE_ITEM[c + 1])
                        act_turned(act, n0 + c)

            @block.vector
            def _(dve):
                def choose(p):
                    code = dve.value_load(table[0:1, 0, bass.ds(p, 1)], min_val=0, max_val=2 * EXPERTS - 1)
                    flat = lambda x, i: x[:, i, :, :].rearrange("p e h -> p (e h)")[:, bass.ds(code, 1)]
                    dve.wait_ge(S["moe_gather"].handle, S["moe_gather"].at(0) + p)
                    for i in range(2):
                        nc.vector.tensor_scalar(pick[:, i, :], iota, flat(place, i), None, ALU.is_equal)
                        last = nc.vector.tensor_scalar(pick_g[:, i, :], iota, flat(place, i), flat(gates, i),
                                                       ALU.is_equal, ALU.mult)
                    last.then_inc(S["moe_sel"].handle, 1)

                n_passes = passes(dve, "vector")
                choose(0)
                with dve.Fori(0, n_passes) as p:
                    n0 = p * CHUNKS2
                    dve.wait_ge(S["moe_scatter"].handle, S["moe_scatter"].at(0) + p * 2)
                    nc.vector.memset(ye[:, :, :], 0.0).then_inc(ye_clear.handle, 1)
                    dve.wait_ge(ye_clear.handle, ye_clear.at(1) + p)
                    dve_hidden(dve, n0, UP_ITEM[0])
                    for c in range(CHUNKS2):
                        if c + 1 < CHUNKS2:
                            dve_hidden(dve, n0 + c + 1, UP_ITEM[c + 1])
                        dve_add(dve, n0 + c, 0, DOWN_ITEM[c])
                    choose(p + 1)
                    for i in range(2):
                        dve.wait_ge(S["moe_scatter"].handle, S["moe_scatter"].at(i + 1) + p * 2)
                        dve.wait_ge(S["moe_added"].handle, S["moe_added"].at(0) + p * 2)
                        add(Y[:, 2 + i, :], (H.ps_y, H.ps_u)[i][:, :, :].rearrange("p h n -> p (h n)"))\
                            .then_inc(S["moe_added"].handle, 1)
            loads_ready.passed(1)
            meet()


    def rest():
        modulate(1)
        O = X[:, 0:2, :]
        odd_mixer(O)
        turn(lambda t, k: O[:, t - 2, k * P:(k + 1) * P], LAT_TILES)
        with ExitStack() as cx:
            Y = sb(cx, "Y2", [P, 4, D])
            linear(a["odd_w_out"][0], LAT_TILES, lambda e, t, lo, hi, ps: copy_on(e, Y[:, t, lo:hi], ps),
                   [(0, 512, 512), (512, 1024, 512)])
            add_gated(0, Y, LAT_TILES)
            normalise(1, LAT_TILES)
            feed_forward(a["ffn_w_gate"][1], a["ffn_w_up"][1], a["ffn_w_down"][1], 704, LAT_TILES, Y)
            add_gated(1, Y, LAT_TILES)
        with ExitStack() as cx:
            rot = sb(cx, "rot", [P, 2, 2, ROT])
            sinks = sb(cx, "sinks", [P, 16])
            Y = sb(cx, "Y3", [P, 4, D])
            rotation_table(rot)

            @block.scalar
            def _(act):
                load(act, "act", (sinks[:, :], a["sinks_2"][0:1, :].partition_broadcast(P)))
            for layer in range(2):
                second_attention(layer, rot, sinks if layer == 1 else None)
                linear(a["w_o_2"][layer], LAT_TILES, lambda e, t, lo, hi, ps: copy_on(e, Y[:, t, lo:hi], ps),
                       [(0, 512, 512), (512, 1024, 512)])
                layer_norm(Y, a["ln_mix_g_2"][layer:layer + 1, :], a["ln_mix_b_2"][layer:layer + 1, :])
                if layer == 0:
                    turn(lambda t, k: X[:, t, k * P:(k + 1) * P], LAT_TILES)
                    feed_forward(a["w_ffn_gate_2"][0], a["w_ffn_up_2"][0], a["w_ffn_down_2"][0], WIDTH2, LAT_TILES, Y)
                else:
                    experts(Y)
                layer_norm(Y, a["ln_ffn_g_2"][layer:layer + 1, :], a["ln_ffn_b_2"][layer:layer + 1, :])
                per_layer_input(layer, Y, passes_of if layer == 1 else None)
        finish(LAT_TILES)
    start()
    modulate(0)
    with ExitStack() as cx:
        A = sb(cx, "even_A", [P, 4, O_END])
        with ExitStack() as cy:
            g = sb(cy, "even_g", [P, 4, 2, GH * GK])
            first_layer_even(A, g)
        Y = A[:, :, 0:D]
        linear(a["even_w_out"][0], ALL_TILES, lambda e, t, lo, hi, ps: copy_on(e, Y[:, t, lo:hi], ps),
               [(0, 512, 512), (512, 1024, 512)])
        add_gated(0, Y, ALL_TILES)
    with ExitStack() as cx:
        Y = sb(cx, "Y", [P, 4, D])
        normalise(1, ALL_TILES)
        feed_forward(a["ffn_w_gate"][0], a["ffn_w_up"][0], a["ffn_w_down"][0], 704, ALL_TILES, Y)
        add_gated(1, Y, ALL_TILES)
    rest()


_INS = ["x", "c", "ctx", "c_ctx", "mod_w", "mod_b", "norm_pre_mix", "norm_post_mix", "norm_pre_ffn", "norm_post_ffn",
        "even_w_in", "gla_w_gate", "gla_b_gate", "gla_out_norm", "att_q_norm", "att_k_norm", "even_w_out",
        "odd_w_in", "hgrn_lower_bounds", "hgrn_out_norm", "odd_w_out", "ffn_w_gate", "ffn_w_up", "ffn_w_down",
        "p_2", "positions_2", "w_qkv_2", "w_o_2", "ln_mix_g_2", "ln_mix_b_2", "ln_ffn_g_2", "ln_ffn_b_2", "sinks_2",
        "w_ffn_gate_2", "w_ffn_up_2", "w_ffn_down_2", "w_router_2", "w_exp_gate_2", "w_exp_up_2", "w_exp_down_2",
        "w_ple_proj_2", "w_ple_gate_2"]


def kernel(**inputs):
    import concourse.bacc as bacc
    from concourse.bass_utils import run_bass_kernel_spmd

    nc = bacc.Bacc("TRN2", target_bir_lowering=False, num_devices=1)
    arrays, access = {}, {}
    inputs["table"] = constants()
    for name in _INS + ["table"]:
        x = np.ascontiguousarray(inputs[name])
        arrays[f"in_{name}_dram"] = x
        access[name] = nc.dram_tensor(f"in_{name}_dram", x.shape, mybir.dt.from_np(x.dtype),
                                      kind="ExternalInput").ap()
    out = nc.dram_tensor("out_0_dram", (1, 256, 1024), F32, kind="ExternalOutput").ap()
    program(nc, access, out)
    r = run_bass_kernel_spmd(nc, [arrays], core_ids=[0])
    return r.results[0]["out_0_dram"]
```
